# Optimizing a Trainium2 kernel written in Bass

```python
import math
import jax, jax.numpy as jnp
from jax import lax
import numpy as np

D_MODEL = 1024
BATCH = 1
SEQ = 512
DEPTH = 2
DEC_BATCH = 8
DEC_SEQ = 1
PAST_LEN = 1024
PAGE_SIZE = 128

F32 = jnp.float32
HEAD_DIM = 64
POOL_WINDOWS = (2, 4, 8, 16)
POOL_GROUPS = len(POOL_WINDOWS)
POOL_DIM = D_MODEL // 4
POOL_GROUP = POOL_DIM // POOL_GROUPS
POOL_BUF = max(POOL_WINDOWS) - 1
NSA_DIM = D_MODEL - POOL_DIM
NSA_HEADS = NSA_DIM // HEAD_DIM
NSA_KV_HEADS = 4
NSA_REP = NSA_HEADS // NSA_KV_HEADS
KV_DIM = NSA_KV_HEADS * HEAD_DIM
CMP_LEN = 32
CMP_STRIDE = 16
SLC_LEN = 64
SLC_TOP = 16
WINDOW = 512
QBLOCK = 128
IN_DIM_EVEN = POOL_DIM + NSA_DIM + 6 * KV_DIM + 3 * NSA_HEADS
RWKV_HEAD = 64
RWKV_HEADS = D_MODEL // RWKV_HEAD
DECAY_LORA = 64
AAA_LORA = 64
MV_LORA = 32
GATE_LORA = 128
LN_X_EPS = 64e-5
D_FF = 4 * D_MODEL
PLE_DIM = 256
RMS_EPS = 1e-6
N_EVEN = (DEPTH + 1) // 2
N_ODD = DEPTH // 2
NEG_INF = -1e30
SEL_BIG = 1e9

kernel_name = 'pool_nsa_rwkv7_hybrid_step'

def rms_norm(x, g):
    xf = x.astype(F32)
    y = xf * lax.rsqrt(jnp.mean(xf * xf, axis=-1, keepdims=True) + RMS_EPS)
    return (y * g.astype(F32)).astype(x.dtype)

def alibi_slopes(n):
    p = 2 ** int(math.floor(math.log2(n)))
    s = [2.0 ** (-8.0 * (i + 1) / p) for i in range(p)]
    if p < n:
        s += [2.0 ** (-8.0 * (i + 1) / (2 * p)) for i in range(0, 2 * p, 2)][: n - p]
    return np.asarray(s, dtype=np.float32)

def masked_softmax(s, valid):
    s = jnp.where(valid, s, NEG_INF)
    e = jnp.exp(s - jnp.max(s, axis=-1, keepdims=True)) * valid
    return e / jnp.maximum(jnp.sum(e, axis=-1, keepdims=True), 1e-30)

def gqa_attend(q, k, v, dist, valid, slopes):
    s = jnp.einsum('...tgrd,...kgd->...grtk', q, k) * (HEAD_DIM ** -0.5)
    s = s - slopes[:, :, None, None] * dist[..., None, None, :, :]
    p = masked_softmax(s, valid[..., None, None, :, :])
    return jnp.einsum('...grtk,...kgd->...tgrd', p, v), p

def compress(x, pe, w):
    n, l, g, d = x.shape
    ratio = CMP_LEN // CMP_STRIDE
    nh = l // CMP_STRIDE
    n_cmp = nh - ratio + 1
    halves = x[:, : nh * CMP_STRIDE].reshape(n, nh, CMP_STRIDE, g, d)
    out = 0.0
    for o in range(ratio):
        sl = slice(o * CMP_STRIDE, (o + 1) * CMP_STRIDE)
        out = out + jnp.einsum('nilgd,lde->nige', halves[:, o:o + n_cmp] + pe[sl, None, :], w[sl])
    return out

def nsa_global(q, k_all, v_all, q_pos, kc_gain, cmp_pe, cmp_w, slopes):
    n, t = q.shape[:2]
    l = k_all.shape[1]
    k_all = k_all.astype(F32)
    v_all = v_all.astype(F32)
    kc = rms_norm(compress(k_all[:, :, 0], cmp_pe[0], cmp_w[0]), kc_gain)
    vc = compress(v_all[:, :, 0], cmp_pe[1], cmp_w[1])
    n_cmp = kc.shape[1]
    cmp_end = jnp.arange(n_cmp) * CMP_STRIDE + (CMP_LEN - 1)
    dist = q_pos[:, None] - cmp_end[None, :]
    o_cmp, p_cmp = gqa_attend(q, kc, vc, dist.astype(F32), dist >= 0, slopes)
    imp = jnp.sum(p_cmp, axis=2)
    n_slc = -(-l // SLC_LEN)
    per = SLC_LEN // CMP_STRIDE
    lead = CMP_LEN // CMP_STRIDE - 1
    cidx = jnp.arange(n_slc)[:, None] * per + jnp.arange(-lead, per)[None, :]
    cval = (cidx >= 0) & (cidx < n_cmp)
    imp = jnp.where(cval, jnp.take(imp, jnp.clip(cidx, 0, n_cmp - 1), axis=-1), 0.0).sum(-1)
    blk = jnp.arange(n_slc)[None, :]
    cur = (q_pos // SLC_LEN)[:, None]
    causal = blk * SLC_LEN <= q_pos[:, None]
    forced = (blk == 0) | (blk == cur) | (blk == cur - 1)
    score = jnp.where(forced, SEL_BIG, jnp.where(causal, imp, -SEL_BIG))
    n_top = min(SLC_TOP, n_slc)
    _, sel = lax.top_k(score, n_top)
    pad = n_slc * SLC_LEN - l

    def to_blocks(z):
        z = jnp.pad(z, ((0, 0), (0, pad), (0, 0), (0, 0)))
        return z.reshape(n, n_slc, SLC_LEN, NSA_KV_HEADS, HEAD_DIM).transpose(0, 3, 1, 2, 4)

    ksb = to_blocks(k_all[:, :, 1])
    vsb = to_blocks(v_all[:, :, 1])
    qb = QBLOCK if t % QBLOCK == 0 else t
    nq = t // qb
    g_idx = jnp.arange(NSA_KV_HEADS)[None, :, None]

    def one(args):
        b, q_blk, pos_blk, sel_blk = args
        kg = ksb[b][g_idx, sel_blk]
        vg = vsb[b][g_idx, sel_blk]
        kpos = sel_blk[..., None] * SLC_LEN + jnp.arange(SLC_LEN)
        d_ = pos_blk[:, None, None, None] - kpos
        s = jnp.einsum('tgrd,tgnkd->tgrnk', q_blk, kg) * (HEAD_DIM ** -0.5)
        s = s - slopes[None, :, :, None, None] * d_[:, :, None].astype(F32)
        s = s.reshape(qb, NSA_KV_HEADS, NSA_REP, n_top * SLC_LEN)
        valid = (d_ >= 0).reshape(qb, NSA_KV_HEADS, 1, n_top * SLC_LEN)
        p = masked_softmax(s, valid).reshape(qb, NSA_KV_HEADS, NSA_REP, n_top, SLC_LEN)
        return jnp.einsum('tgrnk,tgnkd->tgrd', p, vg)

    xs = (jnp.repeat(jnp.arange(n), nq),
          q.reshape(n * nq, qb, NSA_KV_HEADS, NSA_REP, HEAD_DIM),
          jnp.tile(q_pos.reshape(nq, qb), (n, 1)),
          sel.transpose(0, 2, 1, 3).reshape(n * nq, qb, NSA_KV_HEADS, n_top))
    o_slc = lax.map(one, xs).reshape(n, t, NSA_KV_HEADS, NSA_REP, HEAD_DIM)
    return o_cmp, o_slc

def window_prompt(q, kw, vw, slopes):
    n, t = q.shape[:2]
    nb = t // QBLOCK
    span = WINDOW + QBLOCK
    kp = jnp.pad(kw, ((0, 0), (WINDOW, 0), (0, 0), (0, 0)))
    vp = jnp.pad(vw, ((0, 0), (WINDOW, 0), (0, 0), (0, 0)))
    q_blocks = jnp.moveaxis(q.reshape(n, nb, QBLOCK, NSA_KV_HEADS, NSA_REP, HEAD_DIM), 1, 0)

    def one(args):
        b, q_blk = args
        start = b * QBLOCK
        k_blk = lax.dynamic_slice_in_dim(kp, start, span, axis=1)
        v_blk = lax.dynamic_slice_in_dim(vp, start, span, axis=1)
        qpos = start + jnp.arange(QBLOCK)
        kpos = start - WINDOW + jnp.arange(span)
        dist = qpos[:, None] - kpos[None, :]
        valid = (dist >= 0) & (dist < WINDOW) & (kpos[None, :] >= 0)
        o, _ = gqa_attend(q_blk, k_blk, v_blk, dist.astype(F32), valid, slopes)
        return o

    o = lax.map(one, (jnp.arange(nb), q_blocks))
    return jnp.moveaxis(o, 0, 1).reshape(n, t, NSA_KV_HEADS, NSA_REP, HEAD_DIM)

def window_sample(q, k, v, q_pos, k_start, slopes):
    kpos = k_start + jnp.arange(k.shape[1])
    dist = q_pos[:, None] - kpos[None, :]
    o, _ = gqa_attend(q, k, v, dist.astype(F32), (dist >= 0) & (dist < WINDOW), slopes)
    return o

def pool_mix(u, buf, pos0, w, scale):
    n, t, c = u.shape
    uf = u.astype(F32)
    prev = jnp.zeros((n, POOL_BUF, c), F32) if buf is None else buf.astype(F32)
    ext = jnp.concatenate([prev, uf], axis=1)
    cs = jnp.concatenate([jnp.zeros((n, 1, c), F32), jnp.cumsum(ext, axis=1)], axis=1)
    end = cs[:, POOL_BUF + 1:]
    pos = pos0 + jnp.arange(t)
    outs = []
    for gi, win in enumerate(POOL_WINDOWS):
        ch = slice(gi * POOL_GROUP, (gi + 1) * POOL_GROUP)
        start = cs[:, POOL_BUF + 1 - win: POOL_BUF + 1 - win + t, ch]
        cnt = jnp.minimum(win, pos + 1).astype(F32)[None, :, None]
        outs.append((end[:, :, ch] - start) / cnt - uf[:, :, ch])
    mixed = jnp.stack(outs, axis=2)
    y = jnp.einsum('ntgc,gcd->ntgd', mixed, w.astype(F32)).reshape(n, t, c) * scale.astype(F32)
    return y.astype(u.dtype), ext[:, -POOL_BUF:].astype(u.dtype)

def even_mixer(xn, pos0, pool_buf, kv_past, win_buf, wbuf, w_in, pool_w, pool_scale, q_gain, k_gain,
               cmp_pe, cmp_w, w_out, slopes):
    n, t, _ = xn.shape
    z = xn @ w_in
    u, q, kv, gl = jnp.split(z, [POOL_DIM, POOL_DIM + NSA_DIM, POOL_DIM + NSA_DIM + 6 * KV_DIM], axis=-1)
    y_pool, pool_state = pool_mix(u, pool_buf, pos0, pool_w, pool_scale)
    q = rms_norm(q.reshape(n, t, NSA_KV_HEADS, NSA_REP, HEAD_DIM), q_gain).astype(F32)
    kv = kv.reshape(n, t, 6, NSA_KV_HEADS, HEAD_DIM)
    k_s = rms_norm(kv[:, :, 2], k_gain[1])
    k_w = rms_norm(kv[:, :, 4], k_gain[2])
    v_w = kv[:, :, 5]
    new_k = jnp.stack([kv[:, :, 0], k_s], axis=2)
    new_v = jnp.stack([kv[:, :, 1], kv[:, :, 3]], axis=2)
    q_pos = pos0 + jnp.arange(t)
    if kv_past is None:
        k_all, v_all = new_k, new_v
        o_win = window_prompt(q, k_w.astype(F32), v_w.astype(F32), slopes)
        zpad = jnp.zeros((n, wbuf, NSA_KV_HEADS, HEAD_DIM), k_w.dtype)
        win_k = jnp.concatenate([zpad, k_w], axis=1)[:, -wbuf:]
        win_v = jnp.concatenate([zpad, v_w], axis=1)[:, -wbuf:]
    else:
        k_all = jnp.concatenate([kv_past[0], new_k.astype(kv_past[0].dtype)], axis=1)
        v_all = jnp.concatenate([kv_past[1], new_v.astype(kv_past[1].dtype)], axis=1)
        wk_all = jnp.concatenate([win_buf[0], k_w.astype(win_buf[0].dtype)], axis=1)
        wv_all = jnp.concatenate([win_buf[1], v_w.astype(win_buf[1].dtype)], axis=1)
        o_win = window_sample(q, wk_all.astype(F32), wv_all.astype(F32), q_pos, pos0 - wbuf, slopes)
        win_k = wk_all[:, -wbuf:]
        win_v = wv_all[:, -wbuf:]
    o_cmp, o_slc = nsa_global(q, k_all, v_all, q_pos, k_gain[0], cmp_pe, cmp_w, slopes)
    gates = jax.nn.sigmoid(gl.astype(F32)).reshape(n, t, NSA_KV_HEADS, NSA_REP, 3)
    o = gates[..., 0:1] * o_cmp + gates[..., 1:2] * o_slc + gates[..., 2:3] * o_win
    mix = jnp.concatenate([y_pool, o.reshape(n, t, NSA_DIM).astype(xn.dtype)], axis=-1)
    return mix @ w_out, new_k, new_v, win_k, win_v, pool_state

def wkv7_scan(s0, r, w, k, v, kk, a):
    def step(S, inp):
        r_t, w_t, k_t, v_t, kk_t, a_t = inp
        sa = jnp.einsum('nhij,nhj->nhi', S, -kk_t)
        S = S * w_t[:, :, None, :] + sa[..., None] * (kk_t * a_t)[:, :, None, :] + v_t[..., None] * k_t[:, :, None, :]
        return S, jnp.einsum('nhij,nhj->nhi', S, r_t)
    xs = tuple(jnp.swapaxes(z, 0, 1) for z in (r, w, k, v, kk, a))
    s_fin, out = lax.scan(step, s0, xs)
    return jnp.swapaxes(out, 0, 1), s_fin

def rwkv7_mixer(xn, shift_prev, s0, v_first, vres, mu, wr, wk, wv, wo, w0, w1, w2,
                a0, a1, a2, g1, g2, k_k, k_a, r_k, ln_w, ln_b):
    n, t, d = xn.shape
    xf = xn.astype(F32)
    prev = jnp.zeros((n, 1, d), F32) if shift_prev is None else shift_prev[:, None].astype(F32)
    xx = jnp.concatenate([prev, xf[:, :-1]], axis=1) - xf
    xr, xw, xk, xv, xa, xg = [xf + xx * mu[j] for j in range(6)]
    r = xr @ wr
    k = xk @ wk
    v = xv @ wv
    w_log = -jax.nn.softplus(-(w0 + jnp.tanh(xw @ w1) @ w2)) - 0.5
    decay = jnp.exp(-jnp.exp(w_log))
    if vres is None:
        v_first = v
    else:
        v0, v1, v2 = vres
        v = v + (v_first - v) * jax.nn.sigmoid(v0 + (xv @ v1) @ v2)
    a = jax.nn.sigmoid(a0 + (xa @ a1) @ a2)
    g = jax.nn.sigmoid(xg @ g1) @ g2
    hs = lambda z: z.reshape(n, t, RWKV_HEADS, RWKV_HEAD)
    kk = hs(k * k_k)
    kk = kk / jnp.maximum(jnp.sqrt(jnp.sum(kk * kk, axis=-1, keepdims=True)), 1e-12)
    k = k * (1.0 + (a - 1.0) * k_a)
    s_init = jnp.zeros((n, RWKV_HEADS, RWKV_HEAD, RWKV_HEAD), F32) if s0 is None else s0.astype(F32)
    o, s_fin = wkv7_scan(s_init, hs(r), hs(decay), hs(k), hs(v), kk, hs(a))
    mean = jnp.mean(o, axis=-1, keepdims=True)
    var = jnp.mean(jnp.square(o - mean), axis=-1, keepdims=True)
    o = ((o - mean) * lax.rsqrt(var + LN_X_EPS)).reshape(n, t, d) * ln_w + ln_b
    o = o + (jnp.sum(hs(r) * hs(k) * r_k, axis=-1, keepdims=True) * hs(v)).reshape(n, t, d)
    y = (o * g) @ wo
    return y.astype(xn.dtype), xf[:, -1], s_fin, v_first

def layer_tail(h, p, g_mlp, w1, w2, g_ple, w_pe, w_pg):
    u = rms_norm(h, g_mlp)
    h = h + jnp.square(jax.nn.relu(u @ w1)) @ w2
    gate = jax.nn.sigmoid((rms_norm(h, g_ple) @ w_pg).astype(F32))
    return h + (gate * (p @ w_pe).astype(F32)).astype(h.dtype)

def setup_inputs(seed: int = 0) -> dict:
    key = jax.random.key(seed)
    ks = iter(jax.random.split(key, 80))
    nrm = lambda shape, scale=1.0: jax.random.normal(next(ks), shape, F32) * scale
    gain = lambda shape: 1.0 + 0.05 * jax.random.normal(next(ks), shape, F32)
    uni = lambda shape, lo, hi: jax.random.uniform(next(ks), shape, F32, lo, hi)
    d = D_MODEL
    n_pages = PAST_LEN // PAGE_SIZE
    n_phys = (5 * DEC_BATCH * n_pages) // 4
    wbuf = min(WINDOW, PAST_LEN)
    perm = jax.random.permutation(next(ks), n_phys)[: DEC_BATCH * n_pages]
    page_table = perm.reshape(DEC_BATCH, n_pages).astype(jnp.int32)
    return {
        'x_prompt': nrm((BATCH, SEQ, d)),
        'x_sample': nrm((DEC_BATCH, DEC_SEQ, d)),
        'cache_k': nrm((N_EVEN, n_phys, PAGE_SIZE, 2, NSA_KV_HEADS, HEAD_DIM)),
        'cache_v': nrm((N_EVEN, n_phys, PAGE_SIZE, 2, NSA_KV_HEADS, HEAD_DIM)),
        'page_table': page_table,
        'state_win_k': nrm((N_EVEN, DEC_BATCH, wbuf, NSA_KV_HEADS, HEAD_DIM)),
        'state_win_v': nrm((N_EVEN, DEC_BATCH, wbuf, NSA_KV_HEADS, HEAD_DIM)),
        'state_pool': nrm((N_EVEN, DEC_BATCH, POOL_BUF, POOL_DIM)),
        'state_shift': nrm((N_ODD, DEC_BATCH, d)),
        'state_wkv': nrm((N_ODD, DEC_BATCH, RWKV_HEADS, RWKV_HEAD, RWKV_HEAD), 0.3),
        'p_prompt': nrm((DEPTH, BATCH, SEQ, PLE_DIM)),
        'p_sample': nrm((DEPTH, DEC_BATCH, DEC_SEQ, PLE_DIM)),
        'norm_mix': gain((DEPTH, d)),
        'norm_mlp': gain((DEPTH, d)),
        'norm_ple': gain((DEPTH, d)),
        'mlp_w1': nrm((DEPTH, d, D_FF), d ** -0.5),
        'mlp_w2': nrm((DEPTH, D_FF, d), D_FF ** -0.5),
        'ple_proj': nrm((DEPTH, PLE_DIM, d), PLE_DIM ** -0.5),
        'ple_gate': nrm((DEPTH, d, d), d ** -0.5),
        'even_w_in': nrm((N_EVEN, d, IN_DIM_EVEN), d ** -0.5),
        'even_w_out': nrm((N_EVEN, POOL_DIM + NSA_DIM, d), (POOL_DIM + NSA_DIM) ** -0.5),
        'pool_w': nrm((N_EVEN, POOL_GROUPS, POOL_GROUP, POOL_GROUP), POOL_GROUP ** -0.5),
        'pool_scale': gain((N_EVEN, POOL_DIM)),
        'q_gain': gain((N_EVEN, HEAD_DIM)),
        'k_gain': gain((N_EVEN, 3, HEAD_DIM)),
        'cmp_pe': nrm((N_EVEN, 2, CMP_LEN, HEAD_DIM), 0.1),
        'cmp_w': nrm((N_EVEN, 2, CMP_LEN, HEAD_DIM, HEAD_DIM), (CMP_LEN * HEAD_DIM) ** -0.5),
        'rwkv_mu': uni((N_ODD, 6, d), 0.0, 1.0),
        'rwkv_wr': nrm((N_ODD, d, d), d ** -0.5),
        'rwkv_wk': nrm((N_ODD, d, d), d ** -0.5),
        'rwkv_wv': nrm((N_ODD, d, d), d ** -0.5),
        'rwkv_wo': nrm((N_ODD, d, d), d ** -0.5),
        'rwkv_w0': uni((N_ODD, d), -5.0, 0.0),
        'rwkv_w1': nrm((N_ODD, d, DECAY_LORA), 0.1 * d ** -0.5),
        'rwkv_w2': nrm((N_ODD, DECAY_LORA, d), 0.1 * DECAY_LORA ** -0.5),
        'rwkv_a0': nrm((N_ODD, d), 0.1),
        'rwkv_a1': nrm((N_ODD, d, AAA_LORA), 0.1 * d ** -0.5),
        'rwkv_a2': nrm((N_ODD, AAA_LORA, d), 0.1 * AAA_LORA ** -0.5),
        'rwkv_v0': nrm((N_ODD - 1, d), 0.1),
        'rwkv_v1': nrm((N_ODD - 1, d, MV_LORA), 0.1 * d ** -0.5),
        'rwkv_v2': nrm((N_ODD - 1, MV_LORA, d), 0.1 * MV_LORA ** -0.5),
        'rwkv_g1': nrm((N_ODD, d, GATE_LORA), d ** -0.5),
        'rwkv_g2': nrm((N_ODD, GATE_LORA, d), GATE_LORA ** -0.5),
        'rwkv_kk': gain((N_ODD, d)),
        'rwkv_ka': gain((N_ODD, d)),
        'rwkv_rk': nrm((N_ODD, RWKV_HEADS, RWKV_HEAD), 0.1),
        'rwkv_lnw': gain((N_ODD, d)),
        'rwkv_lnb': nrm((N_ODD, d), 0.02),
    }

def reference(x_prompt, x_sample, cache_k, cache_v, page_table, state_win_k, state_win_v, state_pool,
              state_shift, state_wkv, p_prompt, p_sample,
              norm_mix, norm_mlp, norm_ple, mlp_w1, mlp_w2, ple_proj, ple_gate,
              even_w_in, even_w_out, pool_w, pool_scale, q_gain, k_gain, cmp_pe, cmp_w,
              rwkv_mu, rwkv_wr, rwkv_wk, rwkv_wv, rwkv_wo, rwkv_w0, rwkv_w1, rwkv_w2,
              rwkv_a0, rwkv_a1, rwkv_a2, rwkv_v0, rwkv_v1, rwkv_v2, rwkv_g1, rwkv_g2,
              rwkv_kk, rwkv_ka, rwkv_rk, rwkv_lnw, rwkv_lnb):
    slopes = jnp.asarray(alibi_slopes(NSA_HEADS)).reshape(NSA_KV_HEADS, NSA_REP)
    dec_b, n_pages = page_table.shape
    past_len = n_pages * PAGE_SIZE
    wbuf = state_win_k.shape[2]
    h_p, h_s = x_prompt, x_sample
    vf_p = None
    vf_s = None
    nk_p, nv_p, nk_s, nv_s = [], [], [], []
    wk_p, wv_p, wk_s, wv_s = [], [], [], []
    pl_p, pl_s, sh_p, sh_s, st_p, st_s = [], [], [], [], [], []
    for i in range(DEPTH):
        xp = rms_norm(h_p, norm_mix[i])
        xs = rms_norm(h_s, norm_mix[i])
        if i % 2 == 0:
            e = i // 2
            ew = (even_w_in[e], pool_w[e], pool_scale[e], q_gain[e], k_gain[e], cmp_pe[e], cmp_w[e],
                  even_w_out[e], slopes)
            yp, a1_, a2_, a3_, a4_, a5_ = even_mixer(xp, 0, None, None, None, wbuf, *ew)
            past_k = cache_k[e][page_table].reshape(dec_b, past_len, 2, NSA_KV_HEADS, HEAD_DIM)
            past_v = cache_v[e][page_table].reshape(dec_b, past_len, 2, NSA_KV_HEADS, HEAD_DIM)
            ys, b1_, b2_, b3_, b4_, b5_ = even_mixer(xs, past_len, state_pool[e], (past_k, past_v),
                                                     (state_win_k[e], state_win_v[e]), wbuf, *ew)
            nk_p.append(a1_); nv_p.append(a2_); wk_p.append(a3_); wv_p.append(a4_); pl_p.append(a5_)
            nk_s.append(b1_); nv_s.append(b2_); wk_s.append(b3_); wv_s.append(b4_); pl_s.append(b5_)
        else:
            o = i // 2
            vres = None if o == 0 else (rwkv_v0[o - 1], rwkv_v1[o - 1], rwkv_v2[o - 1])
            rw = (rwkv_mu[o], rwkv_wr[o], rwkv_wk[o], rwkv_wv[o], rwkv_wo[o], rwkv_w0[o], rwkv_w1[o], rwkv_w2[o],
                  rwkv_a0[o], rwkv_a1[o], rwkv_a2[o], rwkv_g1[o], rwkv_g2[o], rwkv_kk[o], rwkv_ka[o], rwkv_rk[o],
                  rwkv_lnw[o], rwkv_lnb[o])
            yp, c1_, c2_, vf_p = rwkv7_mixer(xp, None, None, vf_p, vres, *rw)
            ys, d1_, d2_, vf_s = rwkv7_mixer(xs, state_shift[o], state_wkv[o], vf_s, vres, *rw)
            sh_p.append(c1_); st_p.append(c2_); sh_s.append(d1_); st_s.append(d2_)
        h_p = h_p + yp
        h_s = h_s + ys
        h_p = layer_tail(h_p, p_prompt[i], norm_mlp[i], mlp_w1[i], mlp_w2[i], norm_ple[i], ple_proj[i], ple_gate[i])
        h_s = layer_tail(h_s, p_sample[i], norm_mlp[i], mlp_w1[i], mlp_w2[i], norm_ple[i], ple_proj[i], ple_gate[i])
    y_prompt = h_p
    y_sample = h_s
    new_k_prompt = jnp.stack(nk_p)
    new_v_prompt = jnp.stack(nv_p)
    new_k_sample = jnp.stack(nk_s)
    new_v_sample = jnp.stack(nv_s)
    win_k_prompt = jnp.stack(wk_p)
    win_v_prompt = jnp.stack(wv_p)
    win_k_sample = jnp.stack(wk_s)
    win_v_sample = jnp.stack(wv_s)
    pool_prompt = jnp.stack(pl_p)
    pool_sample = jnp.stack(pl_s)
    shift_prompt = jnp.stack(sh_p)
    shift_sample = jnp.stack(sh_s)
    wkv_prompt = jnp.stack(st_p)
    wkv_sample = jnp.stack(st_s)
    return (y_prompt, y_sample, new_k_prompt, new_v_prompt, new_k_sample, new_v_sample,
            win_k_prompt, win_v_prompt, win_k_sample, win_v_sample, pool_prompt, pool_sample,
            shift_prompt, shift_sample, wkv_prompt, wkv_sample)


_drawn_inputs = setup_inputs


def setup_inputs(seed=0):
    import zlib

    import numpy as np

    out = dict(_drawn_inputs(seed))
    spreads = {}
    factors = {'norm_ple': 6.893,
     'q_gain': 5.062,
     'rwkv_w1': 8.0,
     'rwkv_w2': 8.0,
     'rwkv_a1': 8.0,
     'rwkv_a2': 8.0,
     'rwkv_lnw': 3.869,
     'rwkv_lnb': 8.0}
    for name, (base, spread) in spreads.items():
        noise = np.random.default_rng([zlib.crc32(name.encode()), seed]).standard_normal(out[name].shape)
        drawn = base * np.exp(spread * noise) if base else spread * noise
        out[name] = __import__('jax').numpy.asarray(drawn.astype(out[name].dtype))
    for name, factor in factors.items():
        out[name] = (out[name] * factor).astype(out[name].dtype)
    return out
```

```python
import math
from contextlib import ExitStack

import numpy as np
import concourse.bass as bass
from concourse import mybir

F32 = mybir.dt.float32
I32 = mybir.dt.int32
ALU = mybir.AluOpType
ACT = mybir.ActivationFunctionType
AX = mybir.AxisListType

D, SEQ, NS, PAST, PAGE = 1024, 512, 8, 1024, 128
T = SEQ + NS
HT = T // 2
KC = D // 128
HD, HEADS, GROUPS, REP = 64, 12, 4, 3
NQ = SEQ // 128
PAGES = PAST // PAGE
WIN = 512
CL, CS = 32, 16
NC_P = SEQ // CS - 1
NC_S = PAST // CS - 1
UW = 2048
RING = 4
FF = 4 * D
RH = 16
CH = 64
NCH = SEQ // CH
EPS = 1e-6
NEG = -1e30

V_MIX, V_MLP, V_PLE, V_MU = 0, 16, 32, 48
V_W0, V_A0, V_KK, V_KA, V_RK, V_LNW, V_LNB = (96 + 8 * i for i in range(7))
V_PS, V_QG, V_KG = 152, 154, 155
NV = 158

C_SLC, C_NSLC, C_WIN, C_NWIN, C_CMP = 0, 1024, 1032, 1544, 1552
NCOL = C_CMP + NC_S

U_IN, U_OUT, U_T0 = 0, 10, 14
TAIL = 16 + 16 + 4 + 1
U_R = U_T0 + TAIL
U_WO = U_R + 12
U_T1 = U_WO + 4
NU = U_T1 + TAIL


def slopes():
    s = [2.0 ** (-8.0 * (i + 1) / 8) for i in range(8)]
    s += [2.0 ** (-8.0 * (i + 1) / 16) for i in range(0, 16, 2)][:4]
    return np.asarray(s, np.float32)


SLOPE = slopes()


def constants():
    c = {}
    c["ident"] = np.eye(128, dtype=np.float32)
    c["ones"] = np.ones((128, 128), np.float32)
    c["headones"] = np.kron(np.eye(2), np.ones((64, 64))).astype(np.float32)
    p = np.arange(128)[:, None]
    x = np.arange(512)[None, :] - 384 - p
    c["dist"] = np.where(x > 0, NEG, x).astype(np.float32)
    t = (np.arange(NQ)[None, :] * 128 + p)[:, :, None, None]
    j = np.arange(32)[None, None, None, :]
    heads = np.array([(2 * gp + g2) * REP + r for g2 in range(2) for gp in range(2) for r in range(REP)])
    dd = t - (CS * j + CL - 1)
    ok = (dd >= 0) & (j < NC_P)
    c["cmpbias"] = np.where(ok, -SLOPE[heads][None, None, :, None] * dd, NEG).astype(np.float32)
    c["cmpok"] = np.broadcast_to(ok, (128, NQ, 1, 32)).astype(np.float32).copy()
    ic = np.zeros((128, 2, SEQ), np.float32)
    for gi, w in enumerate((2, 4, 8, 16)):
        ic[(gi % 2) * 64:(gi % 2) * 64 + 64, gi // 2] = 1.0 / np.minimum(w, np.arange(SEQ) + 1)
    c["invcnt"] = ic
    row = np.arange(128)
    g, s, r = row // 32, (row % 32) // 3, row % 32 % 3
    live = s < NS
    sl = np.where(live, SLOPE[g * REP + r], 0.0)[:, None]
    same = (np.arange(NS)[None, :] == s[:, None])
    b = np.zeros((128, NCOL), np.float32)
    b[:, C_SLC:C_NSLC] = -sl * (PAST - np.arange(PAST))[None, :]
    dw = WIN - np.arange(WIN)
    b[:, C_WIN:C_NWIN] = np.where((dw < WIN)[None, :], -sl * dw[None, :], NEG)
    b[:, C_NSLC:C_WIN] = np.where(same | ~live[:, None], 0, NEG)
    b[:, C_NWIN:C_CMP] = np.where(same | ~live[:, None], 0, NEG)
    b[:, C_CMP:] = -sl * (PAST - (CS * np.arange(NC_S) + CL - 1))[None, :]
    c["sbias"] = b
    c["samegs"] = ((g[:, None] == g[None, :]) & (s[:, None] == s[None, :])).astype(np.float32)
    c["own_sample"] = (s[None, :] == np.arange(NS)[:, None]).astype(np.float32)
    c["own_head"] = ((g * REP + r)[:, None] == np.arange(HEADS)[None, :]).astype(np.float32) * live[:, None]
    c["blockno"] = np.broadcast_to(np.arange(1, 15, dtype=np.float32), (128, 14)).copy()
    ss, tt = np.arange(CH)[:, None], np.arange(CH)[None, :]
    m = np.concatenate([ss < tt, ss <= tt], 1).astype(np.float32)
    c["tri"] = np.concatenate([m, m], 0)
    lv = []
    for n in range(6):
        w = 1 << n
        lv.append((tt // w % 2 == 1) & (ss // w == tt // w - 1))
    lv = np.stack(lv, 1).astype(np.float32)
    c["level"] = np.concatenate([lv, lv], 0)
    e = np.eye(64, dtype=np.float32)
    c["ident2"] = np.concatenate([e, e], 0)
    rs = np.ones((128, KC, CH + 1), np.float32)
    rs[:, :, 0] = 0
    c["restart"] = rs
    return c


def build(nc, a, o):
    with ExitStack() as top:
        sb = lambda ctx, name, shape, dt=F32: ctx.enter_context(nc.sbuf_tensor(name, shape, dt))
        sem = lambda name: top.enter_context(nc.semaphore(name))
        P = top.enter_context(nc.psum_tensor("P", [128, 8, 512], F32))
        h = sb(top, "h", [128, KC, T])
        vec = sb(top, "vec", [128, NV])
        ring = sb(top, "ring", [128, RING, UW])
        ident = sb(top, "ident", [128, 128])
        ones = sb(top, "ones", [128, 128])
        headones = sb(top, "headones", [128, 128])
        rstd = sb(top, "rstd", [128, T])

        fixed_in = sem("fixed_in")
        stage_in = sem("stage_in")
        weight_in = [sem(f"weight_in{i}") for i in range(RING)]
        stores = sem("stores")
        tile_done = sem("tile_done")
        tile_free = sem("tile_free")
        sq_ready = sem("sq_ready")
        ssum_ready = sem("ssum_ready")
        rvar_ready = sem("rvar_ready")
        rstd_ready = sem("rstd_ready")
        xn_ready = sem("xn_ready")
        dve_step = sem("dve_step")
        act_step = sem("act_step")
        state = {"unit": 0, "tile": 0, "norm": 0, "stage": 0, "stores": 0}
        last_tile_of = {}

        class Chain:
            def __init__(self, eng, s, key):
                self.eng, self.sem, self.key = eng, s, key
                state.setdefault(key, 0)

            def __call__(self, ins):
                state[self.key] += 1
                ins.then_inc(self.sem, 1)
                self.eng.wait_ge(self.sem, state[self.key])

        halves = lambda ap: ap.rearrange("p (a b) -> p a b", a=2)

        def stream_weights(sp, upto):
            upto = min(upto, NU)
            for u in range(state["unit"], upto):
                if u >= RING:
                    sp.wait_ge(tile_done, last_tile_of[u - RING])
                sp.dma_start(ring[:, u % RING, :], a["weights"][u]).then_inc(weight_in[u % RING], 16)
            state["unit"] = max(upto, state["unit"])

        def plan(units, per_group=1, times=1):
            first = state["tile"]
            n = first
            for g in range(0, len(units), per_group):
                n += 2 * times
                for u in units[g:g + per_group]:
                    last_tile_of[u] = n
            state["tile"] = n
            return first

        def dense(pe, first, units, rhs, nk=KC, cols=256, per_group=1, times=1, chunk_ready=None):
            n = first
            for g in range(0, len(units), per_group):
                for rep in range(times):
                    if n - first >= 4 or n >= 4:
                        pe.wait_ge(tile_free, n - 2)
                    for i, u in enumerate(units[g:g + per_group]):
                        pe.wait_ge(weight_in[u % RING], 16 * (u // RING + 1))
                        for m in range(2):
                            for k in range(nk):
                                if chunk_ready and m == 0:
                                    chunk_ready(i * nk + k)
                                w = ring[:, u % RING, k * cols + (2 * rep + m) * 128:k * cols + (2 * rep + m + 1) * 128]
                                for hf in range(2):
                                    mm = pe.matmul(P[:, n // 2 % 2 * 4 + 2 * m + hf, 0:HT], w,
                                                   rhs(i * nk + k)[:, hf * HT:(hf + 1) * HT],
                                                   start=i == 0 and k == 0,
                                                   stop=i == per_group - 1 and k == nk - 1)
                            if i == per_group - 1:
                                mm.then_inc(tile_done, 1)
                    n += 2

        def tile(n):
            b = n // 2 % 2 * 4 + n % 2 * 2
            return P[:, b:b + 2, 0:HT]

        def norm_act(act, i, dst):
            for k in range(KC):
                act.activation(dst[:, k, :], h[:, k, :], ACT.Square).then_inc(sq_ready, 1)
            act.wait_ge(rvar_ready, i + 1)
            act.activation(rstd[:, :], rstd[:, :], ACT.Sqrt).then_inc(rstd_ready, 1)

        def norm_pe(pe, i, dst):
            for k in range(KC):
                pe.wait_ge(sq_ready, i * KC + k + 1)
                for hf in range(2):
                    mm = pe.matmul(P[:, 6 + hf, 0:HT], ones[:, :], dst[:, k, hf * HT:(hf + 1) * HT],
                                   start=k == 0, stop=k == KC - 1)
            mm.then_inc(ssum_ready, 1)

        def norm_dve(dve, step, i, dst, col):
            dve.wait_ge(ssum_ready, i + 1)
            step(dve.tensor_scalar(halves(rstd[:, :]), P[:, 6:8, 0:HT], 1.0 / D, EPS, ALU.mult, ALU.add))
            dve.reciprocal(rstd[:, :], rstd[:, :]).then_inc(rvar_ready, 1)
            dve.wait_ge(rstd_ready, i + 1)
            for k in range(KC):
                dve.scalar_tensor_tensor(out=dst[:, k, :], in0=h[:, k, :], scalar=vec[:, col + k:col + k + 1],
                                         in1=rstd[:, :], op0=ALU.mult, op1=ALU.mult).then_inc(xn_ready, 1)

        def tail(layer, u0):
            with ExitStack() as ctx:
                u = sb(ctx, f"u{layer}", [128, KC, T])
                hid = sb(ctx, f"hid{layer}", [128, FF // 128, T])
                pl = sb(ctx, f"pl{layer}", [128, 2, T])
                hid_ready = sem(f"hid_ready{layer}")
                block = ctx.enter_context(nc.Block(no_gpsimd_drain=True))
                up, down = list(range(u0, u0 + 16)), list(range(u0 + 16, u0 + 32))
                gate, proj = list(range(u0 + 32, u0 + 36)), [u0 + 36]
                t_up = plan(up)
                t_down = plan(down, per_group=4)
                t_gate = plan(gate)
                t_proj = plan(proj, times=4)
                n1 = state["norm"]
                n2 = n1 + 1
                state["norm"] += 2
                state["stage"] += 16
                landed = state["stage"]

                @block.sync
                def _(sp):
                    sp.dma_start(pl[:, :, :], a["p"][layer]).then_inc(stage_in, 16)
                    stream_weights(sp, u0 + TAIL + RING)

                @block.tensor
                def _(pe):
                    norm_pe(pe, n1, u)
                    dense(pe, t_up, up, lambda k: u[:, k, :],
                          chunk_ready=lambda k: pe.wait_ge(xn_ready, n1 * KC + k + 1))
                    dense(pe, t_down, down, lambda k: hid[:, k, :], per_group=4,
                          chunk_ready=lambda k: pe.wait_ge(hid_ready, k + 1))
                    pe.wait_ge(tile_free, t_gate)
                    norm_pe(pe, n2, u)
                    dense(pe, t_gate, gate, lambda k: u[:, k, :],
                          chunk_ready=lambda k: pe.wait_ge(xn_ready, n2 * KC + k + 1))
                    pe.wait_ge(stage_in, landed)
                    dense(pe, t_proj, proj, lambda k: pl[:, k, :], nk=2, cols=D, times=4)

                @block.scalar
                def _(act):
                    norm_act(act, n1, u)
                    for m in range(FF // 128):
                        act.wait_ge(tile_done, t_up + m + 1)
                        act.activation(halves(hid[:, m, :]), tile(t_up + m), ACT.Relu).then_inc(tile_free, 1)
                    act.wait_ge(tile_free, t_gate)
                    norm_act(act, n2, u)
                    for m in range(KC):
                        act.wait_ge(tile_done, t_gate + m + 1)
                        act.activation(halves(hid[:, m, :]), tile(t_gate + m), ACT.Sigmoid).then_inc(tile_free, 1)

                @block.vector
                def _(dve):
                    step = Chain(dve, dve_step, "dve")
                    norm_dve(dve, step, n1, u, V_MLP + KC * layer)
                    for m in range(FF // 128):
                        dve.wait_ge(tile_free, t_up + m + 1)
                        dve.tensor_tensor(hid[:, m, :], hid[:, m, :], hid[:, m, :], ALU.mult).then_inc(hid_ready, 1)
                    for m in range(KC):
                        dve.wait_ge(tile_done, t_down + m + 1)
                        hv = halves(h[:, m, :])
                        dve.tensor_tensor(hv, hv, tile(t_down + m), ALU.add).then_inc(tile_free, 1)
                    norm_dve(dve, step, n2, u, V_PLE + KC * layer)
                    dve.wait_ge(tile_free, t_proj)
                    for m in range(KC):
                        dve.wait_ge(tile_done, t_proj + m + 1)
                        gv = halves(hid[:, m, :])
                        dve.tensor_tensor(gv, gv, tile(t_proj + m), ALU.mult).then_inc(tile_free, 1)
                        dve.wait_ge(tile_free, t_proj + m + 1)
                        step(dve.tensor_tensor(h[:, m, :], h[:, m, :], hid[:, m, :], ALU.add))

        def layer0():
            with ExitStack() as c0:
                xn = sb(c0, "xn0", [128, KC, T])
                Z = sb(c0, "Z", [128, 20, T])
                gates = sb(c0, "gates", [128, NQ + 1, 3 * HEADS])
                Vt = sb(c0, "Vt", [128, 2, NQ, 256])
                Vn = sb(c0, "Vn", [NS, 2, 256])
                VCp = sb(c0, "VCp", [128, 256])
                KCb = sb(c0, "KCb", [128, NS + 1, 2, NC_S])
                KB = lambda b, gp: 8 + 2 * b + gp
                project_in(xn, Z, gates)
                pool_and_values(xn, Z, Vt, Vn)
                with ExitStack() as c1:
                    VCt = sb(c1, "VCt", [64, NS, 256])
                    compress_and_score(xn, Z, KCb, VCt, VCp, KB)
                    sample_attention(xn, gates, Vn, VCt)
                prompt_attention(xn, Z, gates, Vt, VCp, KCb, KB)
                add_product(xn, list(range(U_OUT, U_OUT + 4)), "w_out")

        def add_product(x, units, name):
            first = plan(units)
            with nc.Block(no_gpsimd_drain=True) as block:
                @block.sync
                def _(sp):
                    stream_weights(sp, units[-1] + 1 + RING)

                @block.tensor
                def _(pe):
                    dense(pe, first, units, lambda k: x[:, k, :])

                @block.vector
                def _(dve):
                    for m in range(KC):
                        dve.wait_ge(tile_done, first + m + 1)
                        hv = halves(h[:, m, :])
                        dve.tensor_tensor(hv, hv, tile(first + m), ALU.add).then_inc(tile_free, 1)

        def project_in(xn, Z, gates):
            with ExitStack() as ctx:
                wgl = sb(ctx, "wgl", [128, KC, 3 * HEADS])
                zsq = sb(ctx, "zsq", [128, 2, T])
                zr = sb(ctx, "zr", [128, 2, T])
                logits_ready = sem("logits_ready")
                zsq_ready = sem("zsq_ready")
                zss_ready = sem("zss_ready")
                zvar_ready = sem("zvar_ready")
                zroot_ready = sem("zroot_ready")
                normed = list(range(2, 8)) + [12, 13, 16, 17]
                units = list(range(U_IN, U_IN + 10))
                first = plan(units)
                i = state["norm"]
                state["norm"] += 1
                state["stage"] += 16
                landed = state["stage"]
                last = first + 20

                with nc.Block(no_gpsimd_drain=True) as block:
                    @block.sync
                    def _(sp):
                        sp.dma_start(wgl[:, :, :], a["wgl"]).then_inc(stage_in, 16)
                        stream_weights(sp, U_IN + 10 + RING)

                    @block.tensor
                    def _(pe):
                        norm_pe(pe, i, xn)
                        dense(pe, first, units, lambda k: xn[:, k, :],
                              chunk_ready=lambda k: pe.wait_ge(xn_ready, i * KC + k + 1))
                        pe.wait_ge(stage_in, landed)
                        pe.wait_ge(tile_free, last)
                        for t in range(NQ + 1):
                            n = 128 if t < NQ else NS
                            for k in range(KC):
                                mm = pe.matmul(P[0:n, 0, t * 36:t * 36 + 36], xn[:, k, t * 128:t * 128 + n],
                                               wgl[:, k, :], start=k == 0, stop=k == KC - 1)
                        mm.then_inc(logits_ready, 1)
                        for j in range(len(normed)):
                            pe.wait_ge(zsq_ready, j + 1)
                            if j >= 2:
                                pe.wait_ge(zvar_ready, j - 1)
                            for hf in range(2):
                                mm = pe.matmul(P[:, 4 + 2 * (j % 2) + hf, 0:HT], headones[:, :],
                                               zsq[:, j % 2, hf * HT:(hf + 1) * HT], start=True, stop=True)
                            mm.then_inc(zss_ready, 1)

                    @block.scalar
                    def _(act):
                        step = Chain(act, act_step, "act")
                        norm_act(act, i, xn)
                        for m in range(20):
                            act.wait_ge(tile_done, first + m + 1)
                            act.activation(halves(Z[:, m, :]), tile(first + m), ACT.Copy).then_inc(tile_free, 1)
                        act.wait_ge(logits_ready, 1)
                        act.activation(gates[:, 0:NQ, :], P[:, 0, 0:NQ * 36].rearrange("p (t c) -> p t c", t=NQ),
                                       ACT.Sigmoid)
                        step(act.activation(gates[0:NS, NQ, :], P[0:NS, 0, NQ * 36:NQ * 36 + 36], ACT.Sigmoid))
                        act.wait_ge(tile_free, last)
                        for j in range(len(normed) + 2):
                            if j >= 2:
                                act.wait_ge(zvar_ready, j - 1)
                                act.activation(zr[:, j % 2, :], zr[:, j % 2, :], ACT.Sqrt,
                                               scale=1.0 / 64 if j - 2 < 6 else 1.0).then_inc(zroot_ready, 1)
                            if j < len(normed):
                                act.activation(zsq[:, j % 2, :], Z[:, normed[j], :], ACT.Square)\
                                   .then_inc(zsq_ready, 1)

                    @block.vector
                    def _(dve):
                        step = Chain(dve, dve_step, "dve")
                        norm_dve(dve, step, i, xn, V_MIX)
                        for j, c in enumerate(normed):
                            dve.wait_ge(zss_ready, j + 1)
                            step(dve.tensor_scalar(halves(zr[:, j % 2, :]),
                                                   P[:, 4 + 2 * (j % 2):6 + 2 * (j % 2), 0:HT],
                                                   1.0 / HD, EPS, ALU.mult, ALU.add))
                            dve.reciprocal(zr[:, j % 2, :], zr[:, j % 2, :]).then_inc(zvar_ready, 1)
                            dve.wait_ge(zroot_ready, j + 1)
                            col = V_QG if j < 6 else V_KG + 1 + (j - 6) // 2
                            step(dve.scalar_tensor_tensor(out=Z[:, c, :], in0=Z[:, c, :], scalar=vec[:, col:col + 1],
                                                          in1=zr[:, j % 2, :], op0=ALU.mult, op1=ALU.mult))

        def pool_and_values(mix, Z, Vt, Vn):
            with ExitStack() as ctx:
                ext = sb(ctx, "ext", [128, 2, 15 + SEQ])
                wa = sb(ctx, "wa", [128, 2, 15 + SEQ])
                wb = sb(ctx, "wb", [128, 2, 15 + SEQ])
                dev = sb(ctx, "dev", [128, 2, T])
                inv = sb(ctx, "inv", [128, 2, SEQ])
                past = sb(ctx, "past", [128, 2, NS, 15])
                newpast = sb(ctx, "newpast", [128, 2, NS, 15])
                psum_ = sb(ctx, "psum_", [128, 2, NS])
                pw = sb(ctx, "pw", [128, 2, 128])
                turned = sem("turned")
                vcopied = sem("vcopied")
                dev_ready = sem("dev_ready")
                pooled = sem("pooled")
                rows_ready = sem("rows_ready")
                state["stage"] += 48
                landed = state["stage"]
                state["stores"] += 48
                W = (2, 4, 8, 16)

                with nc.Block(no_gpsimd_drain=True) as block:
                    @block.sync
                    def _(sp):
                        sp.dma_start(inv[:, :, :], a["invcnt"]).then_inc(stage_in, 16)
                        sp.dma_start(past[:, :, :, :], a["state_pool"]).then_inc(stage_in, 16)
                        sp.dma_start(pw[:, :, :], a["pool_w"]).then_inc(stage_in, 16)
                        sp.dma_start(o["kv"], Z[:, 8:20, :]).then_inc(stores, 16)
                        sp.dma_start(o["pool_p"], Z[:, 0:2, SEQ - 15:SEQ]).then_inc(stores, 16)
                        sp.wait_ge(rows_ready, 1)
                        sp.dma_start(o["pool_s"], newpast[:, :, :, :]).then_inc(stores, 16)
                        sp.wait_ge(stores, state["stores"])

                    @block.tensor
                    def _(pe):
                        for b in range(2):
                            for gp in range(2):
                                for t in range(NQ):
                                    mm = pe.transpose(P[:, 2 * b + gp, t * 128:(t + 1) * 128],
                                                      Z[:, 14 + 4 * b + gp, t * 128:(t + 1) * 128], ident[:, :])
                                mm.then_inc(turned, 1)
                        for b in range(2):
                            for gp in range(2):
                                mm = pe.transpose(P[0:NS, 4, (2 * b + gp) * 128:(2 * b + gp + 1) * 128],
                                                  Z[:, 14 + 4 * b + gp, SEQ:T], ident[:, :])
                        mm.then_inc(turned, 1)
                        pe.wait_ge(dev_ready, 1)
                        pe.wait_ge(stage_in, landed)
                        pe.wait_ge(vcopied, 5)
                        for c in range(2):
                            for hf in range(2):
                                mm = pe.matmul(P[:, (5 + hf, hf)[c], 0:HT], pw[:, c, :],
                                               dev[:, c, hf * HT:(hf + 1) * HT], start=True, stop=True)
                            mm.then_inc(pooled, 1)

                    @block.scalar
                    def _(act):
                        for b in range(2):
                            for gp in range(2):
                                act.wait_ge(turned, 2 * b + gp + 1)
                                act.activation(Vt[:, b, :, gp * 128:(gp + 1) * 128],
                                               P[:, 2 * b + gp, :].rearrange("p (t d) -> p t d", t=NQ),
                                               ACT.Copy).then_inc(vcopied, 1)
                        act.wait_ge(turned, 5)
                        act.activation(Vn[:, :, :], P[0:NS, 4, :].rearrange("p (b d) -> p b d", b=2),
                                       ACT.Copy).then_inc(vcopied, 1)

                    @block.vector
                    def _(dve):
                        step = Chain(dve, dve_step, "dve")
                        n = 15 + SEQ
                        dve.memset(ext[:, :, 0:15], 0.0)
                        step(dve.tensor_copy(ext[:, :, 15:n], Z[:, 0:2, 0:SEQ]))
                        dve.wait_ge(stage_in, landed)
                        dve.tensor_copy(newpast[:, :, :, 0:14], past[:, :, :, 1:15])
                        dve.tensor_copy(newpast[:, :, :, 14], Z[:, 0:2, SEQ:T]).then_inc(rows_ready, 1)
                        src = ext
                        for gi, w in enumerate(W):
                            dst = (wa, wb)[gi % 2]
                            step(dve.tensor_tensor(dst[:, :, w - 1:n], src[:, :, w - 1:n],
                                                   src[:, :, w // 2 - 1:n - w // 2], ALU.add))
                            c, r = gi // 2, slice(gi % 2 * 64, gi % 2 * 64 + 64)
                            step(dve.tensor_tensor(dev[r, c, 0:SEQ], dst[r, c, 15:n], inv[r, c, :], ALU.mult))
                            step(dve.tensor_reduce(psum_[r, c, :], past[r, c, :, 16 - w:15], AX.X, ALU.add))
                            src = dst
                        step(dve.tensor_tensor(dev[:, :, 0:SEQ], dev[:, :, 0:SEQ], Z[:, 0:2, 0:SEQ], ALU.subtract))
                        step(dve.tensor_tensor(psum_[:, :, :], psum_[:, :, :], Z[:, 0:2, SEQ:T], ALU.add))
                        for gi, w in enumerate(W):
                            c, r = gi // 2, slice(gi % 2 * 64, gi % 2 * 64 + 64)
                            mm = dve.scalar_tensor_tensor(out=dev[r, c, SEQ:T], in0=psum_[r, c, :], scalar=1.0 / w,
                                                          in1=Z[r, c, SEQ:T], op0=ALU.mult, op1=ALU.subtract)
                            step(mm)
                        dve.sem_inc(dev_ready, 1)
                        for c in range(2):
                            dve.wait_ge(pooled, c + 1)
                            b = (5, 0)[c]
                            step(dve.tensor_scalar(halves(mix[:, c, :]), P[:, b:b + 2, 0:HT],
                                                   vec[:, V_PS + c:V_PS + c + 1], None, ALU.mult))

        def compress_and_score(mix, Z, KCb, VCt, VCp, KB):
            with ExitStack() as ctx:
                cw = sb(ctx, "cw", [128, 2, CL, 128])
                pe_ = sb(ctx, "pe_", [128, 2, CL])
                peb = sb(ctx, "peb", [128, 2])
                pages = sb(ctx, "pages", [1, NS * PAGES], I32)
                kcmp = sb(ctx, "kcmp", [128, 2, 2, PAST])
                vcmp = sb(ctx, "vcmp", [128, 2, 2, PAST])
                kslc = sb(ctx, "kslc", [128, 2, PAST])
                QA = sb(ctx, "QA", [128, 2, 64])
                spare = mix[:, 2:KC, :].rearrange("p k t -> p (k t)")
                kwin = spare[:, 0:2 * WIN].rearrange("p (g c) -> p g c", g=2)
                VCb = spare[:, 2 * WIN:2 * WIN + (NS + 1) * 2 * NC_S].rearrange("p (s g c) -> p s g c", s=NS + 1, g=2)
                QZ = Z[:, 0:2, :].rearrange("p k t -> p (k t)")[:, 0:1024].rearrange("p (g s c) -> p g s c", g=2, s=NS)
                cmp_in = [sem(f"cmp_in{i}") for i in range(2)]
                slc_in = sem("slc_in")
                cmp_done = sem("cmp_done")
                cmp_free = sem("cmp_free")
                scored = sem("scored")
                q_ready = sem("q_ready")
                peb_done = sem("peb_done")
                ksq_ready = sem("ksq_ready")
                kss_ready = sem("kss_ready")
                kvar_ready = sem("kvar_ready")
                kroot_ready = sem("kroot_ready")
                kc_ready = sem("kc_ready")
                vturned = sem("vturned")
                vct_copied = sem("vct_copied")
                state["stage"] += 48
                landed = state["stage"]
                state["stores"] += 16 * NS
                NK = (NS + 1) * 2 * NC_S
                kflat = KCb[:, :, :, :].rearrange("p s g c -> p (s g c)")
                sq = kcmp[:, 0, :, :].rearrange("p g c -> p (g c)")[:, 0:NK]
                kr = kcmp[:, 1, :, :].rearrange("p g c -> p (g c)")[:, 0:NK]
                N3 = NK // 3

                with nc.Block(no_gpsimd_drain=True) as block:
                    @block.sync
                    def _(sp):
                        sp.dma_start(pages[:, :], a["page_table"]).then_inc(stage_in, 16)
                        sp.dma_start(cw[:, :, :, :], a["cmp_w"]).then_inc(stage_in, 16)
                        sp.dma_start(pe_[:, :, :], a["cmp_pe"]).then_inc(stage_in, 16)
                        sp.wait_ge(stage_in, landed)
                        for s in range(NS):
                            page = [sp.value_load(pages[0:1, s * PAGES + n:s * PAGES + n + 1], min_val=0,
                                                  max_val=a["ck_cmp"].shape[0] - 1) for n in range(PAGES)]
                            if s >= 1:
                                sp.wait_ge(scored, s)
                                sp.wait_ge(stores, state["stores"] - 16 * (NS - s))
                            for n in range(PAGES):
                                sp.dma_start(kslc[:, :, n * PAGE:(n + 1) * PAGE], a["ck_slc"][bass.ds(page[n], 1)]
                                             .rearrange("o p g c -> p (o g) c")).then_inc(slc_in, 16)
                            sp.dma_start(kwin[:, :, :], a["win_k"][s]).then_inc(slc_in, 16)
                            if s >= 2:
                                sp.wait_ge(cmp_done, 2 * (s - 1))
                            for n in range(PAGES):
                                for buf, src in ((kcmp, a["ck_cmp"]), (vcmp, a["cv_cmp"])):
                                    sp.dma_start(buf[:, s % 2, :, n * PAGE:(n + 1) * PAGE], src[bass.ds(page[n], 1)]
                                                 .rearrange("o p g c -> p (o g) c")).then_inc(cmp_in[s % 2], 16)
                            sp.wait_ge(slc_in, 16 * (PAGES + 1) * (s + 1))
                            sp.dma_start(o["win_k"][s], kwin[:, :, :]).then_inc(stores, 16)
                        sp.wait_ge(stores, state["stores"])

                    @block.tensor
                    def _(pe):
                        pe.wait_ge(stage_in, landed)
                        for kv in range(2):
                            for l in range(CL):
                                mm = pe.matmul(P[:, 3, kv:kv + 1], cw[:, kv, l, :], pe_[:, kv, l:l + 1],
                                               start=l == 0, stop=l == CL - 1)
                        mm.then_inc(peb_done, 1)
                        pe.wait_ge(q_ready, 1)
                        for s in range(NS + 1):
                            if s < NS:
                                pe.wait_ge(slc_in, 16 * (PAGES + 1) * (s + 1))
                                for gp in range(2):
                                    for bank, keys in ((0, kslc[:, gp, 0:512]), (1, kslc[:, gp, 512:1024]),
                                                       (2, kwin[:, gp, :])):
                                        mm = pe.matmul(P[64 * gp:64 * gp + 64, bank, :], QZ[:, gp, s, :], keys,
                                                       start=s == 0, stop=s == NS - 1)
                                mm.then_inc(scored, 1)
                                pe.wait_ge(cmp_in[s % 2], 32 * PAGES * (s // 2 + 1))
                            for kv, buf in ((0, kcmp), (1, vcmp)):
                                if s >= 2:
                                    pe.wait_ge(cmp_free, 2 * (s - 2) + kv + 1)
                                nc_, width = (NC_S, 2 * NC_S) if s < NS else (NC_P, 2 * NC_P)
                                for l in range(CL):
                                    rows = slice(l, l + CS * (nc_ - 1) + 1, CS)
                                    src = buf[:, s % 2, :, rows] if s < NS else Z[:, KB(kv, 0):KB(kv, 0) + 2, rows]
                                    mm = pe.matmul(P[:, 4 + 2 * kv + s % 2, 0:width]
                                                   .rearrange("p (g c) -> p g c", g=2), cw[:, kv, l, :], src,
                                                   start=l == 0, stop=l == CL - 1)
                                mm.then_inc(cmp_done, 1)
                        pe.wait_ge(ksq_ready, 1)
                        pe.wait_ge(cmp_free, 2 * NS + 2)
                        for n in range(3):
                            mm = pe.matmul(P[:, 4 + n, 0:N3], headones[:, :], sq[:, n * N3:(n + 1) * N3],
                                           start=True, stop=True)
                        mm.then_inc(kss_ready, 1)
                        pe.wait_ge(kc_ready, 1)
                        for gp in range(2):
                            rows = P[64 * gp:64 * gp + 64, 3, :]
                            for s in range(NS):
                                pe.matmul(rows[:, 0:NC_S], QZ[:, gp, s, :], KCb[:, s, gp, :],
                                          start=s == 0, stop=s == NS - 1)
                            pe.matmul(rows[:, 64:72], QA[:, gp, :], Z[:, KB(2, gp), SEQ:T], start=True, stop=True)
                            pe.matmul(rows[:, 72:80], QA[:, gp, :], Z[:, KB(4, gp), SEQ:T], start=True, stop=True)
                        for s in range(NS):
                            for gp in range(2):
                                c = (2 * s + gp) * 128
                                mm = pe.transpose(P[0:NC_S, 4 + c // 512, c % 512:c % 512 + 128],
                                                  VCb[:, s, gp, :], ident[:, :])
                        mm.then_inc(vturned, 1)
                        pe.wait_ge(vct_copied, 2)
                        for j in range(4):
                            for gp in range(2):
                                mm = pe.matmul(P[32 * j:32 * j + 32, 4, gp * 128:(gp + 1) * 128],
                                               VCb[:, NS, gp, 0:32], ident[:, :], start=True, stop=True)
                        mm.then_inc(vturned, 1)

                    @block.scalar
                    def _(act):
                        act.wait_ge(cmp_free, 2 * NS + 2)
                        act.activation(sq, kflat, ACT.Square).then_inc(ksq_ready, 1)
                        act.wait_ge(kvar_ready, 1)
                        act.activation(kr, kr, ACT.Sqrt).then_inc(kroot_ready, 1)
                        act.wait_ge(vturned, 1)
                        for half in range(2):
                            act.activation(VCt[0:NC_S, 4 * half:4 * half + 4, :],
                                           P[0:NC_S, 4 + 2 * half:6 + 2 * half, :]
                                           .rearrange("p b (s d) -> p (b s) d", s=2),
                                           ACT.Copy).then_inc(vct_copied, 1)
                        act.wait_ge(vturned, 2)
                        act.activation(VCp[:, :], P[:, 4, 0:256], ACT.Copy).then_inc(vct_copied, 1)

                    @block.vector
                    def _(dve):
                        step = Chain(dve, dve_step, "dve")
                        step(dve.memset(QZ[:, :, :, :], 0.0))
                        step(dve.memset(QA[:, :, :], 0.0))
                        step(dve.memset(KCb[:, NS, :, :], 0.0))
                        step(dve.memset(VCb[:, NS, :, :], 0.0))
                        for gp in range(2):
                            for g2 in range(2):
                                r = slice(64 * g2, 64 * g2 + 64)
                                step(dve.tensor_copy(
                                    QA[r, gp, 32 * g2:32 * g2 + 24].rearrange("p (s r) -> p s r", r=REP),
                                    Z[r, 2 + 3 * gp:5 + 3 * gp, SEQ:T].rearrange("p r s -> p s r")))
                        for s in range(NS):
                            step(dve.tensor_copy(
                                QZ[:, :, s, :].rearrange("p g (h c) -> p g h c", h=2)[:, :, :, 3 * s:3 * s + 3],
                                QA[:, :, :].rearrange("p g (h c) -> p g h c", h=2)[:, :, :, 3 * s:3 * s + 3]))
                        dve.sem_inc(q_ready, 1)
                        dve.wait_ge(peb_done, 1)
                        step(dve.tensor_copy(peb[:, :], P[:, 3, 0:2]))
                        for s in range(NS + 1):
                            for kv, dst in ((0, KCb), (1, VCb)):
                                n = NC_S if s < NS else NC_P
                                dve.wait_ge(cmp_done, 2 * s + kv + 1)
                                dve.tensor_scalar(dst[:, s, :, 0:n],
                                                  P[:, 4 + 2 * kv + s % 2, 0:2 * n].rearrange("p (g c) -> p g c", g=2),
                                                  peb[:, kv:kv + 1], None, ALU.add).then_inc(cmp_free, 1)
                        dve.wait_ge(kss_ready, 1)
                        step(dve.tensor_scalar(kr.rearrange("p (n c) -> p n c", n=3), P[:, 4:7, 0:N3],
                                               1.0 / HD, EPS, ALU.mult, ALU.add))
                        dve.reciprocal(kr, kr).then_inc(kvar_ready, 1)
                        dve.wait_ge(kroot_ready, 1)
                        dve.scalar_tensor_tensor(out=kflat, in0=kflat, scalar=vec[:, V_KG:V_KG + 1], in1=kr,
                                                 op0=ALU.mult, op1=ALU.mult).then_inc(kc_ready, 1)

        def sample_attention(mix, gates, Vn, VCt):
            with ExitStack() as ctx:
                S = sb(ctx, "S", [128, NCOL])
                bias = sb(ctx, "bias", [128, NCOL])
                samegs = sb(ctx, "samegs", [128, 128])
                blockno = sb(ctx, "blockno", [128, 14])
                own_sample = sb(ctx, "own_sample", [NS, 128])
                own_head = sb(ctx, "own_head", [128, HEADS])
                gall = sb(ctx, "gall", [128, HEADS, 3])
                grow = sb(ctx, "grow", [128, 3])
                PT = sb(ctx, "PT", [128, 15, 128])
                vs = sb(ctx, "vs", [128, 2, PAGES, 256])
                vw = sb(ctx, "vw", [128, 2, WIN // 128, 256])
                pages = sb(ctx, "pages2", [1, NS * PAGES], I32)
                st = sb(ctx, "st", [128, 64])
                v_in = [sem(f"v_in{i}") for i in range(2)]
                grow_done = sem("grow_done")
                mx_ready = sem("mx_ready")
                exp_done = sem("exp_done")
                pc_ready = sem("pc_ready")
                imp_done = sem("imp_done")
                p_ready = sem("p_ready")
                pturned = sem("pturned")
                pt_ready = sem("pt_ready")
                pv_done = sem("pv_done")
                state["stage"] += 96
                landed = state["stage"]
                state["stores"] += 16 * NS
                BR = ((C_CMP, NCOL), (C_SLC, C_WIN), (C_WIN, C_CMP))
                PIECES = [(128 * t, 128) for t in range(8)] + [(C_WIN + 128 * t, 128) for t in range(4)] \
                    + [(C_CMP, NC_S), (C_NSLC, NS), (C_NWIN, NS)]

                with nc.Block(no_gpsimd_drain=True) as block:
                    @block.sync
                    def _(sp):
                        for dst, src in ((bias[:, :], "sbias"), (samegs[:, :], "samegs"), (blockno[:, :], "blockno"),
                                         (own_sample[:, :], "own_sample"), (own_head[:, :], "own_head"),
                                         (pages[:, :], "page_table")):
                            sp.dma_start(dst, a[src]).then_inc(stage_in, 16)
                        sp.wait_ge(stage_in, landed)
                        for s in range(NS):
                            page = [sp.value_load(pages[0:1, s * PAGES + n:s * PAGES + n + 1], min_val=0,
                                                  max_val=a["cv_slc"].shape[0] - 1) for n in range(PAGES)]
                            if s >= 2:
                                sp.wait_ge(pv_done, s - 1)
                                sp.wait_ge(stores, state["stores"] - 16 * NS + 16 * (s - 1))
                            for n in range(PAGES):
                                sp.dma_start(vs[:, s % 2, n, :], a["cv_slc"][bass.ds(page[n], 1)]
                                             .rearrange("o p c -> (o p) c")).then_inc(v_in[s % 2], 16)
                            sp.dma_start(vw[:, s % 2, :, :], a["win_v"][s]).then_inc(v_in[s % 2], 16)
                            sp.wait_ge(v_in[s % 2], 16 * (PAGES + 1) * (s // 2 + 1))
                            sp.dma_start(o["win_v"][s], vw[:, s % 2, :, :]).then_inc(stores, 16)
                        sp.wait_ge(stores, state["stores"])

                    @block.tensor
                    def _(pe):
                        pe.wait_ge(stage_in, landed)
                        pe.matmul(P[:, 5, 0:36], own_sample[:, :], gates[0:NS, NQ, :], start=True, stop=True)\
                          .then_inc(grow_done, 1)
                        pe.wait_ge(pc_ready, 1)
                        pe.matmul(P[:, 4, 0:NC_S], samegs[:, :], S[:, C_CMP:NCOL], start=True, stop=True)\
                          .then_inc(imp_done, 1)
                        pe.wait_ge(p_ready, 1)
                        for i, (c, n) in enumerate(PIECES):
                            mm = pe.transpose(P[0:n, 4 + i // 4, i % 4 * 128:i % 4 * 128 + 128], S[:, c:c + n],
                                              ident[:, :])
                        mm.then_inc(pturned, 1)
                        pe.wait_ge(pt_ready, 1)
                        for gp in range(2):
                            for b in range(2):
                                pe.matmul(P[:, gp, 0:64], Vn[:, b, gp * 128:(gp + 1) * 128],
                                          PT[0:NS, 13 + b, 64 * gp:64 * gp + 64], start=b == 0, stop=b == 1)
                        for s in range(NS):
                            pe.wait_ge(v_in[s % 2], 16 * (PAGES + 1) * (s // 2 + 1))
                            for gp in range(2):
                                d = slice(gp * 128, gp * 128 + 128)
                                own = lambda ap: ap.rearrange("p (g c) -> p g c", g=2)[:, :, 3 * s:3 * s + 3]
                                out = own(P[:, gp, 0:64])
                                for i in range(13):
                                    n = PIECES[i][1]
                                    v = vs[:, s % 2, i, d] if i < 8 else vw[:, s % 2, i - 8, d] if i < 12 \
                                        else VCt[0:n, s, d]
                                    mm = pe.matmul(out, v, own(PT[0:n, i, 64 * gp:64 * gp + 64]), start=False,
                                                   stop=i == 12, skip_group_check=True)
                            mm.then_inc(pv_done, 1)

                    @block.scalar
                    def _(act):
                        for i, b in enumerate((0, 1, 2)):
                            act.wait_ge(mx_ready, i + 1)
                            x = S[:, BR[b][0]:BR[b][1]]
                            act.activation(x, x, ACT.Exp, bias=st[:, b:b + 1], accum_out=st[:, 4 + b:5 + b])\
                               .then_inc(exp_done, 1)
                        act.wait_ge(pturned, 1)
                        step = Chain(act, act_step, "act")
                        step(act.activation(PT[:, 0:12, :], P[:, 4:7, :].rearrange("p b (i c) -> p (b i) c", i=4),
                                            ACT.Copy))
                        step(act.activation(PT[0:NC_S, 12, :], P[0:NC_S, 7, 0:128], ACT.Copy))
                        act.activation(PT[0:NS, 13:15, :], P[0:NS, 7, 128:384].rearrange("p (b c) -> p b c", b=2),
                                       ACT.Copy).then_inc(pt_ready, 1)

                    @block.vector
                    def _(dve):
                        step = Chain(dve, dve_step, "dve")
                        dve.wait_ge(stage_in, landed)
                        add = lambda c, n, ps: step(dve.tensor_tensor(S[:, c:c + n], ps, bias[:, c:c + n], ALU.add))
                        add(C_CMP, NC_S, P[:, 3, 0:NC_S])
                        add(C_SLC, PAST, P[:, 0:2, :].rearrange("p b c -> p (b c)"))
                        add(C_NSLC, NS, P[:, 3, 64:72])
                        add(C_WIN, WIN, P[:, 2, :])
                        add(C_NWIN, NS, P[:, 3, 72:80])

                        def maximum(b):
                            dve.tensor_reduce(st[:, b:b + 1], S[:, BR[b][0]:BR[b][1]], AX.X, ALU.max, negate=True)\
                               .then_inc(mx_ready, 1)

                        def scale(b, gate):
                            c = st[:, 4 + b:5 + b]
                            step(dve.tensor_scalar(c, c, 1e-30, None, ALU.max))
                            step(dve.reciprocal(c, c))
                            if gate:
                                step(dve.tensor_tensor(c, c, grow[:, b:b + 1], ALU.mult))
                            x = S[:, BR[b][0]:BR[b][1]]
                            return dve.tensor_scalar(x, x, c, None, ALU.mult)

                        maximum(0)
                        dve.wait_ge(grow_done, 1)
                        step(dve.tensor_tensor(gall[:, :, :], P[:, 5, 0:36].rearrange("p (h b) -> p h b", b=3),
                                               own_head[:, :].unsqueeze(2).to_broadcast([128, HEADS, 3]), ALU.mult))
                        step(dve.tensor_reduce(grow[:, :], gall[:, :, :].rearrange("p h b -> p b h"), AX.X, ALU.add))
                        dve.wait_ge(exp_done, 1)
                        scale(0, False).then_inc(pc_ready, 1)
                        dve.wait_ge(imp_done, 1)
                        score, last = st[:, 16:30], st[:, 10:11]
                        step(dve.tensor_reduce(score, P[:, 4, 4:60].rearrange("p (b c) -> p b c", c=4), AX.X, ALU.add))
                        step(dve.tensor_tensor(score, score, P[:, 4, 3:56:4], ALU.add))
                        step(dve.tensor_reduce(st[:, 8:9], score, AX.X, ALU.min))
                        step(dve.tensor_scalar(score, score, st[:, 8:9], None, ALU.is_le))
                        step(dve.tensor_tensor(score, score, blockno[:, :], ALU.mult))
                        step(dve.tensor_reduce(last, score, AX.X, ALU.max))
                        step(dve.tensor_scalar(score, blockno[:, :], last, NEG, ALU.is_equal, ALU.mult))
                        sel = S[:, 64:960].rearrange("p (b c) -> p b c", b=14)
                        step(dve.tensor_tensor(sel, sel, score.unsqueeze(2).to_broadcast([128, 14, 64]), ALU.add))
                        maximum(1)
                        maximum(2)
                        x = S[:, C_CMP:NCOL]
                        step(dve.tensor_scalar(x, x, grow[:, 0:1], None, ALU.mult))
                        dve.wait_ge(exp_done, 2)
                        step(scale(1, True))
                        dve.wait_ge(exp_done, 3)
                        scale(2, True).then_inc(p_ready, 1)
                        dve.wait_ge(pv_done, NS)
                        for gp in range(2):
                            for g2 in range(2):
                                r = slice(64 * g2, 64 * g2 + 64)
                                step(dve.tensor_copy(mix[r, 2 + 3 * gp:5 + 3 * gp, SEQ:T],
                                                     P[r, gp, 32 * g2:32 * g2 + 24]
                                                     .rearrange("p (s r) -> p r s", r=REP)))

        def prompt_attention(mix, Z, gates, Vt, VCp, KCb, KB):
            with ExitStack() as ctx:
                dist = sb(ctx, "dist", [128, 512])
                cbias = sb(ctx, "cbias", [128, NQ, HEADS, 32])
                cok = sb(ctx, "cok", [128, NQ, 1, 32])
                Pc = sb(ctx, "Pc", [128, NQ, HEADS, 32])
                PcT = sb(ctx, "PcT", [128, NQ, 3, 128])
                cst = sb(ctx, "cst", [128, 2, NQ * HEADS])
                S = sb(ctx, "S_", [128, 3, 2, 512])
                PT = sb(ctx, "PT_", [128, 2, 2, 512])
                st = sb(ctx, "st_", [128, 3, 4])
                cscored = sem("cscored")
                cmx_ready = sem("cmx_ready")
                cexp_done = sem("cexp_done")
                cp_ready = sem("cp_ready")
                cturned = sem("cturned")
                cpt_ready = sem("cpt_ready")
                s_done = sem("s_done")
                s_read = sem("s_read")
                m_ready = sem("m_ready")
                e_done = sem("e_done")
                pr_ready = sem("pr_ready")
                t_done = sem("t_done")
                t_copied = sem("t_copied")
                o_done = sem("o_done")
                o_copied = sem("o_copied")
                state["stage"] += 48
                landed = state["stage"]
                UNITS = [(gp, r, i, g2) for gp in range(2) for r in range(REP) for i in range(NQ) for g2 in range(2)]
                NUN = len(UNITS)
                head = lambda gp, r, g2: g2 * 6 + gp * 3 + r
                gate_col = lambda gp, r, g2, b: 9 * (2 * gp + g2) + 3 * r + b

                with nc.Block(no_gpsimd_drain=True) as block:
                    @block.sync
                    def _(sp):
                        sp.dma_start(cbias[:, :, :, :], a["cmpbias"]).then_inc(stage_in, 16)
                        sp.dma_start(cok[:, :, :, :], a["cmpok"]).then_inc(stage_in, 16)
                        sp.dma_start(dist[:, :], a["dist"]).then_inc(stage_in, 16)

                    @block.tensor
                    def _(pe):
                        for i in range(NQ):
                            for gp in range(2):
                                for r in range(REP):
                                    for g2 in range(2):
                                        q = slice(64 * g2, 64 * g2 + 64)
                                        c = 32 * head(gp, r, 0)
                                        mm = pe.matmul(P[:, 4 * g2 + i, c:c + 32], Z[q, 2 + 3 * gp + r, i * 128:i * 128 + 128],
                                                       KCb[q, NS, gp, 0:32], start=True, stop=True)
                        mm.then_inc(cscored, 1)
                        pe.wait_ge(cp_ready, 1)
                        for i in range(NQ):
                            for n in range(3):
                                mm = pe.transpose(P[:, 4 + i, n * 128:n * 128 + 128],
                                                  Pc[:, i, 4 * n:4 * n + 4, :].rearrange("p h c -> p (h c)"),
                                                  ident[:, :])
                        mm.then_inc(cturned, 1)

                        def scores(u):
                            gp, r, i, g2 = UNITS[u]
                            if u >= 2:
                                pe.wait_ge(s_read, u - 1)
                            else:
                                pe.wait_ge(cp_ready, 1)
                            q = slice(64 * g2, 64 * g2 + 64)
                            for b in range(2):
                                mm = pe.matmul(P[:, u % 2 * 2 + b, 0:128 * (i + 1)],
                                               Z[q, 2 + 3 * gp + r, i * 128:i * 128 + 128],
                                               Z[q, KB(2 + 2 * b, gp), 0:128 * (i + 1)], start=True, stop=True)
                            mm.then_inc(s_done, 1)

                        def turn(u):
                            pe.wait_ge(pr_ready, u + 1)
                            if u >= 1:
                                pe.wait_ge(t_copied, u)
                            else:
                                pe.wait_ge(cpt_ready, 1)
                            i = UNITS[u][2]
                            for b in range(2):
                                for t in range(i + 1):
                                    mm = pe.transpose(P[:, 4 + b, t * 128:t * 128 + 128],
                                                      S[:, u % 3, b, t * 128:t * 128 + 128], ident[:, :])
                            mm.then_inc(t_done, 1)

                        def values(u):
                            gp, r, i, g2 = UNITS[u]
                            pe.wait_ge(t_copied, u + 1)
                            pair = u // 8
                            if u % 8 == 0 and pair >= 2:
                                pe.wait_ge(o_copied, pair - 1)
                            out = P[64 * g2:64 * g2 + 64, 6 + pair % 2, i * 128:i * 128 + 128]
                            d = slice(128 * gp + 64 * g2, 128 * gp + 64 * g2 + 64)
                            hh = head(gp, r, g2)
                            k = slice(32 * (hh % 4), 32 * (hh % 4) + 32)
                            first = True
                            for b in range(2):
                                for t in range(i + 1):
                                    pe.matmul(out, Vt[:, b, t, d], PT[:, u % 2, b, t * 128:t * 128 + 128],
                                              start=first, stop=False)
                                    first = False
                            pe.matmul(out, VCp[k, d], PcT[k, i, hh // 4, :], start=False, stop=True)\
                              .then_inc(o_done, 1)

                        for u in range(NUN + 2):
                            if u < NUN:
                                scores(u)
                            if 1 <= u <= NUN:
                                turn(u - 1)
                            if u >= 2:
                                values(u - 2)

                    @block.scalar
                    def _(act):
                        act.wait_ge(cmx_ready, 1)
                        act.activation(Pc[:, :, :, :], Pc[:, :, :, :], ACT.Exp).then_inc(cexp_done, 1)
                        act.wait_ge(cturned, 1)
                        act.activation(PcT[:, :, :, :].rearrange("p i n c -> p i (n c)"), P[:, 4:8, 0:384],
                                       ACT.Copy).then_inc(cpt_ready, 1)

                        for u in range(NUN + 2):
                            if u < NUN:
                                act.wait_ge(m_ready, u + 1)
                                n = 128 * (UNITS[u][2] + 1)
                                for b in range(2):
                                    mm = act.activation(S[:, u % 3, b, 0:n], S[:, u % 3, b, 0:n], ACT.Exp,
                                                        bias=st[:, u % 3, b:b + 1],
                                                        accum_out=st[:, u % 3, 2 + b:3 + b])
                                mm.then_inc(e_done, 1)
                            if u >= 2:
                                v = u - 2
                                act.wait_ge(t_done, v + 1)
                                if v >= 2:
                                    act.wait_ge(o_done, v - 1)
                                n = 128 * (UNITS[v][2] + 1)
                                act.activation(PT[:, v % 2, :, 0:n], P[:, 4:6, 0:n], ACT.Copy).then_inc(t_copied, 1)

                    @block.vector
                    def _(dve):
                        step = Chain(dve, dve_step, "dve")
                        dve.wait_ge(stage_in, landed)
                        dve.wait_ge(cscored, 1)
                        flat = lambda x, g2: x[:, :, 6 * g2:6 * g2 + 6, :].rearrange("p i h c -> p i (h c)")
                        for g2 in range(2):
                            step(dve.tensor_tensor(flat(Pc, g2), P[:, 4 * g2:4 * g2 + 4, 0:192], flat(cbias, g2),
                                                   ALU.add))
                        rows = Pc[:, :, :, :].rearrange("p i h c -> p (i h) c")
                        mx, sm = cst[:, 0, :], cst[:, 1, :]
                        wide = lambda x: x.unsqueeze(2).to_broadcast([128, NQ * HEADS, 32])
                        step(dve.tensor_reduce(mx, rows, AX.X, ALU.max))
                        dve.tensor_tensor(rows, rows, wide(mx), ALU.subtract).then_inc(cmx_ready, 1)
                        dve.wait_ge(cexp_done, 1)
                        step(dve.tensor_tensor(Pc[:, :, :, :], Pc[:, :, :, :],
                                               cok[:, :, :, :].to_broadcast([128, NQ, HEADS, 32]), ALU.mult))
                        step(dve.tensor_reduce(sm, rows, AX.X, ALU.add))
                        step(dve.tensor_scalar(sm, sm, 1e-30, None, ALU.max))
                        step(dve.reciprocal(sm, sm))
                        for gp in range(2):
                            for g2 in range(2):
                                c = gate_col(gp, 0, g2, 0)
                                x = sm.rearrange("p (i g q r) -> p i g q r", i=NQ, q=2, g=2)[:, :, g2, gp, :]
                                step(dve.tensor_tensor(x, x, gates[:, 0:NQ, c:c + 7:3], ALU.mult))
                        dve.tensor_tensor(rows, rows, wide(sm), ALU.mult).then_inc(cp_ready, 1)

                        def copy_out(pair):
                            dve.wait_ge(o_done, 8 * (pair + 1))
                            dve.tensor_copy(mix[:, 2 + pair, 0:SEQ], P[:, 6 + pair % 2, :]).then_inc(o_copied, 1)

                        for u in range(NUN + 1):
                            if u < NUN:
                                gp, r, i, g2 = UNITS[u]
                                n = 128 * (i + 1)
                                dve.wait_ge(s_done, u + 1)
                                if u >= 3:
                                    dve.wait_ge(t_done, u - 2)
                                slope = float(SLOPE[(2 * gp + g2) * REP + r])
                                for b in range(2):
                                    mm = dve.scalar_tensor_tensor(
                                        out=S[:, u % 3, b, 0:n], in0=dist[:, 512 - n:512], scalar=slope,
                                        in1=P[:, u % 2 * 2 + b, 0:n], op0=ALU.mult, op1=ALU.add)
                                mm.then_inc(s_read, 1)
                                dve.wait_ge(s_read, u + 1)
                                dve.tensor_reduce(st[:, u % 3, 0:2], S[:, u % 3, :, 0:n], AX.X, ALU.max, negate=True)\
                                   .then_inc(m_ready, 1)
                            if u >= 1:
                                v = u - 1
                                gp, r, i, g2 = UNITS[v]
                                n = 128 * (i + 1)
                                dve.wait_ge(e_done, v + 1)
                                sums = st[:, v % 3, 2:4]
                                step(dve.tensor_scalar(sums, sums, 1e-30, None, ALU.max))
                                step(dve.reciprocal(sums, sums))
                                c = gate_col(gp, r, g2, 1)
                                step(dve.tensor_tensor(sums, sums, gates[:, i, c:c + 2], ALU.mult))
                                for b in range(2):
                                    x = S[:, v % 3, b, 0:n]
                                    mm = dve.tensor_scalar(x, x, sums[:, b:b + 1], None, ALU.mult)
                                mm.then_inc(pr_ready, 1)
                            if u >= 10 and (u - 10) % 8 == 0:
                                copy_out((u - 10) // 8)
                        copy_out(NUN // 8 - 1)

        def layer1():
            with ExitStack() as c0:
                R, K, V = (sb(c0, n, [128, KC, T]) for n in ("R", "K", "V"))
                tg = sb(c0, "tg", [128, T])
                tw = sb(c0, "tw", [64, T])
                ta = sb(c0, "ta", [64, T])
                mix_and_project(R, K, V, tw, ta, tg)
                L = sb(c0, "L", [128, KC, T])
                A = sb(c0, "A", [128, KC, T])
                N_ = sb(c0, "N_", [128, KC, T])
                rates(R, K, L, A, N_, tw, ta)
                chunks(R, K, V, L, A, N_)
                sample_state(R, K, V, L, A, N_)
                output(R, K, V, L, A, tg)

        def mix_and_project(R, K, V, tw, ta, tg):
            with ExitStack() as ctx:
                xn = sb(ctx, "xn1", [128, KC, T])
                xx = sb(ctx, "xx", [128, KC, T])
                xm = sb(ctx, "xm", [128, KC, T])
                prev = sb(ctx, "prev", [128, KC, NS])
                lw = sb(ctx, "lw", [128, KC, 64])
                la = sb(ctx, "la", [128, KC, 64])
                lg = sb(ctx, "lg", [128, KC, 128])
                mixed = sem("mixed")
                low_done = sem("low_done")
                low_free = sem("low_free")
                normed = sem("normed")
                ORDER = ((1, (lw, tw, 64, ACT.Tanh)), (4, (la, ta, 64, ACT.Copy)), (5, (lg, tg, 128, ACT.Sigmoid)),
                         (0, R), (2, K), (3, V))
                firsts = [plan(list(range(U_R + 4 * j, U_R + 4 * j + 4))) for j in range(3)]
                i = state["norm"]
                state["norm"] += 1
                state["stage"] += 64
                landed = state["stage"]
                state["stores"] += 16

                with nc.Block(no_gpsimd_drain=True) as block:
                    @block.sync
                    def _(sp):
                        for dst, src in ((prev, "state_shift"), (lw, "rwkv_w1"), (la, "rwkv_a1"), (lg, "rwkv_g1")):
                            sp.dma_start(dst[:, :, :], a[src]).then_inc(stage_in, 16)
                        stream_weights(sp, U_WO)
                        sp.wait_ge(normed, 1)
                        sp.dma_start(o["shift"], xn[:, :, SEQ - 1:T]).then_inc(stores, 16)
                        stream_weights(sp, U_WO + 1)
                        sp.wait_ge(stores, state["stores"])

                    @block.tensor
                    def _(pe):
                        norm_pe(pe, i, xn)
                        for j in range(3):
                            w, _, n, _ = ORDER[j][1]
                            for k in range(KC):
                                pe.wait_ge(mixed, j * KC + k + 1)
                                for hf in range(2):
                                    mm = pe.matmul(P[0:n, 2 * j + hf, 0:HT], w[:, k, :],
                                                   xm[:, k, hf * HT:(hf + 1) * HT], start=k == 0, stop=k == KC - 1)
                            mm.then_inc(low_done, 1)
                        pe.wait_ge(low_free, 3)
                        for j in range(3):
                            dense(pe, firsts[j], list(range(U_R + 4 * j, U_R + 4 * j + 4)), lambda k: xm[:, k, :],
                                  chunk_ready=lambda k, j=j: pe.wait_ge(mixed, (3 + j) * KC + k + 1))

                    @block.scalar
                    def _(act):
                        norm_act(act, i, xn)
                        for j in range(3):
                            _, dst, n, f = ORDER[j][1]
                            act.wait_ge(low_done, j + 1)
                            act.activation(halves(dst[0:n, :]), P[0:n, 2 * j:2 * j + 2, 0:HT], f).then_inc(low_free, 1)
                        for j, dst in enumerate((R, K, V)):
                            for m in range(KC):
                                act.wait_ge(tile_done, firsts[j] + m + 1)
                                act.activation(halves(dst[:, m, :]), tile(firsts[j] + m), ACT.Copy)\
                                   .then_inc(tile_free, 1)

                    @block.vector
                    def _(dve):
                        step = Chain(dve, dve_step, "dve")
                        norm_dve(dve, step, i, xn, V_MIX + KC)
                        dve.wait_ge(xn_ready, (i + 1) * KC)
                        dve.wait_ge(stage_in, landed)
                        dve.tensor_tensor(xx[:, :, 1:SEQ], xn[:, :, 0:SEQ - 1], xn[:, :, 1:SEQ], ALU.subtract)\
                           .then_inc(normed, 1)
                        dve.tensor_scalar(xx[:, :, 0:1], xn[:, :, 0:1], -1.0, None, ALU.mult)
                        step(dve.tensor_tensor(xx[:, :, SEQ:T], prev[:, :, :], xn[:, :, SEQ:T], ALU.subtract))
                        dve.wait_ge(normed, 1)
                        for j, (mu, _) in enumerate(ORDER):
                            if 1 <= j <= 3:
                                dve.wait_ge(low_done, j)
                            elif j > 3:
                                dve.wait_ge(tile_done, firsts[j - 4] + KC)
                            for k in range(KC):
                                c = V_MU + KC * mu + k
                                dve.scalar_tensor_tensor(out=xm[:, k, :], in0=xx[:, k, :], scalar=vec[:, c:c + 1],
                                                         in1=xn[:, k, :], op0=ALU.mult, op1=ALU.add)\
                                   .then_inc(mixed, 1)

        def rates(R, K, L, A, N_, tw, ta):
            with ExitStack() as ctx:
                w2 = sb(ctx, "w2", [64, D])
                a2 = sb(ctx, "a2", [64, D])
                sq = sb(ctx, "sq2", [128, 2, T])
                lo_done = sem("lo_done")
                lo_free = sem("lo_free")
                kk_sq = sem("kk_sq")
                kk_ss = sem("kk_ss")
                kk_read = sem("kk_read")
                kk_root = sem("kk_root")
                state["stage"] += 32
                landed = state["stage"]
                with nc.Block(no_gpsimd_drain=True) as block:
                    @block.sync
                    def _(sp):
                        sp.dma_start(w2[:, :], a["rwkv_w2"]).then_inc(stage_in, 16)
                        sp.dma_start(a2[:, :], a["rwkv_a2"]).then_inc(stage_in, 16)

                    @block.tensor
                    def _(pe):
                        pe.wait_ge(stage_in, landed)
                        for n in range(2 * KC):
                            if n >= 2:
                                pe.wait_ge(lo_free, n - 1)
                            w, x = ((w2, tw), (a2, ta))[n // KC]
                            m = n % KC
                            for hf in range(2):
                                mm = pe.matmul(P[:, 2 * (n % 2) + hf, 0:HT], w[:, m * 128:(m + 1) * 128],
                                               x[:, hf * HT:(hf + 1) * HT], start=True, stop=True)
                            mm.then_inc(lo_done, 1)
                        for m in range(KC):
                            pe.wait_ge(kk_sq, m + 1)
                            if m >= 2:
                                pe.wait_ge(kk_root, m - 1)
                            for hf in range(2):
                                mm = pe.matmul(P[:, 4 + 2 * (m % 2) + hf, 0:HT], headones[:, :],
                                               sq[:, m % 2, hf * HT:(hf + 1) * HT], start=True, stop=True)
                            mm.then_inc(kk_ss, 1)

                    @block.scalar
                    def _(act):
                        for n in range(2 * KC):
                            dst, col = ((L, V_W0), (A, V_A0))[n // KC]
                            m = n % KC
                            act.wait_ge(lo_done, n + 1)
                            act.activation(halves(dst[:, m, :]), P[:, 2 * (n % 2):2 * (n % 2) + 2, 0:HT], ACT.Sigmoid,
                                           bias=vec[:, col + m:col + m + 1]).then_inc(lo_free, 1)
                        for m in range(KC):
                            act.wait_ge(kk_ss, m + 1)
                            act.activation(halves(sq[:, m % 2, :]), P[:, 4 + 2 * (m % 2):6 + 2 * (m % 2), 0:HT],
                                           ACT.Sqrt).then_inc(kk_root, 1)

                    @block.vector
                    def _(dve):
                        step = Chain(dve, dve_step, "dve")

                        def square(m):
                            c = V_KK + m
                            step(dve.tensor_scalar(N_[:, m, :], K[:, m, :], vec[:, c:c + 1], None, ALU.mult))
                            dve.tensor_tensor(sq[:, m % 2, :], N_[:, m, :], N_[:, m, :], ALU.mult).then_inc(kk_sq, 1)

                        square(0)
                        square(1)
                        for m in range(KC):
                            s = sq[:, m % 2, :]
                            dve.wait_ge(kk_root, m + 1)
                            step(dve.tensor_scalar(s, s, 1e-12, None, ALU.max))
                            step(dve.reciprocal(s, s))
                            step(dve.tensor_tensor(N_[:, m, :], N_[:, m, :], s, ALU.mult))
                            if m + 2 < KC:
                                square(m + 2)
                        dve.wait_ge(lo_free, 2 * KC)
                        Lf = L[:, :, :].rearrange("p k t -> p (k t)")
                        step(dve.tensor_scalar(Lf, Lf, -math.exp(-0.5), None, ALU.mult))
                        for m in range(KC):
                            s = sq[:, m % 2, :]
                            c = V_KA + m
                            step(dve.tensor_scalar(s, A[:, m, :], 1.0, vec[:, c:c + 1], ALU.subtract, ALU.mult))
                            step(dve.scalar_tensor_tensor(out=K[:, m, :], in0=s, scalar=1.0, in1=K[:, m, :],
                                                          op0=ALU.add, op1=ALU.mult))
                            step(dve.tensor_tensor(A[:, m, :], A[:, m, :], N_[:, m, :], ALU.mult))

        def chunks(R, K, V, L, A, N_):
            with ExitStack() as ctx:
                tri = sb(ctx, "tri", [128, 128])
                level = sb(ctx, "level", [128, 6, CH])
                ident2 = sb(ctx, "ident2", [128, 64])
                restart = sb(ctx, "restart", [128, KC, CH + 1])
                Eend = sb(ctx, "Eend", [128, 2, KC])
                Ls = sb(ctx, "Ls", [128, KC, CH + 1])
                Lc = sb(ctx, "Lc", [128, KC, CH + 1])
                Ep = sb(ctx, "Ep", [128, KC, CH + 1])
                Em = sb(ctx, "Em", [128, KC, CH + 1])
                AR = sb(ctx, "AR", [128, 2, KC, 2, CH])
                BK = sb(ctx, "BK", [128, 2, KC, CH])
                G = sb(ctx, "G", [128, 2, 2, KC, 2, CH])
                assert U_WO % RING == RING - 1
                spare = ring[:, 0:RING - 1, :].rearrange("p r c -> p (r c)")
                tm = spare[:, 0:3072].rearrange("p (d j n t) -> p d j n t", d=2, j=3, n=KC)
                TU = spare[:, 3072:4096].rearrange("p (h w n t) -> p h w n t", h=2, w=2, n=4)
                Uf = spare[:, 4096:5120].rearrange("p (d n t) -> p d n t", d=2, n=KC)
                XL = spare[:, 5120:6144].rearrange("p (d n t) -> p d n t", d=2, n=KC)
                Y = sb(ctx, "Y", [128, 2, 4, CH])
                X = sb(ctx, "X", [128, KC, CH])
                SA = sb(ctx, "SA", [128, KC, CH])
                S = sb(ctx, "S1", [128, KC, CH])
                names = ("ls_ready ep_done em_done til_ready g_done g_ready tm_done tm_ready y_done y_ready tu_done "
                         "tu_ready xl_ready x_done x_ready sa_done sa_ready o_done1 s_done1 s_ready o_read").split()
                (ls_ready, ep_done, em_done, til_ready, g_done, g_ready, tm_done, tm_ready, y_done, y_ready, tu_done,
                 tu_ready, xl_ready, x_done, x_ready, sa_done, sa_ready, o_done, s_done, s_ready, o_read) = \
                    (sem("w_" + n) for n in names)
                state["stage"] += 64
                landed = state["stage"]
                state["stores"] += 16
                LEV = 5
                half_rows = [(p, slice(64 * p, 64 * p + 64)) for p in range(2)]

                with nc.Block(no_gpsimd_drain=True) as block:
                    @block.sync
                    def _(sp):
                        for dst, src in ((tri[:, :], "tri"), (level[:, :, :], "level"), (ident2[:, :], "ident2"),
                                         (restart[:, :, :], "restart")):
                            sp.dma_start(dst, a[src]).then_inc(stage_in, 16)
                        sp.wait_ge(x_ready, NCH + 1)
                        sp.dma_start(o["wkv_p"], X[:, :, :]).then_inc(stores, 16)
                        sp.wait_ge(stores, state["stores"])

                    @block.tensor
                    def _(pe):
                        pe.wait_ge(stage_in, landed)

                        def scores(c):
                            pe.wait_ge(til_ready, c + 1)
                            for src in range(2):
                                for n in range(KC):
                                    for p, r in half_rows:
                                        mm = pe.matmul(P[r, 2 * src + n // 4, n % 4 * 128:n % 4 * 128 + 128],
                                                       BK[r, src, n, :],
                                                       AR[r, c % 2, n, :, :].rearrange("p a t -> p (a t)"),
                                                       start=True, stop=True)
                            mm.then_inc(g_done, 1)

                        def turn(c):
                            pe.wait_ge(g_ready, c + 1)
                            for j in range(3):
                                for n in range(KC):
                                    for p, r in half_rows:
                                        x = V[r, n, c * CH:(c + 1) * CH] if j == 0 else BK[r, j - 1, n, :]
                                        mm = pe.matmul(P[r, j, n * CH:(n + 1) * CH], x, ident2[r, :],
                                                       start=True, stop=True)
                            mm.then_inc(tm_done, 1)

                        def times_t(c, lv, hf):
                            e = c * (LEV + 1) + lv
                            pe.wait_ge(xl_ready, e + 1)
                            if lv:
                                pe.wait_ge(tu_ready, 2 * (e - 1) + hf + 1)
                            elif hf == 0:
                                pe.wait_ge(tm_ready, c + 1)
                            for n in range(4):
                                for p, r in half_rows:
                                    rhs = TU[r, hf, 0, n, :] if lv else ident2[r, :]
                                    mm = pe.matmul(P[r, hf, n * CH:(n + 1) * CH], XL[r, e % 2, 4 * hf + n, :], rhs,
                                                   start=True, stop=True)
                            mm.then_inc(y_done, 1)

                        def t_times(c, lv, hf):
                            e = c * (LEV + 1) + lv
                            pe.wait_ge(y_ready, 2 * e + hf + 1)
                            for which in range(2):
                                if which == 0 and lv == LEV:
                                    continue
                                for n in range(4):
                                    for p, r in half_rows:
                                        u, y = TU[r, hf, 1, n, :], Y[r, hf, n, :]
                                        w, x = (u, y) if which == 0 else (y, u)
                                        mm = pe.matmul(P[r, 2 + hf, (4 * which + n) * CH:(4 * which + n + 1) * CH],
                                                       w, x, start=True, stop=True)
                            mm.then_inc(tu_done, 1)

                        def x_part(c):
                            pe.wait_ge(s_ready, c + 1)
                            for n in range(KC):
                                for p, r in half_rows:
                                    out = P[r, 4, n * CH:(n + 1) * CH]
                                    pe.matmul(out, AR[r, c % 2, n, 0, :], S[r, n, :], start=True, stop=False)
                                    mm = pe.matmul(out, G[r, c % 2, 1, n, 0, :], tm[r, c % 2, 0, n, :],
                                                   start=False, stop=True)
                            mm.then_inc(x_done, 1)

                        def sa_part(c):
                            pe.wait_ge(x_ready, c + 1)
                            for n in range(KC):
                                for p, r in half_rows:
                                    mm = pe.matmul(P[r, 5, n * CH:(n + 1) * CH], Uf[r, c % 2, n, :], X[r, n, :],
                                                   start=True, stop=True)
                            mm.then_inc(sa_done, 1)

                        def s_part(c):
                            pe.wait_ge(sa_ready, c + 1)
                            for n in range(KC):
                                for p, r in half_rows:
                                    out = P[r, 7, n * CH:(n + 1) * CH]
                                    pe.matmul(out, tm[r, c % 2, 1, n, :], SA[r, n, :], start=True, stop=False)
                                    mm = pe.matmul(out, tm[r, c % 2, 2, n, :], tm[r, c % 2, 0, n, :],
                                                   start=False, stop=True)
                            mm.then_inc(s_done, 1)

                        def o_part(c):
                            if c:
                                pe.wait_ge(o_read, c)
                            for n in range(KC):
                                for p, r in half_rows:
                                    out = P[r, 6, n * CH:(n + 1) * CH]
                                    pe.matmul(out, S[r, n, :], AR[r, c % 2, n, 1, :], start=True, stop=False)
                                    pe.matmul(out, SA[r, n, :], G[r, c % 2, 0, n, 1, :], start=False, stop=False)
                                    mm = pe.matmul(out, tm[r, c % 2, 0, n, :], G[r, c % 2, 1, n, 1, :],
                                                   start=False, stop=True)
                            mm.then_inc(o_done, 1)

                        for c in range(NCH + 1):
                            if c < NCH:
                                scores(c)
                                turn(c)
                            if c:
                                pe.wait_ge(tu_ready, 2 * c * (LEV + 1))
                                x_part(c - 1)
                            between = [sa_part, s_part, o_part]
                            for lv in range(LEV + 1):
                                if c < NCH:
                                    times_t(c, lv, 0)
                                    times_t(c, lv, 1)
                                    if lv:
                                        t_times(c, lv, 0)
                                        t_times(c, lv, 1)
                                if c and lv < 3:
                                    between[lv](c - 1)
                        pe.wait_ge(s_ready, NCH + 1)
                        for n in range(KC):
                            for p, r in half_rows:
                                mm = pe.matmul(P[r, 4, n * CH:(n + 1) * CH], S[r, n, :], ident2[r, :],
                                               start=True, stop=True)
                        mm.then_inc(x_done, 1)

                    @block.scalar
                    def _(act):
                        def exps(c):
                            act.wait_ge(ls_ready, c + 1)
                            act.activation(Ep[:, :, :], Lc[:, :, :], ACT.Exp).then_inc(ep_done, 1)
                            act.activation(Em[:, :, :], Lc[:, :, :], ACT.Exp, scale=-1.0).then_inc(em_done, 1)

                        def copies(c):
                            act.wait_ge(tm_done, c + 1)
                            act.activation(tm[:, c % 2, :, :, :].rearrange("p j n t -> p j (n t)"), P[:, 0:3, :],
                                           ACT.Copy).then_inc(tm_ready, 1)

                        def y_copy(c, lv, hf):
                            e = c * (LEV + 1) + lv
                            act.wait_ge(y_done, 2 * e + hf + 1)
                            act.activation(Y[:, hf, :, :], P[:, hf, 0:256].rearrange("p (n t) -> p n t", n=4),
                                           ACT.Copy).then_inc(y_ready, 1)

                        def xc(c):
                            act.wait_ge(x_done, c + 1)
                            act.activation(X[:, :, :], P[:, 4, :].rearrange("p (n t) -> p n t", n=KC),
                                           ACT.Copy).then_inc(x_ready, 1)

                        def sac(c):
                            act.wait_ge(sa_done, c + 1)
                            act.activation(SA[:, :, :], P[:, 5, :].rearrange("p (n t) -> p n t", n=KC),
                                           ACT.Copy).then_inc(sa_ready, 1)

                        def oc(c):
                            act.wait_ge(o_done, c + 1)
                            act.activation(L[:, :, c * CH:(c + 1) * CH], P[:, 6, :].rearrange("p (n t) -> p n t", n=KC),
                                           ACT.Copy).then_inc(o_read, 1)

                        exps(0)
                        for c in range(NCH + 1):
                            if c < NCH:
                                copies(c)
                            if c:
                                xc(c - 1)
                            for lv in range(LEV + 1):
                                if c < NCH:
                                    y_copy(c, lv, 0)
                                    y_copy(c, lv, 1)
                                if c and lv == 0:
                                    sac(c - 1)
                                if c and lv == 2:
                                    oc(c - 1)
                                if lv == 3 and c + 1 < NCH:
                                    exps(c + 1)
                        xc(NCH)

                    @block.gpsimd
                    def _(pool):
                        pool.wait_ge(stage_in, landed)
                        for c in range(NCH):
                            pool.wait_ge(g_ready, c + 1)
                            for lv in range(LEV + 1):
                                e = c * (LEV + 1) + lv
                                if e >= 2:
                                    pool.wait_ge(tu_ready, 2 * (e - 1))
                                pool.tensor_tensor(XL[:, e % 2, :, :], G[:, c % 2, 0, :, 0, :],
                                                   level[:, lv, :].unsqueeze(1).to_broadcast([128, KC, CH]),
                                                   ALU.mult).then_inc(xl_ready, 1)

                    @block.vector
                    def _(dve):
                        step = Chain(dve, dve_step, "dve")
                        dve.wait_ge(stage_in, landed)
                        step(dve.memset(Ls[:, :, :], 0.0))
                        dve.memset(S[:, :, :], 0.0).then_inc(s_ready, 1)
                        wide = lambda x: x.unsqueeze(1).to_broadcast([128, 4, CH])
                        flat = lambda x: x.rearrange("p n t -> p (n t)")

                        def decays(c):
                            if c:
                                dve.wait_ge(em_done, c)
                            step(dve.tensor_copy(Ls[:, :, 1:], L[:, :, c * CH:(c + 1) * CH]))
                            dve.tensor_tensor_scan(flat(Lc[:, :, :]), flat(restart[:, :, :]), flat(Ls[:, :, :]), 0.0,
                                                   ALU.mult, ALU.add).then_inc(ls_ready, 1)

                        def tilde(c):
                            t = slice(c * CH, (c + 1) * CH)
                            dve.wait_ge(ep_done, c + 1)
                            step(dve.scalar_tensor_tensor(out=AR[:, c % 2, :, 0, :], in0=N_[:, :, t], scalar=-1.0,
                                                          in1=Ep[:, :, 0:CH], op0=ALU.mult, op1=ALU.mult))
                            step(dve.tensor_tensor(AR[:, c % 2, :, 1, :], R[:, :, t], Ep[:, :, 1:], ALU.mult))
                            dve.wait_ge(em_done, c + 1)
                            if c:
                                dve.wait_ge(tm_done, c)
                            step(dve.tensor_tensor(BK[:, 0, :, :], A[:, :, t], Em[:, :, 1:], ALU.mult))
                            dve.tensor_tensor(BK[:, 1, :, :], K[:, :, t], Em[:, :, 1:], ALU.mult).then_inc(til_ready, 1)

                        def mask(c):
                            dve.wait_ge(g_done, c + 1)
                            for src in range(2):
                                g = G[:, c % 2, src, :, :, :].rearrange("p n a t -> p n (a t)")
                                mm = dve.tensor_tensor(g, P[:, 2 * src:2 * src + 2, :].rearrange(
                                    "p b (n t) -> p (b n) t", n=4),
                                    tri[:, :].unsqueeze(1).to_broadcast([128, KC, 128]), ALU.mult)
                            mm.then_inc(g_ready, 1)

                        def tu_first(c, hf):
                            e = c * (LEV + 1)
                            dve.wait_ge(y_done, 2 * e + hf + 1)
                            dve.wait_ge(y_ready, 2 * e + hf + 1)
                            step(dve.tensor_tensor(TU[:, hf, 0, :, :], Y[:, hf, :, :], wide(ident2[:, :]), ALU.add))
                            dve.tensor_tensor(TU[:, hf, 1, :, :], XL[:, e % 2, 4 * hf:4 * hf + 4, :],
                                              wide(ident2[:, :]), ALU.add).then_inc(tu_ready, 1)

                        def tu(c, lv, hf):
                            e = c * (LEV + 1) + lv
                            dve.wait_ge(tu_done, 2 * (c * LEV + lv - 1) + hf + 1)
                            ps = P[:, 2 + hf, :].rearrange("p (w n t) -> p w n t", w=2, n=4)
                            if lv < LEV:
                                dve.tensor_tensor(TU[:, hf, :, :, :].rearrange("p w n t -> p (w n t)"),
                                                  TU[:, hf, :, :, :].rearrange("p w n t -> p (w n t)"),
                                                  P[:, 2 + hf, :], ALU.add).then_inc(tu_ready, 1)
                            else:
                                dve.tensor_tensor(Uf[:, c % 2, 4 * hf:4 * hf + 4, :], TU[:, hf, 1, :, :], ps[:, 1],
                                                  ALU.add).then_inc(tu_ready, 1)

                        def new_state(c):
                            dve.wait_ge(s_done, c + 1)
                            dve.wait_ge(o_done, c + 1)
                            step(dve.tensor_tensor(S[:, :, :], S[:, :, :],
                                                   P[:, 7, :].rearrange("p (n t) -> p n t", n=KC), ALU.add))
                            dve.tensor_tensor(S[:, :, :], S[:, :, :],
                                              Eend[:, c % 2, :].unsqueeze(2).to_broadcast([128, KC, CH]), ALU.mult)\
                               .then_inc(s_ready, 1)

                        decays(0)
                        for c in range(NCH + 1):
                            if c < NCH:
                                tilde(c)
                                step(dve.tensor_copy(Eend[:, c % 2, :], Ep[:, :, CH]))
                                mask(c)
                            for lv in range(LEV + 1):
                                if c < NCH:
                                    for hf in range(2):
                                        tu_first(c, hf) if lv == 0 else tu(c, lv, hf)
                                if c and lv == 2:
                                    new_state(c - 1)
                                if lv == 2 and c + 1 < NCH:
                                    decays(c + 1)

        def sample_state(R, K, V, L, A, N_):
            with ExitStack() as ctx:
                ident2 = sb(ctx, "ident3", [128, 64])
                S = sb(ctx, "Ss", [128, NS, KC, HD])
                dg = sb(ctx, "dg", [128, NS, KC, HD])
                tmp = sb(ctx, "tmp", [128, NS, KC, HD])
                sa = sb(ctx, "sa", [128, NS, KC])
                dg_ready = sem("dg_ready")
                spread = sem("spread")
                spread_read = sem("spread_read")
                out_ready = sem("out_ready")
                dec_ready = sem("dec_ready")
                state["stage"] += 32
                landed = state["stage"]
                state["stores"] += 16
                VECS = 5
                with nc.Block(no_gpsimd_drain=True) as block:
                    @block.sync
                    def _(sp):
                        sp.dma_start(ident2[:, :], a["ident2"]).then_inc(stage_in, 16)
                        sp.dma_start(S[:, :, :, :], a["state_wkv"]).then_inc(stage_in, 16)
                        stream_weights(sp, U_WO + RING)
                        sp.wait_ge(out_ready, 1)
                        sp.dma_start(o["wkv_s"], S[:, :, :, :]).then_inc(stores, 16)
                        sp.wait_ge(stores, state["stores"])

                    @block.tensor
                    def _(pe):
                        for v in range(VECS):
                            for s in range(NS):
                                n = NS * v + s
                                pe.wait_ge(dg_ready, n + 1)
                                if v:
                                    pe.wait_ge(spread_read, n - NS + 1)
                                pe.matmul(P[:, s, :], headones[:, :], dg[:, s, :, :].rearrange("p n j -> p (n j)"),
                                          start=True, stop=True).then_inc(spread, 1)

                    @block.scalar
                    def _(act):
                        act.activation(L[:, :, SEQ:T], L[:, :, SEQ:T], ACT.Exp).then_inc(dec_ready, 1)

                    @block.gpsimd
                    def _(pool):
                        pool.wait_ge(stage_in, landed)
                        pool.wait_ge(dec_ready, 1)
                        for v, x in enumerate((N_, L, A, K, R)):
                            for s in range(NS):
                                if v:
                                    pool.wait_ge(spread, NS * (v - 1) + s + 1)
                                pool.tensor_tensor(dg[:, s, :, :],
                                                   ident2[:, :].unsqueeze(1).to_broadcast([128, KC, HD]),
                                                   x[:, :, SEQ + s:SEQ + s + 1].to_broadcast([128, KC, HD]),
                                                   ALU.mult).then_inc(dg_ready, 1)

                    @block.vector
                    def _(dve):
                        step = Chain(dve, dve_step, "dve")
                        dve.wait_ge(stage_in, landed)
                        ps = lambda s: P[:, s, :].rearrange("p (n j) -> p n j", n=KC)
                        for v in range(VECS):
                            for s in range(NS):
                                dve.wait_ge(spread, NS * v + s + 1)
                                x, y = S[:, s, :, :], tmp[:, s, :, :]
                                if v == 0:
                                    step(dve.tensor_tensor(y, x, ps(s), ALU.mult))
                                    mm = dve.tensor_reduce(sa[:, s, :], y, AX.X, ALU.add, negate=True)
                                elif v == 1:
                                    mm = dve.tensor_tensor(x, x, ps(s), ALU.mult)
                                elif v < 4:
                                    by = sa[:, s, :] if v == 2 else V[:, :, SEQ + s]
                                    step(dve.tensor_tensor(y, ps(s), by.unsqueeze(2).to_broadcast([128, KC, HD]),
                                                           ALU.mult))
                                    mm = dve.tensor_tensor(x, x, y, ALU.add)
                                else:
                                    step(dve.tensor_tensor(y, x, ps(s), ALU.mult))
                                    mm = dve.tensor_reduce(sa[:, s, :], y, AX.X, ALU.add)
                                mm.then_inc(spread_read, 1)
                                dve.wait_ge(spread_read, NS * v + s + 1)
                            if v == 3:
                                dve.sem_inc(out_ready, 1)
                        step(dve.tensor_copy(L[:, :, SEQ:T].rearrange("p n s -> p s n"), sa[:, :, :]))

        def output(R, K, V, O, B, tg):
            with ExitStack() as ctx:
                g2 = sb(ctx, "g2", [128, D])
                q = sb(ctx, "q", [128, 2, T])
                rs = sb(ctx, "rs", [128, T])
                n_ready = sem("n_ready")
                n_done = sem("n_done")
                n_read = sem("n_read")
                n_var = sem("n_var")
                n_root = sem("n_root")
                state["stage"] += 16
                landed = state["stage"]
                with nc.Block(no_gpsimd_drain=True) as block:
                    @block.sync
                    def _(sp):
                        sp.dma_start(g2[:, :], a["rwkv_g2"]).then_inc(stage_in, 16)

                    @block.tensor
                    def _(pe):
                        pe.wait_ge(stage_in, landed)
                        for m in range(KC):
                            if m:
                                pe.wait_ge(n_read, m)
                            for j, (w, x) in enumerate(((headones[:, :], O[:, m, :]), (headones[:, :], q[:, 1, :]),
                                                        (g2[:, m * 128:(m + 1) * 128], tg[:, :]),
                                                        (headones[:, :], q[:, 0, :]))):
                                if j in (0, 3):
                                    pe.wait_ge(n_ready, 2 * m + j // 3 + 1)
                                for hf in range(2):
                                    mm = pe.matmul(P[:, 2 * j + hf, 0:HT], w, x[:, hf * HT:(hf + 1) * HT],
                                                   start=True, stop=True)
                                if j >= 2:
                                    mm.then_inc(n_done, 1)

                    @block.scalar
                    def _(act):
                        for m in range(KC):
                            act.wait_ge(n_var, m + 1)
                            act.activation(rs[:, :], rs[:, :], ACT.Sqrt).then_inc(n_root, 1)

                    @block.vector
                    def _(dve):
                        step = Chain(dve, dve_step, "dve")
                        sums = lambda j: P[:, 2 * j:2 * j + 2, 0:HT]
                        col = lambda c, m: vec[:, c + m:c + m + 1]
                        for m in range(KC):
                            x = O[:, m, :]
                            step(dve.tensor_tensor(q[:, 1, :], R[:, m, :], K[:, m, :], ALU.mult))
                            dve.tensor_scalar(q[:, 1, :], q[:, 1, :], col(V_RK, m), None, ALU.mult).then_inc(n_ready, 1)
                            dve.wait_ge(n_done, 2 * m + 1)
                            step(dve.scalar_tensor_tensor(out=halves(x), in0=sums(0), scalar=-1.0 / HD, in1=halves(x),
                                                          op0=ALU.mult, op1=ALU.add))
                            dve.tensor_tensor(q[:, 0, :], x, x, ALU.mult).then_inc(n_ready, 1)
                            step(dve.tensor_tensor(halves(q[:, 1, :]), halves(V[:, m, :]), sums(1), ALU.mult))
                            dve.wait_ge(n_done, 2 * m + 2)
                            step(dve.tensor_scalar(halves(rs[:, :]), sums(3), 1.0 / HD, 64e-5, ALU.mult, ALU.add))
                            dve.reciprocal(rs[:, :], rs[:, :]).then_inc(n_var, 1)
                            dve.wait_ge(n_root, m + 1)
                            step(dve.scalar_tensor_tensor(out=x, in0=x, scalar=col(V_LNW, m), in1=rs[:, :],
                                                          op0=ALU.mult, op1=ALU.mult))
                            step(dve.scalar_tensor_tensor(out=x, in0=x, scalar=col(V_LNB, m), in1=q[:, 1, :],
                                                          op0=ALU.add, op1=ALU.add))
                            dve.tensor_tensor(halves(x), halves(x), sums(2), ALU.mult).then_inc(n_read, 1)
                            dve.wait_ge(n_read, m + 1)
                add_product(O, list(range(U_WO, U_WO + 4)), "wo")

        with nc.Block(no_gpsimd_drain=True) as block:
            @block.sync
            def _(sp):
                sp.dma_start(h[:, :, :], a["x"]).then_inc(fixed_in, 16)
                sp.dma_start(vec[:, :], a["vec"]).then_inc(fixed_in, 16)
                sp.dma_start(ones[:, :], a["ones"]).then_inc(fixed_in, 16)
                sp.dma_start(ident[:, :], a["ident"]).then_inc(fixed_in, 16)
                sp.dma_start(headones[:, :], a["headones"]).then_inc(fixed_in, 16)
                stream_weights(sp, RING)
                sp.wait_ge(fixed_in, 80)

        layer0()
        tail(0, U_T0)
        layer1()
        tail(1, U_T1)
        with nc.Block(no_gpsimd_drain=True) as block:
            @block.sync
            def _(sp):
                sp.dma_start(o["y"], h[:, :, :]).then_inc(stores, 16)
                state["stores"] += 16
                sp.wait_ge(stores, state["stores"])


def kernel(**inputs):
    import concourse.bacc as bacc
    from concourse.bass_utils import run_bass_kernel_spmd as run

    x = {k: np.asarray(v) for k, v in inputs.items()}
    fm = lambda v: np.ascontiguousarray(v.reshape(v.shape[0], -1, 128).transpose(2, 1, 0))
    cols = lambda v: v.reshape(-1, 128).T

    def unit_in(w):
        return w.reshape(KC, 128, -1, 256).transpose(2, 1, 0, 3).reshape(-1, 128, UW)

    def unit_down(w):
        return w.reshape(4, KC, 128, 4, 256).transpose(3, 0, 2, 1, 4).reshape(-1, 128, UW)

    def unit_ple(w):
        return w.reshape(2, 128, D).transpose(1, 0, 2).reshape(1, 128, UW)

    order = [(2 * gp + g2) * REP + r for gp in range(2) for r in range(REP) for g2 in range(2)]
    w_in = x["even_w_in"][0]
    wq = w_in[:, 256:1024].reshape(D, HEADS, HD)[:, order].reshape(D, 768)
    w_big = np.concatenate([w_in[:, :256], wq, w_in[:, 1024:2560]], 1)
    w_out = x["even_w_out"][0]
    w_out = np.concatenate([w_out[:256], w_out[256:].reshape(HEADS, HD, D)[order].reshape(768, D)], 0)
    units = [unit_in(w_big), unit_in(w_out)]
    for l in range(2):
        if l == 1:
            units += [unit_in(x[n][0]) for n in ("rwkv_wr", "rwkv_wk", "rwkv_wv", "rwkv_wo")]
        units += [unit_in(x["mlp_w1"][l]), unit_down(x["mlp_w2"][l]), unit_in(x["ple_gate"][l]),
                  unit_ple(x["ple_proj"][l])]

    kg = x["k_gain"][0]
    two = lambda v: np.concatenate([v, v])[:, None]
    vec = np.concatenate(
        [cols(x["norm_mix"]), cols(x["norm_mlp"]), cols(x["norm_ple"]), cols(x["rwkv_mu"])]
        + [cols(x["rwkv_" + n]) for n in ("w0", "a0", "kk", "ka", "rk", "lnw", "lnb")]
        + [cols(x["pool_scale"]), two(x["q_gain"][0]), two(kg[0]), two(kg[1]), two(kg[2])], 1)

    def block_diag(m):
        a_, b_ = m
        z = np.zeros(a_.shape[:-2] + (128, 128), np.float32)
        z[..., :64, :64], z[..., 64:, 64:] = a_, b_
        return z

    cw = x["cmp_w"][0]
    pw = x["pool_w"][0]
    ck, cv = x["cache_k"][0], x["cache_v"][0]
    fmc = lambda c: c.reshape(-1, PAGE, 2, 2, HD).transpose(0, 3, 4, 2, 1).reshape(-1, 128, 2, PAGE)
    ws = x["state_win_v"][0].reshape(NS, WIN // 128, 128, 256).transpose(0, 2, 1, 3)
    wk = x["state_win_k"][0].reshape(NS, WIN, 2, 2, HD).transpose(0, 3, 4, 2, 1).reshape(NS, 128, 2, WIN)
    small = lambda w: w.reshape(KC, 128, -1).transpose(1, 0, 2)
    d = {
        "x": fm(np.concatenate([x["x_prompt"][0], x["x_sample"][:, 0]], 0)),
        "p": np.stack([fm(np.concatenate([x["p_prompt"][l, 0], x["p_sample"][l, :, 0]], 0)) for l in range(2)]),
        "weights": np.concatenate(units, 0),
        "vec": vec,
        "wgl": small(w_in[:, 2560:]),
        "state_pool": x["state_pool"][0].reshape(NS, 15, 2, 128).transpose(3, 2, 0, 1),
        "pool_w": block_diag((pw[0::2], pw[1::2])).transpose(1, 0, 2),
        "cmp_w": block_diag((cw, cw)).transpose(2, 0, 1, 3),
        "cmp_pe": np.concatenate([x["cmp_pe"][0].transpose(2, 0, 1)] * 2, 0),
        "page_table": x["page_table"].reshape(1, -1),
        "ck_cmp": fmc(ck[:, :, 0]), "ck_slc": fmc(ck[:, :, 1]), "cv_cmp": fmc(cv[:, :, 0]),
        "cv_slc": cv[:, :, 1].reshape(-1, PAGE, 256),
        "win_k": wk, "win_v": ws,
        "state_shift": fm(x["state_shift"][0]),
        "rwkv_w1": small(x["rwkv_w1"][0]), "rwkv_a1": small(x["rwkv_a1"][0]), "rwkv_g1": small(x["rwkv_g1"][0]),
        "rwkv_w2": x["rwkv_w2"][0], "rwkv_a2": x["rwkv_a2"][0], "rwkv_g2": x["rwkv_g2"][0],
        "state_wkv": x["state_wkv"][0].reshape(NS, KC, 2, HD, HD).transpose(2, 3, 0, 1, 4).reshape(128, NS, KC, HD),
    }
    d.update(constants())
    outs = {
        "y": (128, KC, T), "kv": (128, 12, T), "pool_p": (128, 2, 15), "pool_s": (128, 2, NS, 15),
        "win_k": (NS, 128, 2, WIN), "win_v": (NS, 128, WIN // 128, 256), "shift": (128, KC, NS + 1),
        "wkv_p": (128, KC, HD), "wkv_s": (128, NS, KC, HD),
    }
    nc = bacc.Bacc("TRN2", target_bir_lowering=False, num_devices=1)
    d = {"in_" + k: np.ascontiguousarray(v) for k, v in d.items()}
    ins = {k[3:]: nc.dram_tensor(k, v.shape, mybir.dt.from_np(v.dtype), kind="ExternalInput").ap() for k, v in d.items()}
    res = {k: nc.dram_tensor("out_" + k, s, F32, kind="ExternalOutput").ap() for k, s in outs.items()}
    build(nc, ins, res)
    r = run(nc, [d], core_ids=[0]).results[0]
    r = {k: np.asarray(r["out_" + k]) for k in outs}

    rows = lambda v: v.transpose(2, 1, 0).reshape(v.shape[2], -1)
    y = rows(r["y"])
    kv = r["kv"].reshape(2, HD, 6, 2, T).transpose(4, 2, 3, 0, 1).reshape(T, 6, GROUPS, HD)
    pair = lambda b, c, s: np.stack([kv[s, b], kv[s, c]], 1)
    pr, sa = slice(0, SEQ), slice(SEQ, T)
    wko = r["win_k"].reshape(NS, 2, HD, 2, WIN).transpose(0, 4, 3, 1, 2).reshape(NS, WIN, GROUPS, HD)
    wvo = r["win_v"].transpose(0, 2, 1, 3).reshape(NS, WIN, GROUPS, HD)
    shift = rows(r["shift"])
    return (
        y[None, :SEQ], y[SEQ:, None],
        pair(0, 2, pr)[None, None], pair(1, 3, pr)[None, None],
        pair(0, 2, sa)[None, :, None], pair(1, 3, sa)[None, :, None],
        kv[None, None, :SEQ, 4], kv[None, None, :SEQ, 5],
        np.concatenate([wko[:, 1:], kv[SEQ:, None, 4]], 1)[None], np.concatenate([wvo[:, 1:], kv[SEQ:, None, 5]], 1)[None],
        rows(r["pool_p"])[None, None], r["pool_s"].transpose(2, 3, 1, 0).reshape(1, NS, 15, 256),
        shift[None, :1], shift[None, 1:],
        r["wkv_p"].reshape(2, HD, KC, HD).transpose(2, 0, 1, 3).reshape(1, 1, RH, HD, HD),
        r["wkv_s"].reshape(2, HD, NS, KC, HD).transpose(2, 3, 0, 1, 4).reshape(1, NS, RH, HD, HD),
    )
```

```python
import math
from contextlib import ExitStack

import numpy as np
import concourse.bass as bass
from concourse import mybir

F32 = mybir.dt.float32
F32R = mybir.dt.float32r
I32 = mybir.dt.int32
ALU = mybir.AluOpType
ACT = mybir.ActivationFunctionType
AX = mybir.AxisListType

D, SEQ, NS, PAST, PAGE = 1024, 512, 8, 1024, 128
T = SEQ + NS
HT = T // 2
KC = D // 128
HD, HEADS, GROUPS, REP = 64, 12, 4, 3
NQ = SEQ // 128
PAGES = PAST // PAGE
WIN = 512
CL, CS = 32, 16
NC_P = SEQ // CS - 1
NC_S = PAST // CS - 1
UW = 2048
RING = 4
FF = 4 * D
RH = 16
CH = 64
NCH = SEQ // CH
EPS = 1e-6
NEG = -1e30

V_MIX, V_MLP, V_PLE, V_MU = 0, 16, 32, 48
V_W0, V_A0, V_KK, V_KA, V_RK, V_LNW, V_LNB = (96 + 8 * i for i in range(7))
V_PS, V_QG, V_KG = 152, 154, 155
NV = 158

C_SLC, C_NSLC, C_WIN, C_NWIN, C_CMP = 0, 1024, 1032, 1544, 1552
NCOL = C_CMP + NC_S

U_IN, U_OUT, U_T0 = 0, 10, 14
TAIL = 16 + 16 + 4 + 1
U_R = U_T0 + TAIL
U_WO = U_R + 12
U_T1 = U_WO + 4
NU = U_T1 + TAIL


def slopes():
    s = [2.0 ** (-8.0 * (i + 1) / 8) for i in range(8)]
    s += [2.0 ** (-8.0 * (i + 1) / 16) for i in range(0, 16, 2)][:4]
    return np.asarray(s, np.float32)


SLOPE = slopes()


def constants():
    c = {}
    c["ident"] = np.eye(128, dtype=np.float32)
    c["ones"] = np.ones((128, 128), np.float32)
    c["headones"] = np.kron(np.eye(2), np.ones((64, 64))).astype(np.float32)
    p = np.arange(128)[:, None]
    x = np.arange(512)[None, :] - 384 - p
    c["dist"] = np.where(x > 0, NEG, x).astype(np.float32)
    t = (np.arange(NQ)[None, :] * 128 + p)[:, :, None, None]
    j = np.arange(32)[None, None, None, :]
    heads = np.array([(2 * gp + g2) * REP + r for g2 in range(2) for gp in range(2) for r in range(REP)])
    dd = t - (CS * j + CL - 1)
    ok = (dd >= 0) & (j < NC_P)
    c["cmpbias"] = np.where(ok, -SLOPE[heads][None, None, :, None] * dd, NEG).astype(np.float32)
    c["cmpok"] = np.broadcast_to(ok, (128, NQ, 1, 32)).astype(np.float32).copy()
    ic = np.zeros((128, 2, SEQ), np.float32)
    for gi, w in enumerate((2, 4, 8, 16)):
        ic[(gi % 2) * 64:(gi % 2) * 64 + 64, gi // 2] = 1.0 / np.minimum(w, np.arange(SEQ) + 1)
    c["invcnt"] = ic
    row = np.arange(128)
    g, s, r = row // 32, (row % 32) // 3, row % 32 % 3
    live = s < NS
    sl = np.where(live, SLOPE[g * REP + r], 0.0)[:, None]
    same = (np.arange(NS)[None, :] == s[:, None])
    b = np.zeros((128, NCOL), np.float32)
    b[:, C_SLC:C_NSLC] = -sl * (PAST - np.arange(PAST))[None, :]
    dw = WIN - np.arange(WIN)
    b[:, C_WIN:C_NWIN] = np.where((dw < WIN)[None, :], -sl * dw[None, :], NEG)
    b[:, C_NSLC:C_WIN] = np.where(same | ~live[:, None], 0, NEG)
    b[:, C_NWIN:C_CMP] = np.where(same | ~live[:, None], 0, NEG)
    b[:, C_CMP:] = -sl * (PAST - (CS * np.arange(NC_S) + CL - 1))[None, :]
    c["sbias"] = b
    c["samegs"] = ((g[:, None] == g[None, :]) & (s[:, None] == s[None, :])).astype(np.float32)
    c["own_sample"] = (s[None, :] == np.arange(NS)[:, None]).astype(np.float32)
    c["own_head"] = ((g * REP + r)[:, None] == np.arange(HEADS)[None, :]).astype(np.float32) * live[:, None]
    c["blockno"] = np.broadcast_to(np.arange(1, 15, dtype=np.float32), (128, 14)).copy()
    ss, tt = np.arange(CH)[:, None], np.arange(CH)[None, :]
    m = np.concatenate([ss < tt, ss <= tt], 1).astype(np.float32)
    c["tri"] = np.concatenate([m, m], 0)
    lv = []
    for n in range(6):
        w = 1 << n
        lv.append((tt // w % 2 == 1) & (ss // w == tt // w - 1))
    lv = np.stack(lv, 1).astype(np.float32)
    c["level"] = np.concatenate([lv, lv], 0)
    e = np.eye(64, dtype=np.float32)
    c["ident2"] = np.concatenate([e, e], 0)
    rs = np.ones((128, KC, CH + 1), np.float32)
    rs[:, :, 0] = 0
    c["restart"] = rs
    return c


def build(nc, a, o):
    with ExitStack() as top:
        sb = lambda ctx, name, shape, dt=F32: ctx.enter_context(nc.sbuf_tensor(name, shape, dt))
        sem = lambda name: top.enter_context(nc.semaphore(name))
        P = top.enter_context(nc.psum_tensor("P", [128, 8, 512], F32))
        h = sb(top, "h", [128, KC, T])
        vec = sb(top, "vec", [128, NV])
        ring = sb(top, "ring", [128, RING, UW])
        ident = sb(top, "ident", [128, 128])
        ones = sb(top, "ones", [128, 128])
        headones = sb(top, "headones", [128, 128])
        rstd = sb(top, "rstd", [128, T])

        fixed_in = sem("fixed_in")
        stage_in = sem("stage_in")
        weight_in = [sem(f"weight_in{i}") for i in range(RING)]
        stores = sem("stores")
        whead_ready = sem("whead_ready")
        wsplit_ready = sem("wsplit_ready")
        xhead_ready = sem("xhead_ready")
        xsplit_ready = sem("xsplit_ready")
        tile_done = sem("tile_done")
        tile_free = sem("tile_free")
        half_used = sem("half_used")
        sq_ready = sem("sq_ready")
        ssum_ready = sem("ssum_ready")
        rvar_ready = sem("rvar_ready")
        rstd_ready = sem("rstd_ready")
        xn_ready = sem("xn_ready")
        dve_step = sem("dve_step")
        act_step = sem("act_step")
        state = {"split": 0, "unit": 0, "tile": 0, "norm": 0, "stage": 0, "stores": 0, "half": 0}
        used_up = {}

        class Chain:
            def __init__(self, eng, s, key):
                self.eng, self.sem, self.key = eng, s, key
                state.setdefault(key, 0)

            def __call__(self, ins):
                state[self.key] += 1
                ins.then_inc(self.sem, 1)
                self.eng.wait_ge(self.sem, state[self.key])

        halves = lambda ap: ap.rearrange("p (a b) -> p a b", a=2)

        def stream_weights(sp, upto):
            upto = min(upto, NU)
            for u in range(state["unit"], upto):
                if u >= RING:
                    sp.wait_ge(wsplit_ready, u - RING + 1)
                sp.dma_start(ring[:, u % RING, :], a["weights"][u]).then_inc(weight_in[u % RING], 16)
            state["unit"] = max(upto, state["unit"])

        def plan(units, per_group=1, times=1):
            first = state["tile"]
            n = first
            for g in range(0, len(units), per_group):
                n += 2 * times
                for u in units[g:g + per_group - 1]:
                    state["half"] += 1
                    used_up[u] = half_used, state["half"]
                used_up[units[g + per_group - 1]] = tile_done, n
            state["tile"] = n
            return first

        def dense(pe, first, units, ws, x, nk=KC, cols=256, per_group=1, times=1, chunk_ready=None):
            xh, xl = x
            n = first
            for g in range(0, len(units), per_group):
                for rep in range(times):
                    if n >= 4:
                        pe.wait_ge(tile_free, n - 2)
                    for i, u in enumerate(units[g:g + per_group]):
                        pe.wait_ge(wsplit_ready, u + 1)
                        for m in range(2):
                            for k in range(nk):
                                if chunk_ready and m == 0 and rep == 0:
                                    chunk_ready(i * nk + k)
                                c = slice(k * cols + (2 * rep + m) * 128, k * cols + (2 * rep + m + 1) * 128)
                                wh, wl = ws[:, u % 2, 0, c], ws[:, u % 2, 1, c]
                                first_k, last_k = i == 0 and k == 0, i == per_group - 1 and k == nk - 1
                                for w, xs in ((wh, xh), (wh, xl), (wl, xh)):
                                    for hf in range(2):
                                        mm = pe.matmul(P[:, n // 2 % 2 * 4 + 2 * m + hf, 0:HT], w,
                                                       xs[:, i * nk + k, hf * HT:(hf + 1) * HT],
                                                       start=first_k and w is wh and xs is xh,
                                                       stop=last_k and w is wl)
                            if i == per_group - 1:
                                mm.then_inc(tile_done, 1)
                        if i < per_group - 1:
                            mm.then_inc(half_used, 1)
                    n += 2

        def weight_head(act, u, units, ws):
            if u >= units[-1] + 1:
                return
            act.wait_ge(weight_in[u % RING], 16 * (u // RING + 1))
            if u >= units[0] + 2:
                act.wait_ge(*used_up[u - 2])
            act.activation(ws[:, u % 2, 0, :], ring[:, u % RING, :], ACT.Copy).then_inc(whead_ready, 1)

        def weight_rests(pool, units, ws):
            for u in units:
                pool.wait_ge(whead_ready, u + 1)
                pool.tensor_tensor(ws[:, u % 2, 1, :], ring[:, u % RING, :], ws[:, u % 2, 0, :].bitcast(F32),
                                   ALU.subtract).then_inc(wsplit_ready, 1)

        def take_splits(n):
            state["split"] += n
            return state["split"] - n

        def split_head(act, src, dst):
            act.activation(dst, src, ACT.Copy).then_inc(xhead_ready, 1)

        def split_rest(dve, n, src, xh, dst):
            dve.wait_ge(xhead_ready, n + 1)
            dve.tensor_tensor(dst, src, xh.bitcast(F32), ALU.subtract).then_inc(xsplit_ready, 1)

        def tile(n):
            b = n // 2 % 2 * 4 + n % 2 * 2
            return P[:, b:b + 2, 0:HT]

        def norm_act(act, i, dst, halves_of=None, units=None, ws=None):
            for k in range(KC):
                act.activation(dst[:, k, :], h[:, k, :], ACT.Square).then_inc(sq_ready, 1)
            if units:
                for u in units[0:2]:
                    weight_head(act, u, units, ws)
            act.wait_ge(rvar_ready, i + 1)
            act.activation(rstd[:, :], rstd[:, :], ACT.Sqrt).then_inc(rstd_ready, 1)
            if halves_of:
                for k in range(KC):
                    act.wait_ge(xn_ready, i * KC + k + 1)
                    split_head(act, dst[:, k, :], halves_of[0][:, k, :])

        def norm_pe(pe, i, dst):
            for k in range(KC):
                pe.wait_ge(sq_ready, i * KC + k + 1)
                for hf in range(2):
                    mm = pe.matmul(P[:, 6 + hf, 0:HT], ones[:, :], dst[:, k, hf * HT:(hf + 1) * HT],
                                   start=k == 0, stop=k == KC - 1)
            mm.then_inc(ssum_ready, 1)

        def norm_dve(dve, step, i, dst, col, halves_of=None, n=0):
            dve.wait_ge(ssum_ready, i + 1)
            step(dve.tensor_scalar(halves(rstd[:, :]), P[:, 6:8, 0:HT], 1.0 / D, EPS, ALU.mult, ALU.add))
            dve.reciprocal(rstd[:, :], rstd[:, :]).then_inc(rvar_ready, 1)
            dve.wait_ge(rstd_ready, i + 1)
            for k in range(KC):
                dve.scalar_tensor_tensor(out=dst[:, k, :], in0=h[:, k, :], scalar=vec[:, col + k:col + k + 1],
                                         in1=rstd[:, :], op0=ALU.mult, op1=ALU.mult).then_inc(xn_ready, 1)
                if halves_of and k >= 2:
                    split_rest(dve, n + k - 2, dst[:, k - 2, :], halves_of[0][:, k - 2, :], halves_of[1][:, k - 2, :])
            for k in range(KC - 2, KC):
                if halves_of:
                    split_rest(dve, n + k, dst[:, k, :], halves_of[0][:, k, :], halves_of[1][:, k, :])

        def tail(layer, u0):
            HC = FF // 128 // 2
            with ExitStack() as ctx:
                ws = sb(ctx, f"ws_t{layer}", [128, 2, 2, UW], F32R)
                u = [sb(ctx, f"u{n}{layer}", [128, KC, T], F32R) for n in "hl"]
                hid = [sb(ctx, f"hid{n}{layer}", [128, HC, T], F32R) for n in "hl"]
                full = sb(ctx, f"full{layer}", [128, KC, T])
                act_ = sb(ctx, f"act{layer}", [128, 2, T])
                sqr = sb(ctx, f"sqr{layer}", [128, 2, T])
                pl, pls = full[:, 0:2, :], [x[:, 0:2, :] for x in hid]
                sq_done = sem(f"hid_squared{layer}")
                block = ctx.enter_context(nc.Block(no_gpsimd_drain=True))
                halves_ = []
                for b in range(2):
                    up = list(range(u0 + 16 * b, u0 + 16 * b + 8))
                    down = list(range(u0 + 16 * b + 8, u0 + 16 * b + 16))
                    halves_.append((up, plan(up), down, plan(down, per_group=2)))
                gate, proj = list(range(u0 + 32, u0 + 36)), [u0 + 36]
                t_gate = plan(gate)
                t_proj = plan(proj, times=4)
                n1 = state["norm"]
                n2 = n1 + 1
                state["norm"] += 2
                state["stage"] += 16
                landed = state["stage"]
                x_1 = take_splits(KC)
                x_hid = [take_splits(HC) for _ in range(2)]
                x_pl = take_splits(2)
                x_2 = take_splits(KC)
                ready = lambda pe, n: (lambda k: pe.wait_ge(xsplit_ready, n + k + 1))

                @block.sync
                def _(sp):
                    stream_weights(sp, u0 + 16)
                    sp.wait_ge(xsplit_ready, x_1 + KC)
                    sp.dma_start(pl, a["p"][layer]).then_inc(stage_in, 16)
                    stream_weights(sp, u0 + TAIL + RING)

                @block.gpsimd
                def _(pool):
                    weight_rests(pool, range(u0, u0 + TAIL), ws)

                @block.tensor
                def _(pe):
                    norm_pe(pe, n1, full)
                    for b, (up, t_up, down, t_down) in enumerate(halves_):
                        dense(pe, t_up, up, ws, u, chunk_ready=ready(pe, x_1))
                        dense(pe, t_down, down, ws, hid, per_group=2, chunk_ready=ready(pe, x_hid[b]))
                    pe.wait_ge(tile_free, t_gate)
                    norm_pe(pe, n2, full)
                    dense(pe, t_gate, gate, ws, u, chunk_ready=ready(pe, x_2))
                    dense(pe, t_proj, proj, ws, pls, nk=2, cols=D, times=4, chunk_ready=ready(pe, x_pl))

                @block.scalar
                def _(act):
                    units = range(u0, u0 + TAIL)
                    norm_act(act, n1, full, u, units, ws)
                    for b, (up, t_up, down, t_down) in enumerate(halves_):
                        for m in range(HC + 1):
                            if m < HC:
                                if m >= 2 or b:
                                    act.wait_ge(sq_done, HC * b + m - 1)
                                act.wait_ge(tile_done, t_up + m + 1)
                                act.activation(halves(act_[:, m % 2, :]), tile(t_up + m), ACT.Relu)\
                                   .then_inc(tile_free, 1)
                            if m:
                                act.wait_ge(sq_done, HC * b + m)
                                split_head(act, sqr[:, (m - 1) % 2, :], hid[0][:, m - 1, :])
                            if m % 2 and m < HC:
                                weight_head(act, up[m // 2] + 2, units, ws)
                        for d in down:
                            weight_head(act, d + 2, units, ws)
                        if b == 0:
                            act.wait_ge(tile_free, t_down + KC)
                    act.wait_ge(stage_in, landed)
                    act.wait_ge(tile_free, t_gate)
                    for k in range(2):
                        split_head(act, pl[:, k, :], pls[0][:, k, :])
                    act.wait_ge(xsplit_ready, x_pl + 2)
                    norm_act(act, n2, full, u)
                    act.wait_ge(xsplit_ready, x_2 + KC)
                    for m in range(KC):
                        act.wait_ge(tile_done, t_gate + m + 1)
                        act.activation(halves(full[:, m, :]), tile(t_gate + m), ACT.Sigmoid).then_inc(tile_free, 1)
                        if m % 2:
                            weight_head(act, gate[m // 2] + 2, units, ws)

                @block.vector
                def _(dve):
                    step = Chain(dve, dve_step, "dve")
                    norm_dve(dve, step, n1, full, V_MLP + KC * layer, u, x_1)
                    for b, (up, t_up, down, t_down) in enumerate(halves_):
                        for m in range(HC + 2):
                            if m < HC:
                                dve.wait_ge(tile_free, t_up + m + 1)
                                if m >= 2:
                                    dve.wait_ge(xsplit_ready, x_hid[b] + m - 1)
                                dve.tensor_tensor(sqr[:, m % 2, :], act_[:, m % 2, :], act_[:, m % 2, :], ALU.mult)\
                                   .then_inc(sq_done, 1)
                            if m >= 1 and m <= HC:
                                split_rest(dve, x_hid[b] + m - 1, sqr[:, (m - 1) % 2, :], hid[0][:, m - 1, :],
                                           hid[1][:, m - 1, :])
                        for m in range(KC):
                            dve.wait_ge(tile_done, t_down + m + 1)
                            hv = halves(h[:, m, :])
                            dve.tensor_tensor(hv, hv, tile(t_down + m), ALU.add).then_inc(tile_free, 1)
                    for k in range(2):
                        split_rest(dve, x_pl + k, pl[:, k, :], pls[0][:, k, :], pls[1][:, k, :])
                    norm_dve(dve, step, n2, full, V_PLE + KC * layer, u, x_2)
                    dve.wait_ge(tile_free, t_proj)
                    for m in range(KC):
                        dve.wait_ge(tile_done, t_proj + m + 1)
                        gv = halves(full[:, m, :])
                        dve.tensor_tensor(gv, gv, tile(t_proj + m), ALU.mult).then_inc(tile_free, 1)
                        dve.wait_ge(tile_free, t_proj + m + 1)
                        step(dve.tensor_tensor(h[:, m, :], h[:, m, :], full[:, m, :], ALU.add))

        def layer0():
            with ExitStack() as c0:
                xn = sb(c0, "xn0", [128, KC, T])
                Z = sb(c0, "Z", [128, 20, T])
                gates = sb(c0, "gates", [128, NQ + 1, 3 * HEADS])
                Vt = sb(c0, "Vt", [128, 2, NQ, 256])
                Vn = sb(c0, "Vn", [NS, 2, 256])
                VCp = sb(c0, "VCp", [128, 256])
                KCb = sb(c0, "KCb", [128, NS + 1, 2, NC_S])
                KB = lambda b, gp: 8 + 2 * b + gp
                project_in(xn, Z, gates)
                pool_and_values(xn, Z, Vt, Vn)
                with ExitStack() as c1:
                    VCt = sb(c1, "VCt", [64, NS, 256])
                    pages = sb(c1, "pages", [1, NS * PAGES], I32)
                    compress_and_score(xn, Z, KCb, VCt, VCp, KB, pages)
                    sample_attention(xn, gates, Vn, VCt, pages)
                prompt_attention(xn, Z, gates, Vt, VCp, KCb, KB)
                add_product(xn, list(range(U_OUT, U_OUT + 4)), "w_out")

        def add_product(x, units, name):
            with ExitStack() as ctx:
                ws = sb(ctx, "ws_" + name, [128, 2, 2, UW], F32R)
                xs = [sb(ctx, f"x{n}_{name}", [128, KC, T], F32R) for n in "hl"]
                first = plan(units)
                x0 = take_splits(KC)
                with nc.Block(no_gpsimd_drain=True) as block:
                    @block.sync
                    def _(sp):
                        stream_weights(sp, units[-1] + 1 + RING)

                    @block.gpsimd
                    def _(pool):
                        weight_rests(pool, units, ws)

                    @block.tensor
                    def _(pe):
                        dense(pe, first, units, ws, xs, chunk_ready=lambda k: pe.wait_ge(xsplit_ready, x0 + k + 1))

                    @block.scalar
                    def _(act):
                        weight_head(act, units[0], units, ws)
                        for k in range(KC):
                            split_head(act, x[:, k, :], xs[0][:, k, :])
                        for u in units[1:]:
                            weight_head(act, u, units, ws)

                    @block.vector
                    def _(dve):
                        for k in range(KC):
                            split_rest(dve, x0 + k, x[:, k, :], xs[0][:, k, :], xs[1][:, k, :])
                        for m in range(KC):
                            dve.wait_ge(tile_done, first + m + 1)
                            hv = halves(h[:, m, :])
                            dve.tensor_tensor(hv, hv, tile(first + m), ALU.add).then_inc(tile_free, 1)

        def project_in(xn, Z, gates):
            with ExitStack() as ctx:
                wgl = sb(ctx, "wgl", [128, KC, 3 * HEADS])
                ws = sb(ctx, "ws_in", [128, 2, 2, UW], F32R)
                xs = [sb(ctx, f"x{n}_in", [128, KC, T], F32R) for n in "hl"]
                zsq = sb(ctx, "zsq", [128, 2, T])
                zr = sb(ctx, "zr", [128, 2, T])
                logits_ready = sem("logits_ready")
                zsq_ready = sem("zsq_ready")
                zss_ready = sem("zss_ready")
                zvar_ready = sem("zvar_ready")
                zroot_ready = sem("zroot_ready")
                normed = list(range(2, 8)) + [12, 13, 16, 17]
                units = list(range(U_IN, U_IN + 10))
                first = plan(units)
                i = state["norm"]
                state["norm"] += 1
                state["stage"] += 16
                landed = state["stage"]
                last = first + 20
                x0 = take_splits(KC)

                with nc.Block(no_gpsimd_drain=True) as block:
                    @block.gpsimd
                    def _(pool):
                        weight_rests(pool, units, ws)

                    @block.sync
                    def _(sp):
                        sp.dma_start(wgl[:, :, :], a["wgl"]).then_inc(stage_in, 16)
                        stream_weights(sp, U_OUT)

                    @block.tensor
                    def _(pe):
                        norm_pe(pe, i, xn)
                        dense(pe, first, units, ws, xs, chunk_ready=lambda k: pe.wait_ge(xsplit_ready, x0 + k + 1))
                        pe.wait_ge(stage_in, landed)
                        pe.wait_ge(tile_free, last)
                        for t in range(NQ + 1):
                            n = 128 if t < NQ else NS
                            for k in range(KC):
                                mm = pe.matmul(P[0:n, 0, t * 36:t * 36 + 36], xn[:, k, t * 128:t * 128 + n],
                                               wgl[:, k, :], start=k == 0, stop=k == KC - 1)
                        mm.then_inc(logits_ready, 1)
                        for j in range(len(normed)):
                            pe.wait_ge(zsq_ready, j + 1)
                            if j >= 2:
                                pe.wait_ge(zvar_ready, j - 1)
                            for hf in range(2):
                                mm = pe.matmul(P[:, 4 + 2 * (j % 2) + hf, 0:HT], headones[:, :],
                                               zsq[:, j % 2, hf * HT:(hf + 1) * HT], start=True, stop=True)
                            mm.then_inc(zss_ready, 1)

                    @block.scalar
                    def _(act):
                        step = Chain(act, act_step, "act")
                        norm_act(act, i, xn, xs, units, ws)
                        for m in range(20):
                            act.wait_ge(tile_done, first + m + 1)
                            act.activation(halves(Z[:, m, :]), tile(first + m), ACT.Copy).then_inc(tile_free, 1)
                            if m % 2:
                                weight_head(act, units[m // 2] + 2, units, ws)
                        act.wait_ge(logits_ready, 1)
                        act.activation(gates[:, 0:NQ, :], P[:, 0, 0:NQ * 36].rearrange("p (t c) -> p t c", t=NQ),
                                       ACT.Sigmoid)
                        step(act.activation(gates[0:NS, NQ, :], P[0:NS, 0, NQ * 36:NQ * 36 + 36], ACT.Sigmoid))
                        act.wait_ge(tile_free, last)
                        for j in range(len(normed) + 2):
                            if j >= 2:
                                act.wait_ge(zvar_ready, j - 1)
                                act.activation(zr[:, j % 2, :], zr[:, j % 2, :], ACT.Sqrt,
                                               scale=1.0 / 64 if j - 2 < 6 else 1.0).then_inc(zroot_ready, 1)
                            if j < len(normed):
                                act.activation(zsq[:, j % 2, :], Z[:, normed[j], :], ACT.Square)\
                                   .then_inc(zsq_ready, 1)

                    @block.vector
                    def _(dve):
                        step = Chain(dve, dve_step, "dve")
                        norm_dve(dve, step, i, xn, V_MIX, xs, x0)
                        for j, c in enumerate(normed):
                            dve.wait_ge(zss_ready, j + 1)
                            step(dve.tensor_scalar(halves(zr[:, j % 2, :]),
                                                   P[:, 4 + 2 * (j % 2):6 + 2 * (j % 2), 0:HT],
                                                   1.0 / HD, EPS, ALU.mult, ALU.add))
                            dve.reciprocal(zr[:, j % 2, :], zr[:, j % 2, :]).then_inc(zvar_ready, 1)
                            dve.wait_ge(zroot_ready, j + 1)
                            col = V_QG if j < 6 else V_KG + 1 + (j - 6) // 2
                            step(dve.scalar_tensor_tensor(out=Z[:, c, :], in0=Z[:, c, :], scalar=vec[:, col:col + 1],
                                                          in1=zr[:, j % 2, :], op0=ALU.mult, op1=ALU.mult))

        def pool_and_values(mix, Z, Vt, Vn):
            with ExitStack() as ctx:
                ext = sb(ctx, "ext", [128, 2, 15 + SEQ])
                wa = sb(ctx, "wa", [128, 2, 15 + SEQ])
                wb = sb(ctx, "wb", [128, 2, 15 + SEQ])
                dev = sb(ctx, "dev", [128, 2, T])
                inv = sb(ctx, "inv", [128, 2, SEQ])
                past = sb(ctx, "past", [128, 2, NS, 15])
                newpast = sb(ctx, "newpast", [128, 2, NS, 15])
                psum_ = sb(ctx, "psum_", [128, 2, NS])
                pw = sb(ctx, "pw", [128, 2, 128])
                turned = sem("turned")
                vcopied = sem("vcopied")
                dev_ready = sem("dev_ready")
                pooled = sem("pooled")
                rows_ready = sem("rows_ready")
                state["stage"] += 48
                landed = state["stage"]
                state["stores"] += 48
                W = (2, 4, 8, 16)

                with nc.Block(no_gpsimd_drain=True) as block:
                    @block.sync
                    def _(sp):
                        sp.dma_start(inv[:, :, :], a["invcnt"]).then_inc(stage_in, 16)
                        sp.dma_start(past[:, :, :, :], a["state_pool"]).then_inc(stage_in, 16)
                        sp.dma_start(pw[:, :, :], a["pool_w"]).then_inc(stage_in, 16)
                        sp.dma_start(o["kv"], Z[:, 8:20, :]).then_inc(stores, 16)
                        sp.dma_start(o["pool_p"], Z[:, 0:2, SEQ - 15:SEQ]).then_inc(stores, 16)
                        sp.wait_ge(rows_ready, 1)
                        sp.dma_start(o["pool_s"], newpast[:, :, :, :]).then_inc(stores, 16)
                        sp.wait_ge(stores, state["stores"])

                    @block.tensor
                    def _(pe):
                        for b in range(2):
                            for gp in range(2):
                                for t in range(NQ):
                                    mm = pe.transpose(P[:, 2 * b + gp, t * 128:(t + 1) * 128],
                                                      Z[:, 14 + 4 * b + gp, t * 128:(t + 1) * 128], ident[:, :])
                                mm.then_inc(turned, 1)
                        for b in range(2):
                            for gp in range(2):
                                mm = pe.transpose(P[0:NS, 4, (2 * b + gp) * 128:(2 * b + gp + 1) * 128],
                                                  Z[:, 14 + 4 * b + gp, SEQ:T], ident[:, :])
                        mm.then_inc(turned, 1)
                        pe.wait_ge(dev_ready, 1)
                        pe.wait_ge(stage_in, landed)
                        pe.wait_ge(vcopied, 5)
                        for c in range(2):
                            for hf in range(2):
                                mm = pe.matmul(P[:, (5 + hf, hf)[c], 0:HT], pw[:, c, :],
                                               dev[:, c, hf * HT:(hf + 1) * HT], start=True, stop=True)
                            mm.then_inc(pooled, 1)

                    @block.scalar
                    def _(act):
                        for b in range(2):
                            for gp in range(2):
                                act.wait_ge(turned, 2 * b + gp + 1)
                                act.activation(Vt[:, b, :, gp * 128:(gp + 1) * 128],
                                               P[:, 2 * b + gp, :].rearrange("p (t d) -> p t d", t=NQ),
                                               ACT.Copy).then_inc(vcopied, 1)
                        act.wait_ge(turned, 5)
                        act.activation(Vn[:, :, :], P[0:NS, 4, :].rearrange("p (b d) -> p b d", b=2),
                                       ACT.Copy).then_inc(vcopied, 1)

                    @block.vector
                    def _(dve):
                        step = Chain(dve, dve_step, "dve")
                        n = 15 + SEQ
                        dve.memset(ext[:, :, 0:15], 0.0)
                        step(dve.tensor_copy(ext[:, :, 15:n], Z[:, 0:2, 0:SEQ]))
                        dve.wait_ge(stage_in, landed)
                        dve.tensor_copy(newpast[:, :, :, 0:14], past[:, :, :, 1:15])
                        dve.tensor_copy(newpast[:, :, :, 14], Z[:, 0:2, SEQ:T]).then_inc(rows_ready, 1)
                        src = ext
                        for gi, w in enumerate(W):
                            dst = (wa, wb)[gi % 2]
                            step(dve.tensor_tensor(dst[:, :, w - 1:n], src[:, :, w - 1:n],
                                                   src[:, :, w // 2 - 1:n - w // 2], ALU.add))
                            c, r = gi // 2, slice(gi % 2 * 64, gi % 2 * 64 + 64)
                            step(dve.tensor_tensor(dev[r, c, 0:SEQ], dst[r, c, 15:n], inv[r, c, :], ALU.mult))
                            step(dve.tensor_reduce(psum_[r, c, :], past[r, c, :, 16 - w:15], AX.X, ALU.add))
                            src = dst
                        step(dve.tensor_tensor(dev[:, :, 0:SEQ], dev[:, :, 0:SEQ], Z[:, 0:2, 0:SEQ], ALU.subtract))
                        step(dve.tensor_tensor(psum_[:, :, :], psum_[:, :, :], Z[:, 0:2, SEQ:T], ALU.add))
                        for gi, w in enumerate(W):
                            c, r = gi // 2, slice(gi % 2 * 64, gi % 2 * 64 + 64)
                            mm = dve.scalar_tensor_tensor(out=dev[r, c, SEQ:T], in0=psum_[r, c, :], scalar=1.0 / w,
                                                          in1=Z[r, c, SEQ:T], op0=ALU.mult, op1=ALU.subtract)
                            step(mm)
                        dve.sem_inc(dev_ready, 1)
                        for c in range(2):
                            dve.wait_ge(pooled, c + 1)
                            b = (5, 0)[c]
                            step(dve.tensor_scalar(halves(mix[:, c, :]), P[:, b:b + 2, 0:HT],
                                                   vec[:, V_PS + c:V_PS + c + 1], None, ALU.mult))

        def compress_and_score(mix, Z, KCb, VCt, VCp, KB, pages):
            with ExitStack() as ctx:
                cw = sb(ctx, "cw", [128, 2, CL, 128])
                pe_ = sb(ctx, "pe_", [128, 2, CL])
                peb = sb(ctx, "peb", [128, 2])
                raw = [sb(ctx, "raw", [128, 3, 2, PAST]),
                       ring[:, 1:RING, :].rearrange("p r (g c) -> p r g c", g=2)]
                QA = sb(ctx, "QA", [128, 2, 64])
                spare = mix[:, 2:KC, :].rearrange("p k t -> p (k t)")
                kwin = [[spare[:, 0:WIN], spare[:, WIN:2 * WIN]], [spare[:, 2 * WIN:3 * WIN], rstd[:, 0:WIN]]]
                VCb = spare[:, 3 * WIN:3 * WIN + (NS + 1) * 2 * NC_S].rearrange("p (s g c) -> p s g c", s=NS + 1, g=2)
                QZ = Z[:, 0:2, :].rearrange("p k t -> p (k t)")[:, 0:1024].rearrange("p (g s c) -> p g s c", g=2, s=NS)
                rows_in = [sem(f"rows_in{i}") for i in range(2)]
                pages_in = sem("pages_in")
                cmp_done = sem("cmp_done")
                cmp_free = sem("cmp_free")
                scored = sem("scored")
                q_ready = sem("q_ready")
                peb_done = sem("peb_done")
                ksq_ready = sem("ksq_ready")
                kss_ready = sem("kss_ready")
                kvar_ready = sem("kvar_ready")
                kroot_ready = sem("kroot_ready")
                kc_ready = sem("kc_ready")
                vturned = sem("vturned")
                vct_copied = sem("vct_copied")
                state["stage"] += 32
                landed = state["stage"]
                stored = state["stores"]
                state["stores"] += 32 * NS
                NK = (NS + 1) * 2 * NC_S
                kflat = KCb[:, :, :, :].rearrange("p s g c -> p (s g c)")
                sq = raw[0][:, 0, :, :].rearrange("p g c -> p (g c)")[:, 0:NK]
                kr = raw[0][:, 1, :, :].rearrange("p g c -> p (g c)")[:, 0:NK]
                N3 = NK // 3

                with nc.Block(no_gpsimd_drain=True) as block:
                    @block.sync
                    def _(sp):
                        sp.dma_start(pages[:, :], a["page_table"]).then_inc(pages_in, 16)
                        sp.wait_ge(pages_in, 16)
                        for s in range(NS + 1):
                            if s < NS:
                                page = [sp.value_load(pages[0:1, s * PAGES + n:s * PAGES + n + 1], min_val=0,
                                                      max_val=a["rows"].shape[0] - 1) for n in range(PAGES)]
                                if s >= 2:
                                    sp.wait_ge(cmp_done, 2 * (s - 1))
                                    sp.wait_ge(stores, stored + 32 * (s - 1))
                                for n in range(PAGES):
                                    sp.dma_start(raw[s % 2][:, :, :, n * PAGE:(n + 1) * PAGE]
                                                 .rearrange("p k g c -> p (k g) c"), a["rows"][bass.ds(page[n], 1)]
                                                 .rearrange("o p k c -> p (o k) c")).then_inc(rows_in[s % 2], 16)
                                for g in range(2):
                                    sp.dma_start(kwin[s % 2][g], a["win_k"][s][:, g, :]).then_inc(rows_in[s % 2], 16)
                                if s == 0:
                                    sp.dma_start(pe_[:, :, :], a["cmp_pe"]).then_inc(stage_in, 16)
                                    sp.dma_start(cw[:, :, :, :], a["cmp_w"]).then_inc(stage_in, 16)
                            if s >= 1:
                                v = s - 1
                                sp.wait_ge(rows_in[v % 2], 16 * (PAGES + 2) * (v // 2 + 1))
                                for g in range(2):
                                    sp.dma_start(o["win_k"][v][:, g, :], kwin[v % 2][g]).then_inc(stores, 16)
                        sp.wait_ge(stores, state["stores"])

                    @block.tensor
                    def _(pe):
                        pe.wait_ge(q_ready, 1)
                        for s in range(NS + 1):
                            if s < NS:
                                pe.wait_ge(rows_in[s % 2], 16 * (PAGES + 2) * (s // 2 + 1))
                                for gp in range(2):
                                    kslc = raw[s % 2][:, 2, gp, :]
                                    for bank, keys in ((0, kslc[:, 0:512]), (1, kslc[:, 512:1024]),
                                                       (2, kwin[s % 2][gp])):
                                        mm = pe.matmul(P[64 * gp:64 * gp + 64, bank, :], QZ[:, gp, s, :], keys,
                                                       start=s == 0, stop=s == NS - 1)
                                mm.then_inc(scored, 1)
                                if s == 0:
                                    pe.wait_ge(stage_in, landed)
                                    for kv in range(2):
                                        for l in range(CL):
                                            mm = pe.matmul(P[:, 3, kv:kv + 1], cw[:, kv, l, :], pe_[:, kv, l:l + 1],
                                                           start=l == 0, stop=l == CL - 1)
                                    mm.then_inc(peb_done, 1)
                            for kv in range(2):
                                if s >= 2:
                                    pe.wait_ge(cmp_free, 2 * (s - 2) + kv + 1)
                                nc_, width = (NC_S, 2 * NC_S) if s < NS else (NC_P, 2 * NC_P)
                                for l in range(CL):
                                    rows = slice(l, l + CS * (nc_ - 1) + 1, CS)
                                    src = raw[s % 2][:, kv, :, rows] if s < NS else Z[:, KB(kv, 0):KB(kv, 0) + 2, rows]
                                    mm = pe.matmul(P[:, 4 + 2 * kv + s % 2, 0:width]
                                                   .rearrange("p (g c) -> p g c", g=2), cw[:, kv, l, :], src,
                                                   start=l == 0, stop=l == CL - 1)
                                mm.then_inc(cmp_done, 1)
                        pe.wait_ge(ksq_ready, 1)
                        pe.wait_ge(cmp_free, 2 * NS + 2)
                        for n in range(3):
                            mm = pe.matmul(P[:, 4 + n, 0:N3], headones[:, :], sq[:, n * N3:(n + 1) * N3],
                                           start=True, stop=True)
                        mm.then_inc(kss_ready, 1)
                        pe.wait_ge(kc_ready, 1)
                        for gp in range(2):
                            rows = P[64 * gp:64 * gp + 64, 3, :]
                            for s in range(NS):
                                pe.matmul(rows[:, 0:NC_S], QZ[:, gp, s, :], KCb[:, s, gp, :],
                                          start=s == 0, stop=s == NS - 1)
                            pe.matmul(rows[:, 64:72], QA[:, gp, :], Z[:, KB(2, gp), SEQ:T], start=True, stop=True)
                            pe.matmul(rows[:, 72:80], QA[:, gp, :], Z[:, KB(4, gp), SEQ:T], start=True, stop=True)
                        for s in range(NS):
                            for gp in range(2):
                                c = (2 * s + gp) * 128
                                mm = pe.transpose(P[0:NC_S, 4 + c // 512, c % 512:c % 512 + 128],
                                                  VCb[:, s, gp, :], ident[:, :])
                        mm.then_inc(vturned, 1)
                        pe.wait_ge(vct_copied, 2)
                        for j in range(4):
                            for gp in range(2):
                                mm = pe.matmul(P[32 * j:32 * j + 32, 4, gp * 128:(gp + 1) * 128],
                                               VCb[:, NS, gp, 0:32], ident[:, :], start=True, stop=True)
                        mm.then_inc(vturned, 1)

                    @block.scalar
                    def _(act):
                        act.wait_ge(cmp_free, 2 * NS + 2)
                        act.activation(sq, kflat, ACT.Square).then_inc(ksq_ready, 1)
                        act.wait_ge(kvar_ready, 1)
                        act.activation(kr, kr, ACT.Sqrt).then_inc(kroot_ready, 1)
                        act.wait_ge(vturned, 1)
                        for half in range(2):
                            act.activation(VCt[0:NC_S, 4 * half:4 * half + 4, :],
                                           P[0:NC_S, 4 + 2 * half:6 + 2 * half, :]
                                           .rearrange("p b (s d) -> p (b s) d", s=2),
                                           ACT.Copy).then_inc(vct_copied, 1)
                        act.wait_ge(vturned, 2)
                        act.activation(VCp[:, :], P[:, 4, 0:256], ACT.Copy).then_inc(vct_copied, 1)

                    @block.vector
                    def _(dve):
                        step = Chain(dve, dve_step, "dve")
                        step(dve.memset(QZ[:, :, :, :], 0.0))
                        step(dve.memset(QA[:, :, :], 0.0))
                        step(dve.memset(KCb[:, NS, :, :], 0.0))
                        step(dve.memset(VCb[:, NS, :, :], 0.0))
                        for gp in range(2):
                            for g2 in range(2):
                                r = slice(64 * g2, 64 * g2 + 64)
                                step(dve.tensor_copy(
                                    QA[r, gp, 32 * g2:32 * g2 + 24].rearrange("p (s r) -> p s r", r=REP),
                                    Z[r, 2 + 3 * gp:5 + 3 * gp, SEQ:T].rearrange("p r s -> p s r")))
                        for s in range(NS):
                            step(dve.tensor_copy(
                                QZ[:, :, s, :].rearrange("p g (h c) -> p g h c", h=2)[:, :, :, 3 * s:3 * s + 3],
                                QA[:, :, :].rearrange("p g (h c) -> p g h c", h=2)[:, :, :, 3 * s:3 * s + 3]))
                        dve.sem_inc(q_ready, 1)
                        dve.wait_ge(peb_done, 1)
                        step(dve.tensor_copy(peb[:, :], P[:, 3, 0:2]))
                        for s in range(NS + 1):
                            for kv, dst in ((0, KCb), (1, VCb)):
                                n = NC_S if s < NS else NC_P
                                dve.wait_ge(cmp_done, 2 * s + kv + 1)
                                dve.tensor_scalar(dst[:, s, :, 0:n],
                                                  P[:, 4 + 2 * kv + s % 2, 0:2 * n].rearrange("p (g c) -> p g c", g=2),
                                                  peb[:, kv:kv + 1], None, ALU.add).then_inc(cmp_free, 1)
                        dve.wait_ge(kss_ready, 1)
                        step(dve.tensor_scalar(kr.rearrange("p (n c) -> p n c", n=3), P[:, 4:7, 0:N3],
                                               1.0 / HD, EPS, ALU.mult, ALU.add))
                        dve.reciprocal(kr, kr).then_inc(kvar_ready, 1)
                        dve.wait_ge(kroot_ready, 1)
                        dve.scalar_tensor_tensor(out=kflat, in0=kflat, scalar=vec[:, V_KG:V_KG + 1], in1=kr,
                                                 op0=ALU.mult, op1=ALU.mult).then_inc(kc_ready, 1)

        def sample_attention(mix, gates, Vn, VCt, pages):
            with ExitStack() as ctx:
                S = sb(ctx, "S", [128, NCOL])
                bias = sb(ctx, "bias", [128, NCOL])
                samegs = sb(ctx, "samegs", [128, 128])
                blockno = sb(ctx, "blockno", [128, 14])
                own_sample = sb(ctx, "own_sample", [NS, 128])
                own_head = sb(ctx, "own_head", [128, HEADS])
                gall = sb(ctx, "gall", [128, HEADS, 3])
                grow = sb(ctx, "grow", [128, 3])
                PT = sb(ctx, "PT", [128, 15, 128])
                VB = 4
                vs = sb(ctx, "vs", [128, VB, PAGES, 256])
                vw = sb(ctx, "vw", [128, VB, WIN // 128, 256])
                st = sb(ctx, "st", [128, 64])
                stored = [sem(f"stored{i}") for i in range(2)]
                v_in = [sem(f"v_in{i}") for i in range(VB)]
                grow_done = sem("grow_done")
                mx_ready = sem("mx_ready")
                exp_done = sem("exp_done")
                pc_ready = sem("pc_ready")
                imp_done = sem("imp_done")
                p_ready = sem("p_ready")
                pturned = sem("pturned")
                pt_ready = sem("pt_ready")
                pv_done = sem("pv_done")
                state["stage"] += 80
                landed = state["stage"]
                BR = ((C_CMP, NCOL), (C_SLC, C_WIN), (C_WIN, C_CMP))
                PIECES = [(128 * t, 128) for t in range(8)] + [(C_WIN + 128 * t, 128) for t in range(4)] \
                    + [(C_CMP, NC_S), (C_NSLC, NS), (C_NWIN, NS)]

                def load_values(eng, s):
                    page = [eng.value_load(pages[0:1, s * PAGES + n:s * PAGES + n + 1], min_val=0,
                                           max_val=a["cv_slc"].shape[0] - 1) for n in range(PAGES)]
                    if s >= VB:
                        eng.wait_ge(pv_done, s - VB + 1)
                        eng.wait_ge(stored[s % 2], 16 * ((s - VB) // 2 + 1))
                    for n in range(PAGES):
                        eng.dma_start(vs[:, s % VB, n, :], a["cv_slc"][bass.ds(page[n], 1)]
                                      .rearrange("o p c -> (o p) c")).then_inc(v_in[s % VB], 16)
                    eng.dma_start(vw[:, s % VB, :, :], a["win_v"][s]).then_inc(v_in[s % VB], 16)
                    eng.wait_ge(v_in[s % VB], 16 * (PAGES + 1) * (s // VB + 1))
                    eng.dma_start(o["win_v"][s], vw[:, s % VB, :, :]).then_inc(stored[s % 2], 16)

                with nc.Block(no_gpsimd_drain=True) as block:
                    @block.sync
                    def _(sp):
                        for dst, src in ((bias[:, :], "sbias"), (samegs[:, :], "samegs"), (blockno[:, :], "blockno"),
                                         (own_sample[:, :], "own_sample"), (own_head[:, :], "own_head")):
                            sp.dma_start(dst, a[src]).then_inc(stage_in, 16)
                        for s in range(0, NS, 2):
                            load_values(sp, s)
                        for p in range(2):
                            sp.wait_ge(stored[p], 16 * NS // 2)

                    @block.tensor
                    def _(pe):
                        pe.wait_ge(stage_in, landed)
                        pe.matmul(P[:, 5, 0:36], own_sample[:, :], gates[0:NS, NQ, :], start=True, stop=True)\
                          .then_inc(grow_done, 1)
                        pe.wait_ge(pc_ready, 1)
                        pe.matmul(P[:, 4, 0:NC_S], samegs[:, :], S[:, C_CMP:NCOL], start=True, stop=True)\
                          .then_inc(imp_done, 1)
                        pe.wait_ge(p_ready, 1)
                        for i, (c, n) in enumerate(PIECES):
                            mm = pe.transpose(P[0:n, 4 + i // 4, i % 4 * 128:i % 4 * 128 + 128], S[:, c:c + n],
                                              ident[:, :])
                        mm.then_inc(pturned, 1)
                        pe.wait_ge(pt_ready, 1)
                        for gp in range(2):
                            for b in range(2):
                                pe.matmul(P[:, gp, 0:64], Vn[:, b, gp * 128:(gp + 1) * 128],
                                          PT[0:NS, 13 + b, 64 * gp:64 * gp + 64], start=b == 0, stop=b == 1)
                        for s in range(NS):
                            pe.wait_ge(v_in[s % VB], 16 * (PAGES + 1) * (s // VB + 1))
                            for g in range(GROUPS):
                                d = slice(64 * g, 64 * g + 64)
                                rows = slice(32 * (g % 2) + 3 * s, 32 * (g % 2) + 3 * s + 3)
                                out = P[64 * (g % 2):64 * (g % 2) + 64, g // 2, rows]
                                for i in range(13):
                                    n = PIECES[i][1]
                                    v = vs[:, s % VB, i, d] if i < 8 else vw[:, s % VB, i - 8, d] if i < 12 \
                                        else VCt[0:n, s, d]
                                    mm = pe.matmul(out, v, PT[0:n, i, 32 * g + 3 * s:32 * g + 3 * s + 3], start=False,
                                                   stop=i == 12, skip_group_check=True)
                            mm.then_inc(pv_done, 1)

                    @block.scalar
                    def _(act):
                        load_values(act, 1)
                        for i, b in enumerate((0, 1, 2)):
                            act.wait_ge(mx_ready, i + 1)
                            x = S[:, BR[b][0]:BR[b][1]]
                            act.activation(x, x, ACT.Exp, bias=st[:, b:b + 1], accum_out=st[:, 4 + b:5 + b])\
                               .then_inc(exp_done, 1)
                        act.wait_ge(pturned, 1)
                        step = Chain(act, act_step, "act")
                        step(act.activation(PT[:, 0:12, :], P[:, 4:7, :].rearrange("p b (i c) -> p (b i) c", i=4),
                                            ACT.Copy))
                        step(act.activation(PT[0:NC_S, 12, :], P[0:NC_S, 7, 0:128], ACT.Copy))
                        act.activation(PT[0:NS, 13:15, :], P[0:NS, 7, 128:384].rearrange("p (b c) -> p b c", b=2),
                                       ACT.Copy).then_inc(pt_ready, 1)
                        for s in range(3, NS, 2):
                            load_values(act, s)

                    @block.vector
                    def _(dve):
                        step = Chain(dve, dve_step, "dve")
                        dve.wait_ge(stage_in, landed)
                        add = lambda c, n, ps: step(dve.tensor_tensor(S[:, c:c + n], ps, bias[:, c:c + n], ALU.add))
                        add(C_CMP, NC_S, P[:, 3, 0:NC_S])
                        add(C_SLC, PAST, P[:, 0:2, :].rearrange("p b c -> p (b c)"))
                        add(C_NSLC, NS, P[:, 3, 64:72])
                        add(C_WIN, WIN, P[:, 2, :])
                        add(C_NWIN, NS, P[:, 3, 72:80])

                        def maximum(b):
                            dve.tensor_reduce(st[:, b:b + 1], S[:, BR[b][0]:BR[b][1]], AX.X, ALU.max, negate=True)\
                               .then_inc(mx_ready, 1)

                        def scale(b, gate):
                            c = st[:, 4 + b:5 + b]
                            step(dve.tensor_scalar(c, c, 1e-30, None, ALU.max))
                            step(dve.reciprocal(c, c))
                            if gate:
                                step(dve.tensor_tensor(c, c, grow[:, b:b + 1], ALU.mult))
                            x = S[:, BR[b][0]:BR[b][1]]
                            return dve.tensor_scalar(x, x, c, None, ALU.mult)

                        maximum(0)
                        dve.wait_ge(grow_done, 1)
                        step(dve.tensor_tensor(gall[:, :, :], P[:, 5, 0:36].rearrange("p (h b) -> p h b", b=3),
                                               own_head[:, :].unsqueeze(2).to_broadcast([128, HEADS, 3]), ALU.mult))
                        step(dve.tensor_reduce(grow[:, :], gall[:, :, :].rearrange("p h b -> p b h"), AX.X, ALU.add))
                        dve.wait_ge(exp_done, 1)
                        scale(0, False).then_inc(pc_ready, 1)
                        dve.wait_ge(imp_done, 1)
                        score, last = st[:, 16:30], st[:, 10:11]
                        step(dve.tensor_reduce(score, P[:, 4, 4:60].rearrange("p (b c) -> p b c", c=4), AX.X, ALU.add))
                        step(dve.tensor_tensor(score, score, P[:, 4, 3:56:4], ALU.add))
                        step(dve.tensor_reduce(st[:, 8:9], score, AX.X, ALU.min))
                        step(dve.tensor_scalar(score, score, st[:, 8:9], None, ALU.is_le))
                        step(dve.tensor_tensor(score, score, blockno[:, :], ALU.mult))
                        step(dve.tensor_reduce(last, score, AX.X, ALU.max))
                        step(dve.tensor_scalar(score, blockno[:, :], last, NEG, ALU.is_equal, ALU.mult))
                        sel = S[:, 64:960].rearrange("p (b c) -> p b c", b=14)
                        step(dve.tensor_tensor(sel, sel, score.unsqueeze(2).to_broadcast([128, 14, 64]), ALU.add))
                        maximum(1)
                        maximum(2)
                        x = S[:, C_CMP:NCOL]
                        step(dve.tensor_scalar(x, x, grow[:, 0:1], None, ALU.mult))
                        dve.wait_ge(exp_done, 2)
                        step(scale(1, True))
                        dve.wait_ge(exp_done, 3)
                        scale(2, True).then_inc(p_ready, 1)
                        dve.wait_ge(pv_done, NS)
                        for gp in range(2):
                            for g2 in range(2):
                                r = slice(64 * g2, 64 * g2 + 64)
                                step(dve.tensor_copy(mix[r, 2 + 3 * gp:5 + 3 * gp, SEQ:T],
                                                     P[r, gp, 32 * g2:32 * g2 + 24]
                                                     .rearrange("p (s r) -> p r s", r=REP)))

        def prompt_attention(mix, Z, gates, Vt, VCp, KCb, KB):
            with ExitStack() as ctx:
                dist = sb(ctx, "dist", [128, 512])
                cbias = sb(ctx, "cbias", [128, NQ, HEADS, 32])
                cok = sb(ctx, "cok", [128, NQ, 1, 32])
                Pc = sb(ctx, "Pc", [128, NQ, HEADS, 32])
                PcT = sb(ctx, "PcT", [128, NQ, 3, 128])
                cst = sb(ctx, "cst", [128, 2, NQ * HEADS])
                SB = 5
                S = sb(ctx, "S_", [128, SB, 2, 512])
                PT = sb(ctx, "PT_", [128, 2, 2, 512])
                st = sb(ctx, "st_", [128, SB, 4])
                cscored = sem("cscored")
                cmx_ready = sem("cmx_ready")
                cexp_done = sem("cexp_done")
                cp_ready = sem("cp_ready")
                cturned = sem("cturned")
                cpt_ready = sem("cpt_ready")
                s_done = sem("s_done")
                s_read = sem("s_read")
                m_ready = sem("m_ready")
                e_done = sem("e_done")
                pr_ready = sem("pr_ready")
                t_done = sem("t_done")
                t_copied = sem("t_copied")
                o_done = sem("o_done")
                o_copied = sem("o_copied")
                state["stage"] += 48
                landed = state["stage"]
                UNITS = [(gp, r, i, g2) for gp in range(2) for r in range(REP) for i in range(NQ) for g2 in range(2)]
                NUN = len(UNITS)
                head = lambda gp, r, g2: g2 * 6 + gp * 3 + r
                gate_col = lambda gp, r, g2, b: 9 * (2 * gp + g2) + 3 * r + b

                with nc.Block(no_gpsimd_drain=True) as block:
                    @block.sync
                    def _(sp):
                        sp.dma_start(cbias[:, :, :, :], a["cmpbias"]).then_inc(stage_in, 16)
                        sp.dma_start(cok[:, :, :, :], a["cmpok"]).then_inc(stage_in, 16)
                        sp.dma_start(dist[:, :], a["dist"]).then_inc(stage_in, 16)
                        stream_weights(sp, U_OUT + RING)

                    @block.tensor
                    def _(pe):
                        for i in range(NQ):
                            for gp in range(2):
                                for r in range(REP):
                                    for g2 in range(2):
                                        q = slice(64 * g2, 64 * g2 + 64)
                                        c = 32 * head(gp, r, 0)
                                        mm = pe.matmul(P[:, 4 * g2 + i, c:c + 32], Z[q, 2 + 3 * gp + r, i * 128:i * 128 + 128],
                                                       KCb[q, NS, gp, 0:32], start=True, stop=True)
                        mm.then_inc(cscored, 1)
                        pe.wait_ge(cp_ready, 1)
                        for i in range(NQ):
                            for n in range(3):
                                mm = pe.transpose(P[:, 4 + i, n * 128:n * 128 + 128],
                                                  Pc[:, i, 4 * n:4 * n + 4, :].rearrange("p h c -> p (h c)"),
                                                  ident[:, :])
                        mm.then_inc(cturned, 1)

                        def scores(u):
                            gp, r, i, g2 = UNITS[u]
                            if u >= 2:
                                pe.wait_ge(s_read, u - 1)
                            else:
                                pe.wait_ge(cp_ready, 1)
                            q = slice(64 * g2, 64 * g2 + 64)
                            for b in range(2):
                                mm = pe.matmul(P[:, u % 2 * 2 + b, 0:128 * (i + 1)],
                                               Z[q, 2 + 3 * gp + r, i * 128:i * 128 + 128],
                                               Z[q, KB(2 + 2 * b, gp), 0:128 * (i + 1)], start=True, stop=True)
                            mm.then_inc(s_done, 1)

                        def turn(u):
                            pe.wait_ge(pr_ready, u + 1)
                            if u == 0:
                                pe.wait_ge(cpt_ready, 1)
                            i = UNITS[u][2]
                            for b in range(2):
                                if u:
                                    pe.wait_ge(t_copied, 2 * u - 1 + b)
                                for t in range(i + 1):
                                    mm = pe.transpose(P[:, 4 + b, t * 128:t * 128 + 128],
                                                      S[:, u % SB, b, t * 128:t * 128 + 128], ident[:, :])
                                mm.then_inc(t_done, 1)

                        def values(u):
                            gp, r, i, g2 = UNITS[u]
                            pair = u // 8
                            if u % 8 == 0 and pair >= 2:
                                pe.wait_ge(o_copied, pair - 1)
                            out = P[64 * g2:64 * g2 + 64, 6 + pair % 2, i * 128:i * 128 + 128]
                            d = slice(128 * gp + 64 * g2, 128 * gp + 64 * g2 + 64)
                            hh = head(gp, r, g2)
                            k = slice(32 * (hh % 4), 32 * (hh % 4) + 32)
                            first = True
                            for b in range(2):
                                pe.wait_ge(t_copied, 2 * u + b + 1)
                                for t in range(i + 1):
                                    pe.matmul(out, Vt[:, b, t, d], PT[:, u % 2, b, t * 128:t * 128 + 128],
                                              start=first, stop=False)
                                    first = False
                            pe.matmul(out, VCp[k, d], PcT[k, i, hh // 4, :], start=False, stop=True)\
                              .then_inc(o_done, 1)

                        scores(0)
                        scores(1)
                        scores(2)
                        for u in range(NUN + 1):
                            if u + 3 < NUN:
                                scores(u + 3)
                            if u < NUN:
                                turn(u)
                            if u >= 1:
                                values(u - 1)

                    @block.scalar
                    def _(act):
                        act.wait_ge(cmx_ready, 1)
                        act.activation(Pc[:, :, :, :], Pc[:, :, :, :], ACT.Exp).then_inc(cexp_done, 1)
                        act.wait_ge(cturned, 1)
                        act.activation(PcT[:, :, :, :].rearrange("p i n c -> p i (n c)"), P[:, 4:8, 0:384],
                                       ACT.Copy).then_inc(cpt_ready, 1)

                        for u in range(NUN + 3):
                            if u < NUN:
                                act.wait_ge(m_ready, u + 1)
                                n = 128 * (UNITS[u][2] + 1)
                                for b in range(2):
                                    mm = act.activation(S[:, u % SB, b, 0:n], S[:, u % SB, b, 0:n], ACT.Exp,
                                                        bias=st[:, u % SB, b:b + 1],
                                                        accum_out=st[:, u % SB, 2 + b:3 + b])
                                mm.then_inc(e_done, 1)
                            if u >= 3:
                                v = u - 3
                                if v >= 2:
                                    act.wait_ge(o_done, v - 1)
                                n = 128 * (UNITS[v][2] + 1)
                                for b in range(2):
                                    act.wait_ge(t_done, 2 * v + b + 1)
                                    act.activation(PT[:, v % 2, b, 0:n], P[:, 4 + b, 0:n], ACT.Copy)\
                                       .then_inc(t_copied, 1)

                    @block.vector
                    def _(dve):
                        step = Chain(dve, dve_step, "dve")
                        dve.wait_ge(stage_in, landed)
                        dve.wait_ge(cscored, 1)
                        flat = lambda x, g2: x[:, :, 6 * g2:6 * g2 + 6, :].rearrange("p i h c -> p i (h c)")
                        for g2 in range(2):
                            step(dve.tensor_tensor(flat(Pc, g2), P[:, 4 * g2:4 * g2 + 4, 0:192], flat(cbias, g2),
                                                   ALU.add))
                        rows = Pc[:, :, :, :].rearrange("p i h c -> p (i h) c")
                        mx, sm = cst[:, 0, :], cst[:, 1, :]
                        wide = lambda x: x.unsqueeze(2).to_broadcast([128, NQ * HEADS, 32])
                        step(dve.tensor_reduce(mx, rows, AX.X, ALU.max))
                        dve.tensor_tensor(rows, rows, wide(mx), ALU.subtract).then_inc(cmx_ready, 1)
                        dve.wait_ge(cexp_done, 1)
                        step(dve.tensor_tensor(Pc[:, :, :, :], Pc[:, :, :, :],
                                               cok[:, :, :, :].to_broadcast([128, NQ, HEADS, 32]), ALU.mult))
                        step(dve.tensor_reduce(sm, rows, AX.X, ALU.add))
                        step(dve.tensor_scalar(sm, sm, 1e-30, None, ALU.max))
                        step(dve.reciprocal(sm, sm))
                        for gp in range(2):
                            for g2 in range(2):
                                c = gate_col(gp, 0, g2, 0)
                                x = sm.rearrange("p (i g q r) -> p i g q r", i=NQ, q=2, g=2)[:, :, g2, gp, :]
                                step(dve.tensor_tensor(x, x, gates[:, 0:NQ, c:c + 7:3], ALU.mult))
                        dve.tensor_tensor(rows, rows, wide(sm), ALU.mult).then_inc(cp_ready, 1)

                        def copy_out(pair):
                            dve.wait_ge(o_done, 8 * (pair + 1))
                            dve.tensor_copy(mix[:, 2 + pair, 0:SEQ], P[:, 6 + pair % 2, :]).then_inc(o_copied, 1)

                        for u in range(NUN + 2):
                            if u < NUN:
                                gp, r, i, g2 = UNITS[u]
                                n = 128 * (i + 1)
                                dve.wait_ge(s_done, u + 1)
                                if u >= SB:
                                    dve.wait_ge(t_done, 2 * (u - SB + 1))
                                slope = float(SLOPE[(2 * gp + g2) * REP + r])
                                for b in range(2):
                                    mm = dve.scalar_tensor_tensor(
                                        out=S[:, u % SB, b, 0:n], in0=dist[:, 512 - n:512], scalar=slope,
                                        in1=P[:, u % 2 * 2 + b, 0:n], op0=ALU.mult, op1=ALU.add)
                                mm.then_inc(s_read, 1)
                                dve.wait_ge(s_read, u + 1)
                                dve.tensor_reduce(st[:, u % SB, 0:2], S[:, u % SB, :, 0:n], AX.X, ALU.max, negate=True)\
                                   .then_inc(m_ready, 1)
                            if u >= 2:
                                v = u - 2
                                gp, r, i, g2 = UNITS[v]
                                n = 128 * (i + 1)
                                dve.wait_ge(e_done, v + 1)
                                sums = st[:, v % SB, 2:4]
                                step(dve.tensor_scalar(sums, sums, 1e-30, None, ALU.max))
                                step(dve.reciprocal(sums, sums))
                                c = gate_col(gp, r, g2, 1)
                                step(dve.tensor_tensor(sums, sums, gates[:, i, c:c + 2], ALU.mult))
                                for b in range(2):
                                    x = S[:, v % SB, b, 0:n]
                                    mm = dve.tensor_scalar(x, x, sums[:, b:b + 1], None, ALU.mult)
                                mm.then_inc(pr_ready, 1)
                            if u >= 12 and (u - 12) % 8 == 0:
                                copy_out((u - 12) // 8)
                        copy_out(NUN // 8 - 1)

        def layer1():
            with ExitStack() as c0:
                R = sb(c0, "R", [128, KC, T])
                with ExitStack() as c1:
                    K, V = (sb(c1, n, [128, KC, T]) for n in ("K", "V"))
                    tg = sb(c1, "tg", [128, T])
                    tw = sb(c1, "tw", [64, T])
                    ta = sb(c1, "ta", [64, T])
                    mix_and_project(R, K, V, tw, ta, tg)
                    L = sb(c1, "L", [128, KC, T])
                    A = sb(c1, "A", [128, KC, T])
                    N_ = sb(c1, "N_", [128, KC, T])
                    rates(R, K, L, A, N_, tw, ta)
                    chunks(R, K, V, L, A, N_)
                    sample_state(R, K, V, L, A, N_)
                    output(R, K, V, L, A, tg)
                add_product(R, list(range(U_WO, U_WO + 4)), "wo")

        def mix_and_project(R, K, V, tw, ta, tg):
            with ExitStack() as ctx:
                xn = sb(ctx, "xn1", [128, KC, T])
                xx = sb(ctx, "xx", [128, KC, T])
                xf = V[:, 5:7, :]
                xm = [sb(ctx, "xm" + n, [128, KC, T], F32R) for n in "hl"]
                ws = sb(ctx, "ws_mix", [128, 2, 2, UW], F32R)
                lw = [V[:, 0, k * 64:k * 64 + 64] for k in range(KC)]
                la = [V[:, 1, k * 64:k * 64 + 64] for k in range(KC)]
                lg = [V[:, 2 + k // 4, k % 4 * 128:k % 4 * 128 + 128] for k in range(KC)]
                prev = V[:, 4, 0:KC * NS].rearrange("p (k s) -> p k s", k=KC)
                mixed = sem("mixed")
                low_free = sem("low_free")
                low_used = sem("low_used")
                normed = sem("normed")
                ORDER = ((1, (lw, tw, 64, ACT.Tanh)), (4, (la, ta, 64, ACT.Copy)), (5, (lg, tg, 128, ACT.Sigmoid)),
                         (0, R), (2, K), (3, V))
                x0 = take_splits(3 * KC)
                firsts = [plan(list(range(U_R + 4 * j, U_R + 4 * j + 4))) for j in range(3)]
                i = state["norm"]
                state["norm"] += 1
                state["stage"] += 64
                landed = state["stage"]
                state["stores"] += 16

                with nc.Block(no_gpsimd_drain=True) as block:
                    @block.sync
                    def _(sp):
                        for dst, src in ((prev, a["state_shift"]),
                                         (V[:, 0, 0:512], a["rwkv_w1"].rearrange("p k c -> p (k c)")),
                                         (V[:, 1, 0:512], a["rwkv_a1"].rearrange("p k c -> p (k c)")),
                                         (V[:, 2:4, 0:512], a["rwkv_g1"].rearrange("p (b k) c -> p b (k c)", b=2))):
                            sp.dma_start(dst, src).then_inc(stage_in, 16)
                        stream_weights(sp, U_WO)
                        sp.wait_ge(normed, 1)
                        sp.dma_start(o["shift"], xn[:, :, SEQ - 1:T]).then_inc(stores, 16)
                        stream_weights(sp, U_WO + 1)
                        sp.wait_ge(stores, state["stores"])

                    @block.gpsimd
                    def _(pool):
                        weight_rests(pool, range(U_R, U_WO), ws)

                    @block.tensor
                    def _(pe):
                        norm_pe(pe, i, xn)
                        for j in range(3):
                            w, _, n, _ = ORDER[j][1]
                            for k in range(KC):
                                pe.wait_ge(mixed, j * KC + k + 1)
                                for hf in range(2):
                                    mm = pe.matmul(P[0:n, 2 * j + hf, 0:HT], w[k],
                                                   xf[:, k % 2, hf * HT:(hf + 1) * HT], start=k == 0,
                                                   stop=k == KC - 1)
                                mm.then_inc(low_used, 1)
                        pe.wait_ge(low_free, 3)
                        for j in range(3):
                            dense(pe, firsts[j], list(range(U_R + 4 * j, U_R + 4 * j + 4)), ws, xm,
                                  chunk_ready=lambda k, j=j: pe.wait_ge(xsplit_ready, x0 + j * KC + k + 1))

                    @block.scalar
                    def _(act):
                        units = range(U_R, U_WO)
                        norm_act(act, i, xn, None, units, ws)
                        for j in range(3):
                            _, dst, n, f = ORDER[j][1]
                            act.wait_ge(low_used, KC * (j + 1))
                            act.activation(halves(dst[0:n, :]), P[0:n, 2 * j:2 * j + 2, 0:HT], f).then_inc(low_free, 1)
                        for j, dst in enumerate((R, K, V)):
                            for k in range(KC):
                                act.wait_ge(mixed, (3 + j) * KC + k + 1)
                                if k == 0 and j:
                                    act.wait_ge(tile_done, firsts[j])
                                split_head(act, xf[:, k % 2, :], xm[0][:, k, :])
                            for m in range(KC):
                                act.wait_ge(tile_done, firsts[j] + m + 1)
                                act.activation(halves(dst[:, m, :]), tile(firsts[j] + m), ACT.Copy)\
                                   .then_inc(tile_free, 1)
                                if m % 2:
                                    weight_head(act, U_R + 4 * j + m // 2 + 2, units, ws)

                    @block.vector
                    def _(dve):
                        step = Chain(dve, dve_step, "dve")
                        norm_dve(dve, step, i, xn, V_MIX + KC)
                        dve.wait_ge(xn_ready, (i + 1) * KC)
                        dve.wait_ge(stage_in, landed)
                        dve.tensor_tensor(xx[:, :, 1:SEQ], xn[:, :, 0:SEQ - 1], xn[:, :, 1:SEQ], ALU.subtract)\
                           .then_inc(normed, 1)
                        dve.tensor_scalar(xx[:, :, 0:1], xn[:, :, 0:1], -1.0, None, ALU.mult)
                        step(dve.tensor_tensor(xx[:, :, SEQ:T], prev, xn[:, :, SEQ:T], ALU.subtract))
                        dve.wait_ge(normed, 1)
                        for j, (mu, _) in enumerate(ORDER):
                            for k in range(KC):
                                n = j * KC + k
                                if 2 <= n < 3 * KC + 2:
                                    dve.wait_ge(low_used, n - 1)
                                c = V_MU + KC * mu + k
                                dve.scalar_tensor_tensor(out=xf[:, k % 2, :], in0=xx[:, k, :], scalar=vec[:, c:c + 1],
                                                         in1=xn[:, k, :], op0=ALU.mult, op1=ALU.add)\
                                   .then_inc(mixed, 1)
                                if j >= 3:
                                    if k == 0 and j > 3:
                                        dve.wait_ge(tile_done, firsts[j - 3])
                                    split_rest(dve, x0 + n - 3 * KC, xf[:, k % 2, :], xm[0][:, k, :], xm[1][:, k, :])

        def rates(R, K, L, A, N_, tw, ta):
            with ExitStack() as ctx:
                w2 = sb(ctx, "w2", [64, D])
                a2 = sb(ctx, "a2", [64, D])
                sq = sb(ctx, "sq2", [128, 2, T])
                lo_done = sem("lo_done")
                lo_free = sem("lo_free")
                kk_sq = sem("kk_sq")
                kk_ss = sem("kk_ss")
                kk_read = sem("kk_read")
                kk_root = sem("kk_root")
                state["stage"] += 32
                landed = state["stage"]
                with nc.Block(no_gpsimd_drain=True) as block:
                    @block.sync
                    def _(sp):
                        sp.dma_start(w2[:, :], a["rwkv_w2"]).then_inc(stage_in, 16)
                        sp.dma_start(a2[:, :], a["rwkv_a2"]).then_inc(stage_in, 16)

                    @block.tensor
                    def _(pe):
                        pe.wait_ge(stage_in, landed)
                        for n in range(2 * KC):
                            if n >= 2:
                                pe.wait_ge(lo_free, n - 1)
                            w, x = ((w2, tw), (a2, ta))[n // KC]
                            m = n % KC
                            for hf in range(2):
                                mm = pe.matmul(P[:, 2 * (n % 2) + hf, 0:HT], w[:, m * 128:(m + 1) * 128],
                                               x[:, hf * HT:(hf + 1) * HT], start=True, stop=True)
                            mm.then_inc(lo_done, 1)
                        for m in range(KC):
                            pe.wait_ge(kk_sq, m + 1)
                            if m >= 2:
                                pe.wait_ge(kk_root, m - 1)
                            for hf in range(2):
                                mm = pe.matmul(P[:, 4 + 2 * (m % 2) + hf, 0:HT], headones[:, :],
                                               sq[:, m % 2, hf * HT:(hf + 1) * HT], start=True, stop=True)
                            mm.then_inc(kk_ss, 1)

                    @block.scalar
                    def _(act):
                        for n in range(2 * KC):
                            dst, col = ((L, V_W0), (A, V_A0))[n // KC]
                            m = n % KC
                            act.wait_ge(lo_done, n + 1)
                            act.activation(halves(dst[:, m, :]), P[:, 2 * (n % 2):2 * (n % 2) + 2, 0:HT], ACT.Sigmoid,
                                           bias=vec[:, col + m:col + m + 1]).then_inc(lo_free, 1)
                        for m in range(KC):
                            act.wait_ge(kk_ss, m + 1)
                            act.activation(halves(sq[:, m % 2, :]), P[:, 4 + 2 * (m % 2):6 + 2 * (m % 2), 0:HT],
                                           ACT.Sqrt).then_inc(kk_root, 1)

                    @block.vector
                    def _(dve):
                        step = Chain(dve, dve_step, "dve")

                        def square(m):
                            c = V_KK + m
                            step(dve.tensor_scalar(N_[:, m, :], K[:, m, :], vec[:, c:c + 1], None, ALU.mult))
                            dve.tensor_tensor(sq[:, m % 2, :], N_[:, m, :], N_[:, m, :], ALU.mult).then_inc(kk_sq, 1)

                        square(0)
                        square(1)
                        for m in range(KC):
                            s = sq[:, m % 2, :]
                            dve.wait_ge(kk_root, m + 1)
                            step(dve.tensor_scalar(s, s, 1e-12, None, ALU.max))
                            step(dve.reciprocal(s, s))
                            step(dve.tensor_tensor(N_[:, m, :], N_[:, m, :], s, ALU.mult))
                            if m + 2 < KC:
                                square(m + 2)
                        dve.wait_ge(lo_free, 2 * KC)
                        Lf = L[:, :, :].rearrange("p k t -> p (k t)")
                        step(dve.tensor_scalar(Lf, Lf, -math.exp(-0.5), None, ALU.mult))
                        for m in range(KC):
                            s = sq[:, m % 2, :]
                            c = V_KA + m
                            step(dve.tensor_scalar(s, A[:, m, :], 1.0, vec[:, c:c + 1], ALU.subtract, ALU.mult))
                            step(dve.scalar_tensor_tensor(out=K[:, m, :], in0=s, scalar=1.0, in1=K[:, m, :],
                                                          op0=ALU.add, op1=ALU.mult))
                            step(dve.tensor_tensor(A[:, m, :], A[:, m, :], N_[:, m, :], ALU.mult))

        def chunks(R, K, V, L, A, N_):
            with ExitStack() as ctx:
                tri = sb(ctx, "tri", [128, 128])
                level = sb(ctx, "level", [128, 6, CH])
                ident2 = sb(ctx, "ident2", [128, 64])
                restart = sb(ctx, "restart", [128, KC, CH + 1])
                Eend = sb(ctx, "Eend", [128, 3, KC])
                E = sb(ctx, "E", [128, 2, KC, CH + 1])
                Ls, Lc = E[:, 0], E[:, 1]
                Ep, Em = E[:, 0], E[:, 1]
                AR = sb(ctx, "AR", [128, 2, KC, 2, CH])
                BK = sb(ctx, "BK", [128, 2, KC, CH])
                G = sb(ctx, "G", [128, 2, 2, KC, 2, CH])
                assert U_WO % RING == RING - 1
                spare = ring[:, 0:RING - 1, :].rearrange("p r c -> p (r c)")
                tm = spare[:, 0:3072].rearrange("p (d j n t) -> p d j n t", d=2, j=3, n=KC)
                XL = spare[:, 3072:4096].rearrange("p (d n t) -> p d n t", d=2, n=KC)
                Uf = spare[:, 4096:4608].rearrange("p (n t) -> p n t", n=KC)
                TUP = 512 + 32
                TU = spare[:, 4608:4608 + 2 * TUP].rearrange("p (h c) -> p h c", h=2)
                Tm = lambda hf: TU[:, hf, 0:256].rearrange("p (n t) -> p n t", n=4)
                Um = lambda hf: TU[:, hf, 256:512].rearrange("p (n t) -> p n t", n=4)
                Y = sb(ctx, "Y", [128, 5, 2, 4, CH])
                X = rstd[:, 0:512].rearrange("p (n t) -> p n t", n=KC)
                SA = sb(ctx, "SA", [128, KC, CH])
                S = sb(ctx, "S1", [128, KC, CH])
                names = ("ls_ready ep_done em_done til_ready g_done g_ready tm_done tm_ready y_done y_ready tu_done "
                         "tu_ready uf_ready y_zero xl_ready x_done x_ready sa_done sa_ready o_done s_done s_ready o_read")
                (ls_ready, ep_done, em_done, til_ready, g_done, g_ready, tm_done, tm_ready, y_done, y_ready, tu_done,
                 tu_ready, uf_ready, y_zero, xl_ready, x_done, x_ready, sa_done, sa_ready, o_done, s_done, s_ready, o_read) = \
                    (sem("w_" + n) for n in names.split())
                state["stage"] += 64
                landed = state["stage"]
                state["stores"] += 16
                LEV = 5
                half_rows = [(p, slice(64 * p, 64 * p + 64)) for p in range(2)]
                blocks = lambda x, lv, odd: x.rearrange("p (m two w) -> p m two w", two=2, w=1 << lv)[:, :, odd, :]
                compact = lambda x, lv: x.rearrange("p (m w) -> p m w", w=1 << lv)
                y_no = lambda c, lv, hf: 2 * (c * LEV + lv - 1) + hf + 1
                tu_no = lambda c, lv, hf: 2 * (c * (LEV + 1) + lv) + hf + 1

                with nc.Block(no_gpsimd_drain=True) as block:
                    @block.sync
                    def _(sp):
                        for dst, src in ((tri[:, :], "tri"), (level[:, :, :], "level"), (ident2[:, :], "ident2"),
                                         (restart[:, :, :], "restart")):
                            sp.dma_start(dst, a[src]).then_inc(stage_in, 16)
                        sp.wait_ge(x_ready, NCH + 1)
                        sp.dma_start(o["wkv_p"], X[:, :, :]).then_inc(stores, 16)
                        sp.wait_ge(stores, state["stores"])

                    G_BANK = (2, 3, 6, 7)

                    @block.tensor
                    def _(pe):
                        pe.wait_ge(stage_in, landed)

                        def scores(c, q):
                            pe.wait_ge(til_ready, c + 1)
                            if c and q < 3:
                                pe.wait_ge(tm_ready, 3 * (c - 1) + q + 1)
                            elif c:
                                pe.wait_ge(g_ready, 4 * c)
                            for p, r in half_rows:
                                for n in range(4):
                                    nn = q % 2 * 4 + n
                                    mm = pe.matmul(P[r, G_BANK[q], n * 128:n * 128 + 128], BK[r, q // 2, nn, :],
                                                   AR[r, c % 2, nn, :, :].rearrange("p a t -> p (a t)"),
                                                   start=True, stop=True)
                            mm.then_inc(g_done, 1)

                        def turn(c, j):
                            pe.wait_ge(g_ready, 4 * c + j + 1)
                            for p, r in half_rows:
                                for n in range(KC):
                                    x = V[r, n, c * CH:(c + 1) * CH] if j == 0 else BK[r, j - 1, n, :]
                                    mm = pe.matmul(P[r, G_BANK[j], n * CH:(n + 1) * CH], x, ident2[r, :],
                                                   start=True, stop=True)
                            mm.then_inc(tm_done, 1)

                        def times_t(c, lv):
                            pe.wait_ge(xl_ready, c * (LEV + 1) + lv + 1)
                            for hf in range(2):
                                if c or lv:
                                    pe.wait_ge(tu_ready, tu_no(c, lv, hf) - 2)
                                for p, r in half_rows:
                                    for n in range(4):
                                        t = blocks(Tm(hf)[r, n, :] if lv else ident2[r, :], lv, 0)
                                        mm = pe.matmul(compact(P[r, hf, n * 32:n * 32 + 32], lv),
                                                       XL[r, (c * (LEV + 1) + lv) % 2, 4 * hf + n, :], t,
                                                       start=True, stop=True)
                                mm.then_inc(y_done, 1)

                        def t_times(c, lv):
                            for hf in range(2):
                                pe.wait_ge(y_ready, y_no(c, lv, hf))
                                for which in range(2):
                                    if which == 0 and lv == LEV:
                                        continue
                                    for p, r in half_rows:
                                        for n in range(4):
                                            u, y = Um(hf)[r, n, :], Y[r, lv - 1, hf, n, :]
                                            w, x = (u, blocks(y, lv, 0)) if which == 0 else (y, blocks(u, lv, 1))
                                            at = 128 + 128 * which + 32 * n
                                            mm = pe.matmul(compact(P[r, hf, at:at + 32], lv), w, x,
                                                           start=True, stop=True)
                                mm.then_inc(tu_done, 1)

                        def x_part(c):
                            pe.wait_ge(s_ready, c + 1)
                            pe.wait_ge(g_ready, 4 * c + 4)
                            pe.wait_ge(tm_ready, 3 * c + 3)
                            if c:
                                pe.wait_ge(o_read, c)
                            for p, r in half_rows:
                                for n in range(KC):
                                    out = P[r, 4, n * CH:(n + 1) * CH]
                                    pe.matmul(out, AR[r, c % 2, n, 0, :], S[r, n, :], start=True, stop=False)
                                    mm = pe.matmul(out, G[r, c % 2, 1, n, 0, :], tm[r, c % 2, 0, n, :],
                                                   start=False, stop=True)
                            mm.then_inc(x_done, 1)

                        def sa_part(c):
                            pe.wait_ge(tu_ready, tu_no(c, LEV, 1))
                            pe.wait_ge(uf_ready, c + 1)
                            pe.wait_ge(x_ready, c + 1)
                            for p, r in half_rows:
                                for n in range(KC):
                                    mm = pe.matmul(P[r, 5, n * CH:(n + 1) * CH], Uf[r, n, :], X[r, n, :],
                                                   start=True, stop=True)
                            mm.then_inc(sa_done, 1)

                        def o_part(c, hf):
                            pe.wait_ge(sa_ready, c + 1)
                            for p, r in half_rows:
                                for n in range(4 * hf, 4 * hf + 4):
                                    out = P[r, 4, n * CH:(n + 1) * CH]
                                    pe.matmul(out, S[r, n, :], AR[r, c % 2, n, 1, :], start=True, stop=False)
                                    pe.matmul(out, SA[r, n, :], G[r, c % 2, 0, n, 1, :], start=False, stop=False)
                                    mm = pe.matmul(out, tm[r, c % 2, 0, n, :], G[r, c % 2, 1, n, 1, :],
                                                   start=False, stop=True)
                            if hf:
                                mm.then_inc(o_done, 1)

                        def s_part(c):
                            for p, r in half_rows:
                                for n in range(KC):
                                    out = P[r, 5, n * CH:(n + 1) * CH]
                                    pe.matmul(out, tm[r, c % 2, 1, n, :], SA[r, n, :], start=True, stop=False)
                                    mm = pe.matmul(out, tm[r, c % 2, 2, n, :], tm[r, c % 2, 0, n, :],
                                                   start=False, stop=True)
                            mm.then_inc(s_done, 1)

                        for q in range(4):
                            scores(0, q)
                        for j in range(3):
                            turn(0, j)
                        for c in range(NCH + 1):
                            before, after = c > 0, c + 1 < NCH
                            for lv in range(LEV + 1):
                                if c < NCH:
                                    times_t(c, lv)
                                if before and lv == 0:
                                    x_part(c - 1)
                                if before and lv == 1:
                                    sa_part(c - 1)
                                if before and lv == 2:
                                    o_part(c - 1, 1)
                                if after and lv in (3, 4):
                                    scores(c + 1, 2 * (lv - 3))
                                if after and lv == 5:
                                    turn(c + 1, 0)
                                if c < NCH and lv:
                                    t_times(c, lv)
                                if before and lv == 1:
                                    o_part(c - 1, 0)
                                if before and lv == 2:
                                    s_part(c - 1)
                                if after and lv in (3, 4):
                                    scores(c + 1, 2 * (lv - 3) + 1)
                                if after and lv == 5:
                                    turn(c + 1, 1)
                                    turn(c + 1, 2)
                        pe.wait_ge(s_ready, NCH + 1)
                        pe.wait_ge(o_read, NCH)
                        for p, r in half_rows:
                            for n in range(KC):
                                mm = pe.matmul(P[r, 4, n * CH:(n + 1) * CH], S[r, n, :], ident2[r, :],
                                               start=True, stop=True)
                        mm.then_inc(x_done, 1)

                    @block.scalar
                    def _(act):
                        by_n = lambda bank: P[:, bank, :].rearrange("p (n t) -> p n t", n=KC)

                        def exps(c):
                            act.wait_ge(ls_ready, c + 1)
                            act.activation(Ep, Lc, ACT.Exp).then_inc(ep_done, 1)
                            act.activation(Em, Lc, ACT.Exp, scale=-1.0).then_inc(em_done, 1)

                        def copies(c):
                            if c >= 2:
                                act.wait_ge(o_done, c - 1)
                                act.wait_ge(s_done, c - 1)
                            for j in range(3):
                                act.wait_ge(tm_done, 3 * c + j + 1)
                                act.activation(tm[:, c % 2, j, :, :], by_n(G_BANK[j]), ACT.Copy).then_inc(tm_ready, 1)

                        def y_copy(c, lv):
                            for hf in range(2):
                                act.wait_ge(y_done, tu_no(c, lv, hf))
                                act.activation(blocks(Y[:, lv - 1, hf, :, :].rearrange("p n t -> p (n t)"), lv, 0),
                                               compact(P[:, hf, 0:128], lv), ACT.Copy).then_inc(y_ready, 1)

                        def xc(c):
                            act.wait_ge(x_done, c + 1)
                            act.activation(X[:, :, :], by_n(4), ACT.Copy).then_inc(x_ready, 1)

                        def sac(c):
                            act.wait_ge(sa_done, c + 1)
                            act.activation(SA[:, :, :], by_n(5), ACT.Copy).then_inc(sa_ready, 1)

                        def oc(c):
                            act.wait_ge(o_done, c + 1)
                            act.activation(L[:, :, c * CH:(c + 1) * CH], by_n(4), ACT.Copy).then_inc(o_read, 1)

                        exps(0)
                        exps(1)
                        copies(0)
                        for c in range(NCH + 1):
                            for lv in range(LEV + 1):
                                if lv == 1:
                                    act.wait_ge(y_zero, 1)
                                if c < NCH and lv:
                                    y_copy(c, lv)
                                if c and lv < 3:
                                    (xc, sac, oc)[lv](c - 1)
                            if c + 1 < NCH:
                                copies(c + 1)
                            if c + 2 < NCH:
                                exps(c + 2)
                        xc(NCH)

                    @block.gpsimd
                    def _(pool):
                        pool.wait_ge(stage_in, landed)
                        for c in range(NCH):
                            pool.wait_ge(g_ready, 4 * c + 2)
                            for lv in range(LEV + 1):
                                e = c * (LEV + 1) + lv
                                if e >= 2:
                                    pool.wait_ge(tu_ready, 2 * (e - 1))
                                pool.tensor_tensor(XL[:, e % 2, :, :], G[:, c % 2, 0, :, 0, :],
                                                   level[:, lv, :].unsqueeze(1).to_broadcast([128, KC, CH]),
                                                   ALU.mult).then_inc(xl_ready, 1)
                            pool.wait_ge(tu_ready, tu_no(c, LEV - 1, 1))
                            if c:
                                pool.wait_ge(sa_done, c)
                            pool.tensor_copy(Uf[:, :, 0:32].rearrange("p (h n) t -> p h n t", h=2),
                                             TU[:, :, 256:512].rearrange("p h (n t) -> p h n t", n=4)[:, :, :, 0:32])\
                                .then_inc(uf_ready, 1)

                    @block.vector
                    def _(dve):
                        step = Chain(dve, dve_step, "dve")
                        dve.wait_ge(stage_in, landed)
                        dve.memset(S[:, :, :], 0.0).then_inc(s_ready, 1)
                        dve.memset(Y[:, :, :, :, :], 0.0).then_inc(y_zero, 1)
                        flat = lambda x: x.rearrange("p n t -> p (n t)")

                        def decays(c):
                            step(dve.memset(Ls[:, :, 0:1], 0.0))
                            step(dve.tensor_copy(Ls[:, :, 1:], L[:, :, c * CH:(c + 1) * CH]))
                            dve.tensor_tensor_scan(flat(Lc), flat(restart[:, :, :]), flat(Ls), 0.0,
                                                   ALU.mult, ALU.add).then_inc(ls_ready, 1)

                        def tilde_sources(c):
                            t = slice(c * CH, (c + 1) * CH)
                            dve.wait_ge(em_done, c + 1)
                            if c:
                                dve.wait_ge(tm_done, 3 * c)
                            dve.tensor_tensor(BK[:, 0, :, :], A[:, :, t], Em[:, :, 1:], ALU.mult)
                            step(dve.tensor_tensor(BK[:, 1, :, :], K[:, :, t], Em[:, :, 1:], ALU.mult))

                        def tilde_targets(c):
                            t = slice(c * CH, (c + 1) * CH)
                            dve.wait_ge(ep_done, c + 1)
                            if c >= 2:
                                dve.wait_ge(o_done, c - 1)
                            dve.tensor_copy(Eend[:, c % 3, :], Ep[:, :, CH])
                            dve.scalar_tensor_tensor(out=AR[:, c % 2, :, 0, :], in0=N_[:, :, t], scalar=-1.0,
                                                     in1=Ep[:, :, 0:CH], op0=ALU.mult, op1=ALU.mult)
                            step(dve.tensor_tensor(AR[:, c % 2, :, 1, :], R[:, :, t], Ep[:, :, 1:], ALU.mult))
                            dve.sem_inc(til_ready, 1)

                        def mask(c, q):
                            dve.wait_ge(g_done, 4 * c + q + 1)
                            n = slice(q % 2 * 4, q % 2 * 4 + 4)
                            dve.tensor_tensor(G[:, c % 2, q // 2, n, :, :].rearrange("p n a t -> p n (a t)"),
                                              P[:, G_BANK[q], :].rearrange("p (n t) -> p n t", n=4),
                                              tri[:, :].unsqueeze(1).to_broadcast([128, 4, 128]), ALU.mult)\
                               .then_inc(g_ready, 1)

                        def tu_first(c):
                            e = c * (LEV + 1)
                            dve.wait_ge(xl_ready, e + 1)
                            if c:
                                dve.wait_ge(uf_ready, c)
                                dve.wait_ge(tu_ready, 2 * e)
                            for hf in range(2):
                                dve.tensor_tensor(Um(hf), XL[:, e % 2, 4 * hf:4 * hf + 4, :],
                                                  ident2[:, :].unsqueeze(1).to_broadcast([128, 4, CH]), ALU.add)
                                dve.tensor_copy(Tm(hf)[:, :, 1::2],
                                                ident2[:, 1::2].unsqueeze(1).to_broadcast([128, 4, 32]))
                            for hf in range(2):
                                dve.wait_ge(y_done, tu_no(c, 0, hf))
                                dve.tensor_tensor(Tm(hf)[:, :, 0::2],
                                                  P[:, hf, 0:128].rearrange("p (n t) -> p n t", n=4),
                                                  ident2[:, 0::2].unsqueeze(1).to_broadcast([128, 4, 32]), ALU.add)\
                                   .then_inc(tu_ready, 1)

                        def tu(c, lv):
                            w = 1 << lv
                            for hf in range(2):
                                dve.wait_ge(tu_done, y_no(c, lv, hf))
                                dve.wait_ge(tu_ready, tu_no(c, lv - 1, hf))
                                if lv < LEV:
                                    x = TU[:, hf, 0:512 + 2 * w].rearrange("p (q c) -> p q c", q=2)[:, :, 0:256]
                                    x = x.rearrange("p q (m two w) -> p q m two w", two=2, w=w)[:, :, :, 0, :]
                                    dve.tensor_tensor(x, x, P[:, hf, 128:384].rearrange(
                                        "p (q m w) -> p q m w", q=2, w=w), ALU.add).then_inc(tu_ready, 1)
                                else:
                                    dve.tensor_tensor(Uf[:, 4 * hf:4 * hf + 4, 32:64], Um(hf)[:, :, 32:64],
                                                      P[:, hf, 256:384].rearrange("p (n t) -> p n t", n=4),
                                                      ALU.add).then_inc(tu_ready, 1)

                        def new_state(c):
                            dve.wait_ge(s_done, c + 1)
                            dve.wait_ge(o_done, c + 1)
                            step(dve.tensor_tensor(S[:, :, :], S[:, :, :],
                                                   P[:, 5, :].rearrange("p (n t) -> p n t", n=KC), ALU.add))
                            dve.tensor_tensor(S[:, :, :], S[:, :, :],
                                              Eend[:, c % 3, :].unsqueeze(2).to_broadcast([128, KC, CH]), ALU.mult)\
                               .then_inc(s_ready, 1)

                        decays(0)
                        tilde_sources(0)
                        tilde_targets(0)
                        decays(1)
                        for q in range(4):
                            mask(0, q)
                        for c in range(NCH + 1):
                            before, after = c > 0, c + 1 < NCH
                            for lv in range(LEV + 1):
                                if c < NCH:
                                    tu(c, lv) if lv else tu_first(c)
                                if after and lv == 1:
                                    tilde_sources(c + 1)
                                if after and lv == 2:
                                    tilde_targets(c + 1)
                                if before and lv == 3:
                                    new_state(c - 1)
                                if after and lv in (3, 4):
                                    mask(c + 1, 2 * (lv - 3))
                                    mask(c + 1, 2 * (lv - 3) + 1)
                            if c + 2 < NCH:
                                decays(c + 2)

        def sample_state(R, K, V, L, A, N_):
            with ExitStack() as ctx:
                ident2 = sb(ctx, "ident3", [128, 64])
                S = sb(ctx, "Ss", [128, NS, KC, HD])
                dg = sb(ctx, "dg", [128, NS, KC, HD])
                tmp = sb(ctx, "tmp", [128, NS, KC, HD])
                sa = sb(ctx, "sa", [128, NS, KC])
                dg_ready = sem("dg_ready")
                spread = sem("spread")
                spread_read = sem("spread_read")
                out_ready = sem("out_ready")
                dec_ready = sem("dec_ready")
                state["stage"] += 32
                landed = state["stage"]
                state["stores"] += 16
                VECS = 5
                with nc.Block(no_gpsimd_drain=True) as block:
                    @block.sync
                    def _(sp):
                        sp.dma_start(ident2[:, :], a["ident2"]).then_inc(stage_in, 16)
                        sp.dma_start(S[:, :, :, :], a["state_wkv"]).then_inc(stage_in, 16)
                        stream_weights(sp, U_WO + RING)
                        sp.wait_ge(out_ready, 1)
                        sp.dma_start(o["wkv_s"], S[:, :, :, :]).then_inc(stores, 16)
                        sp.wait_ge(stores, state["stores"])

                    @block.tensor
                    def _(pe):
                        for v in range(VECS):
                            for s in range(NS):
                                n = NS * v + s
                                pe.wait_ge(dg_ready, n + 1)
                                if v:
                                    pe.wait_ge(spread_read, n - NS + 1)
                                pe.matmul(P[:, s, :], headones[:, :], dg[:, s, :, :].rearrange("p n j -> p (n j)"),
                                          start=True, stop=True).then_inc(spread, 1)

                    @block.scalar
                    def _(act):
                        act.activation(L[:, :, SEQ:T], L[:, :, SEQ:T], ACT.Exp).then_inc(dec_ready, 1)

                    @block.gpsimd
                    def _(pool):
                        pool.wait_ge(stage_in, landed)
                        pool.wait_ge(dec_ready, 1)
                        for v, x in enumerate((N_, L, A, K, R)):
                            for s in range(NS):
                                if v:
                                    pool.wait_ge(spread, NS * (v - 1) + s + 1)
                                pool.tensor_tensor(dg[:, s, :, :],
                                                   ident2[:, :].unsqueeze(1).to_broadcast([128, KC, HD]),
                                                   x[:, :, SEQ + s:SEQ + s + 1].to_broadcast([128, KC, HD]),
                                                   ALU.mult).then_inc(dg_ready, 1)

                    @block.vector
                    def _(dve):
                        step = Chain(dve, dve_step, "dve")
                        dve.wait_ge(stage_in, landed)
                        ps = lambda s: P[:, s, :].rearrange("p (n j) -> p n j", n=KC)
                        for v in range(VECS):
                            for s in range(NS):
                                dve.wait_ge(spread, NS * v + s + 1)
                                x, y = S[:, s, :, :], tmp[:, s, :, :]
                                if v == 0:
                                    step(dve.tensor_tensor(y, x, ps(s), ALU.mult))
                                    mm = dve.tensor_reduce(sa[:, s, :], y, AX.X, ALU.add, negate=True)
                                elif v == 1:
                                    mm = dve.tensor_tensor(x, x, ps(s), ALU.mult)
                                elif v < 4:
                                    by = sa[:, s, :] if v == 2 else V[:, :, SEQ + s]
                                    step(dve.tensor_tensor(y, ps(s), by.unsqueeze(2).to_broadcast([128, KC, HD]),
                                                           ALU.mult))
                                    mm = dve.tensor_tensor(x, x, y, ALU.add)
                                else:
                                    step(dve.tensor_tensor(y, x, ps(s), ALU.mult))
                                    mm = dve.tensor_reduce(sa[:, s, :], y, AX.X, ALU.add)
                                mm.then_inc(spread_read, 1)
                                dve.wait_ge(spread_read, NS * v + s + 1)
                            if v == 3:
                                dve.sem_inc(out_ready, 1)
                        step(dve.tensor_copy(L[:, :, SEQ:T].rearrange("p n s -> p s n"), sa[:, :, :]))

        def output(R, K, V, O, B, tg):
            with ExitStack() as ctx:
                g2 = sb(ctx, "g2", [128, D])
                q = sb(ctx, "q", [128, 2, T])
                rs = sb(ctx, "rs", [128, T])
                n_ready = sem("n_ready")
                n_done = sem("n_done")
                n_read = sem("n_read")
                n_var = sem("n_var")
                n_root = sem("n_root")
                state["stage"] += 16
                landed = state["stage"]
                with nc.Block(no_gpsimd_drain=True) as block:
                    @block.sync
                    def _(sp):
                        sp.dma_start(g2[:, :], a["rwkv_g2"]).then_inc(stage_in, 16)

                    @block.tensor
                    def _(pe):
                        pe.wait_ge(stage_in, landed)
                        for m in range(KC):
                            if m:
                                pe.wait_ge(n_read, m)
                            for j, (w, x) in enumerate(((headones[:, :], O[:, m, :]), (headones[:, :], q[:, 1, :]),
                                                        (g2[:, m * 128:(m + 1) * 128], tg[:, :]),
                                                        (headones[:, :], q[:, 0, :]))):
                                if j in (0, 3):
                                    pe.wait_ge(n_ready, 2 * m + j // 3 + 1)
                                for hf in range(2):
                                    mm = pe.matmul(P[:, 2 * j + hf, 0:HT], w, x[:, hf * HT:(hf + 1) * HT],
                                                   start=True, stop=True)
                                if j >= 2:
                                    mm.then_inc(n_done, 1)

                    @block.scalar
                    def _(act):
                        for m in range(KC):
                            act.wait_ge(n_var, m + 1)
                            act.activation(rs[:, :], rs[:, :], ACT.Sqrt).then_inc(n_root, 1)

                    @block.vector
                    def _(dve):
                        step = Chain(dve, dve_step, "dve")
                        sums = lambda j: P[:, 2 * j:2 * j + 2, 0:HT]
                        col = lambda c, m: vec[:, c + m:c + m + 1]
                        for m in range(KC):
                            x = O[:, m, :]
                            step(dve.tensor_tensor(q[:, 1, :], R[:, m, :], K[:, m, :], ALU.mult))
                            dve.tensor_scalar(q[:, 1, :], q[:, 1, :], col(V_RK, m), None, ALU.mult).then_inc(n_ready, 1)
                            dve.wait_ge(n_done, 2 * m + 1)
                            step(dve.scalar_tensor_tensor(out=halves(x), in0=sums(0), scalar=-1.0 / HD, in1=halves(x),
                                                          op0=ALU.mult, op1=ALU.add))
                            dve.tensor_tensor(q[:, 0, :], x, x, ALU.mult).then_inc(n_ready, 1)
                            step(dve.tensor_tensor(halves(q[:, 1, :]), halves(V[:, m, :]), sums(1), ALU.mult))
                            dve.wait_ge(n_done, 2 * m + 2)
                            step(dve.tensor_scalar(halves(rs[:, :]), sums(3), 1.0 / HD, 64e-5, ALU.mult, ALU.add))
                            dve.reciprocal(rs[:, :], rs[:, :]).then_inc(n_var, 1)
                            dve.wait_ge(n_root, m + 1)
                            step(dve.scalar_tensor_tensor(out=x, in0=x, scalar=col(V_LNW, m), in1=rs[:, :],
                                                          op0=ALU.mult, op1=ALU.mult))
                            step(dve.scalar_tensor_tensor(out=x, in0=x, scalar=col(V_LNB, m), in1=q[:, 1, :],
                                                          op0=ALU.add, op1=ALU.add))
                            dve.tensor_tensor(halves(R[:, m, :]), halves(x), sums(2), ALU.mult).then_inc(n_read, 1)
                            dve.wait_ge(n_read, m + 1)

        with nc.Block(no_gpsimd_drain=True) as block:
            @block.sync
            def _(sp):
                sp.dma_start(h[:, :, :], a["x"]).then_inc(fixed_in, 16)
                sp.dma_start(vec[:, :], a["vec"]).then_inc(fixed_in, 16)
                sp.dma_start(ones[:, :], a["ones"]).then_inc(fixed_in, 16)
                sp.dma_start(ident[:, :], a["ident"]).then_inc(fixed_in, 16)
                sp.dma_start(headones[:, :], a["headones"]).then_inc(fixed_in, 16)
                stream_weights(sp, RING)
                sp.wait_ge(fixed_in, 80)

        layer0()
        tail(0, U_T0)
        layer1()
        tail(1, U_T1)
        with nc.Block(no_gpsimd_drain=True) as block:
            @block.sync
            def _(sp):
                sp.dma_start(o["y"], h[:, :, :]).then_inc(stores, 16)
                state["stores"] += 16
                sp.wait_ge(stores, state["stores"])


def kernel(**inputs):
    import concourse.bacc as bacc
    from concourse.bass_utils import run_bass_kernel_spmd as run

    x = {k: np.asarray(v) for k, v in inputs.items()}
    fm = lambda v: np.ascontiguousarray(v.reshape(v.shape[0], -1, 128).transpose(2, 1, 0))
    cols = lambda v: v.reshape(-1, 128).T

    def unit_in(w):
        return w.reshape(KC, 128, -1, 256).transpose(2, 1, 0, 3).reshape(-1, 128, UW)

    def unit_down(w):
        return w.reshape(2, 2, KC, 128, 4, 256).transpose(0, 4, 1, 3, 2, 5).reshape(2, 8, 128, UW)

    def unit_ple(w):
        return w.reshape(2, 128, D).transpose(1, 0, 2).reshape(1, 128, UW)

    order = [(2 * gp + g2) * REP + r for gp in range(2) for r in range(REP) for g2 in range(2)]
    w_in = x["even_w_in"][0]
    wq = w_in[:, 256:1024].reshape(D, HEADS, HD)[:, order].reshape(D, 768)
    w_big = np.concatenate([w_in[:, :256], wq, w_in[:, 1024:2560]], 1)
    w_out = x["even_w_out"][0]
    w_out = np.concatenate([w_out[:256], w_out[256:].reshape(HEADS, HD, D)[order].reshape(768, D)], 0)
    units = [unit_in(w_big), unit_in(w_out)]
    for l in range(2):
        if l == 1:
            units += [unit_in(x[n][0]) for n in ("rwkv_wr", "rwkv_wk", "rwkv_wv", "rwkv_wo")]
        up, down = unit_in(x["mlp_w1"][l]).reshape(2, 8, 128, UW), unit_down(x["mlp_w2"][l])
        units += [up[0], down[0], up[1], down[1], unit_in(x["ple_gate"][l]),
                  unit_ple(x["ple_proj"][l])]

    kg = x["k_gain"][0]
    two = lambda v: np.concatenate([v, v])[:, None]
    vec = np.concatenate(
        [cols(x["norm_mix"]), cols(x["norm_mlp"]), cols(x["norm_ple"]), cols(x["rwkv_mu"])]
        + [cols(x["rwkv_" + n]) for n in ("w0", "a0", "kk", "ka", "rk", "lnw", "lnb")]
        + [cols(x["pool_scale"]), two(x["q_gain"][0]), two(kg[0]), two(kg[1]), two(kg[2])], 1)

    def block_diag(m):
        a_, b_ = m
        z = np.zeros(a_.shape[:-2] + (128, 128), np.float32)
        z[..., :64, :64], z[..., 64:, 64:] = a_, b_
        return z

    cw = x["cmp_w"][0]
    pw = x["pool_w"][0]
    ck, cv = x["cache_k"][0], x["cache_v"][0]
    fmc = lambda c: c.reshape(-1, PAGE, 2, 2, HD).transpose(0, 3, 4, 2, 1).reshape(-1, 128, 2, PAGE)
    ws = x["state_win_v"][0].reshape(NS, WIN // 128, 128, 256).transpose(0, 2, 1, 3)
    wk = x["state_win_k"][0].reshape(NS, WIN, 2, 2, HD).transpose(0, 3, 4, 2, 1).reshape(NS, 128, 2, WIN)
    small = lambda w: w.reshape(KC, 128, -1).transpose(1, 0, 2)
    d = {
        "x": fm(np.concatenate([x["x_prompt"][0], x["x_sample"][:, 0]], 0)),
        "p": np.stack([fm(np.concatenate([x["p_prompt"][l, 0], x["p_sample"][l, :, 0]], 0)) for l in range(2)]),
        "weights": np.concatenate(units, 0),
        "vec": vec,
        "wgl": small(w_in[:, 2560:]),
        "state_pool": x["state_pool"][0].reshape(NS, 15, 2, 128).transpose(3, 2, 0, 1),
        "pool_w": block_diag((pw[0::2], pw[1::2])).transpose(1, 0, 2),
        "cmp_w": block_diag((cw, cw)).transpose(2, 0, 1, 3),
        "cmp_pe": np.concatenate([x["cmp_pe"][0].transpose(2, 0, 1)] * 2, 0),
        "page_table": x["page_table"].reshape(1, -1),
        "rows": np.concatenate([fmc(ck[:, :, 0]), fmc(cv[:, :, 0]), fmc(ck[:, :, 1])], 2),
        "cv_slc": cv[:, :, 1].reshape(-1, PAGE, 256),
        "win_k": wk, "win_v": ws,
        "state_shift": fm(x["state_shift"][0]),
        "rwkv_w1": small(x["rwkv_w1"][0]), "rwkv_a1": small(x["rwkv_a1"][0]), "rwkv_g1": small(x["rwkv_g1"][0]),
        "rwkv_w2": x["rwkv_w2"][0], "rwkv_a2": x["rwkv_a2"][0], "rwkv_g2": x["rwkv_g2"][0],
        "state_wkv": x["state_wkv"][0].reshape(NS, KC, 2, HD, HD).transpose(2, 3, 0, 1, 4).reshape(128, NS, KC, HD),
    }
    d.update(constants())
    outs = {
        "y": (128, KC, T), "kv": (128, 12, T), "pool_p": (128, 2, 15), "pool_s": (128, 2, NS, 15),
        "win_k": (NS, 128, 2, WIN), "win_v": (NS, 128, WIN // 128, 256), "shift": (128, KC, NS + 1),
        "wkv_p": (128, KC, HD), "wkv_s": (128, NS, KC, HD),
    }
    nc = bacc.Bacc("TRN2", target_bir_lowering=False, num_devices=1)
    d = {"in_" + k: np.ascontiguousarray(v) for k, v in d.items()}
    ins = {k[3:]: nc.dram_tensor(k, v.shape, mybir.dt.from_np(v.dtype), kind="ExternalInput").ap() for k, v in d.items()}
    res = {k: nc.dram_tensor("out_" + k, s, F32, kind="ExternalOutput").ap() for k, s in outs.items()}
    build(nc, ins, res)
    r = run(nc, [d], core_ids=[0]).results[0]
    r = {k: np.asarray(r["out_" + k]) for k in outs}

    rows = lambda v: v.transpose(2, 1, 0).reshape(v.shape[2], -1)
    y = rows(r["y"])
    kv = r["kv"].reshape(2, HD, 6, 2, T).transpose(4, 2, 3, 0, 1).reshape(T, 6, GROUPS, HD)
    pair = lambda b, c, s: np.stack([kv[s, b], kv[s, c]], 1)
    pr, sa = slice(0, SEQ), slice(SEQ, T)
    wko = r["win_k"].reshape(NS, 2, HD, 2, WIN).transpose(0, 4, 3, 1, 2).reshape(NS, WIN, GROUPS, HD)
    wvo = r["win_v"].transpose(0, 2, 1, 3).reshape(NS, WIN, GROUPS, HD)
    shift = rows(r["shift"])
    return (
        y[None, :SEQ], y[SEQ:, None],
        pair(0, 2, pr)[None, None], pair(1, 3, pr)[None, None],
        pair(0, 2, sa)[None, :, None], pair(1, 3, sa)[None, :, None],
        kv[None, None, :SEQ, 4], kv[None, None, :SEQ, 5],
        np.concatenate([wko[:, 1:], kv[SEQ:, None, 4]], 1)[None], np.concatenate([wvo[:, 1:], kv[SEQ:, None, 5]], 1)[None],
        rows(r["pool_p"])[None, None], r["pool_s"].transpose(2, 3, 1, 0).reshape(1, NS, 15, 256),
        shift[None, :1], shift[None, 1:],
        r["wkv_p"].reshape(2, HD, KC, HD).transpose(2, 0, 1, 3).reshape(1, 1, RH, HD, HD),
        r["wkv_s"].reshape(2, HD, NS, KC, HD).transpose(2, 3, 0, 1, 4).reshape(1, NS, RH, HD, HD),
    )
```

```python
import math
from contextlib import ExitStack

import numpy as np
import concourse.bass as bass
from concourse import mybir

F32 = mybir.dt.float32
F32R = mybir.dt.float32r
I32 = mybir.dt.int32
ALU = mybir.AluOpType
ACT = mybir.ActivationFunctionType
AX = mybir.AxisListType

D, SEQ, NS, PAST, PAGE = 1024, 512, 8, 1024, 128
T = SEQ + NS
HT = T // 2
KC = D // 128
HD, HEADS, GROUPS, REP = 64, 12, 4, 3
NQ = SEQ // 128
PAGES = PAST // PAGE
WIN = 512
CL, CS = 32, 16
NC_P = SEQ // CS - 1
NC_S = PAST // CS - 1
UW = 2048
RING = 4
HROWS = 20
FF = 4 * D
RH = 16
CH = 64
NCH = SEQ // CH
EPS = 1e-6
NEG = -1e30

V_MIX, V_MLP, V_PLE, V_MU = 0, 16, 32, 48
V_W0, V_A0, V_KK, V_KA, V_RK, V_LNW, V_LNB = (96 + 8 * i for i in range(7))
V_PS, V_QG, V_KG = 152, 154, 155
NV = 158

C_SLC, C_NSLC, C_WIN, C_NWIN, C_CMP = 0, 1024, 1032, 1544, 1552
NCOL = C_CMP + NC_S

U_IN, U_OUT, U_T0 = 0, 10, 14
TAIL = 16 + 16 + 4 + 1
U_R = U_T0 + TAIL
U_WO = U_R + 12
U_T1 = U_WO + 4
NU = U_T1 + TAIL


def slopes():
    s = [2.0 ** (-8.0 * (i + 1) / 8) for i in range(8)]
    s += [2.0 ** (-8.0 * (i + 1) / 16) for i in range(0, 16, 2)][:4]
    return np.asarray(s, np.float32)


SLOPE = slopes()


def constants():
    c = {}
    c["ident"] = np.eye(128, dtype=np.float32)
    c["ones"] = np.ones((128, 128), np.float32)
    to_rows = (2 * np.arange(10)[None, :, None] + np.arange(128)[:, None, None] // 64
               == np.arange(HROWS)[None, None, :]).astype(np.float32)
    c["to_rows"] = to_rows
    c["from_rows"] = to_rows.transpose(2, 1, 0).copy()
    c["headones"] = np.kron(np.eye(2), np.ones((64, 64))).astype(np.float32)
    p = np.arange(128)[:, None]
    x = np.arange(512)[None, :] - 384 - p
    c["dist"] = np.where(x > 0, NEG, x).astype(np.float32)
    t = (np.arange(NQ)[None, :] * 128 + p)[:, :, None, None]
    j = np.arange(32)[None, None, None, :]
    heads = np.array([(2 * gp + g2) * REP + r for gp in range(2) for r in range(REP) for g2 in range(2)])
    dd = t - (CS * j + CL - 1)
    ok = (dd >= 0) & (j < NC_P)
    c["cmpbias"] = np.where(ok, -SLOPE[heads][None, None, :, None] * dd, NEG).astype(np.float32)
    c["cmpok"] = np.broadcast_to(ok, (128, NQ, 1, 32)).astype(np.float32).copy()
    ic = np.zeros((128, 2, SEQ), np.float32)
    for gi, w in enumerate((2, 4, 8, 16)):
        ic[(gi % 2) * 64:(gi % 2) * 64 + 64, gi // 2] = 1.0 / np.minimum(w, np.arange(SEQ) + 1)
    c["invcnt"] = ic
    row = np.arange(128)
    g, s, r = row // 32, (row % 32) // 3, row % 32 % 3
    live = s < NS
    sl = np.where(live, SLOPE[g * REP + r], 0.0)[:, None]
    same = (np.arange(NS)[None, :] == s[:, None])
    b = np.zeros((128, NCOL), np.float32)
    b[:, C_SLC:C_NSLC] = -sl * (PAST - np.arange(PAST))[None, :]
    dw = WIN - np.arange(WIN)
    b[:, C_WIN:C_NWIN] = np.where((dw < WIN)[None, :], -sl * dw[None, :], NEG)
    b[:, C_NSLC:C_WIN] = np.where(same | ~live[:, None], 0, NEG)
    b[:, C_NWIN:C_CMP] = np.where(same | ~live[:, None], 0, NEG)
    b[:, C_CMP:] = -sl * (PAST - (CS * np.arange(NC_S) + CL - 1))[None, :]
    c["sbias"] = b
    c["samegs"] = ((g[:, None] == g[None, :]) & (s[:, None] == s[None, :])).astype(np.float32)
    c["own_sample"] = (s[None, :] == np.arange(NS)[:, None]).astype(np.float32)
    c["own_head"] = ((g * REP + r)[:, None] == np.arange(HEADS)[None, :]).astype(np.float32) * live[:, None]
    c["blockno"] = np.broadcast_to(np.arange(1, 15, dtype=np.float32), (128, 14)).copy()
    ss, tt = np.arange(CH)[:, None], np.arange(CH)[None, :]
    m = np.concatenate([ss < tt, ss <= tt], 1).astype(np.float32)
    c["tri"] = np.concatenate([m, m], 0)
    lv = []
    for n in range(6):
        w = 1 << n
        lv.append((tt // w % 2 == 1) & (ss // w == tt // w - 1))
    lv = np.stack(lv, 1).astype(np.float32)
    c["level"] = np.concatenate([lv, lv], 0)
    e = np.eye(64, dtype=np.float32)
    c["ident2"] = np.concatenate([e, e], 0)
    rs = np.ones((128, KC, CH + 1), np.float32)
    rs[:, :, 0] = 0
    c["restart"] = rs
    return c


def build(nc, a, o):
    with ExitStack() as top:
        sb = lambda ctx, name, shape, dt=F32: ctx.enter_context(nc.sbuf_tensor(name, shape, dt))
        sem = lambda name: top.enter_context(nc.semaphore(name))
        P = top.enter_context(nc.psum_tensor("P", [128, 8, 512], F32))
        h = sb(top, "h", [128, KC, T])
        vec = sb(top, "vec", [128, NV])
        ring = sb(top, "ring", [128, RING, UW])
        ident = sb(top, "ident", [128, 128])
        ones = sb(top, "ones", [128, 128])
        headones = sb(top, "headones", [128, 128])
        rstd = sb(top, "rstd", [128, T])

        fixed_in = sem("fixed_in")
        stage_in = sem("stage_in")
        weight_in = [sem(f"weight_in{i}") for i in range(RING)]
        stores = sem("stores")
        whead_ready = sem("whead_ready")
        wsplit_ready = sem("wsplit_ready")
        xhead_ready = sem("xhead_ready")
        xsplit_ready = sem("xsplit_ready")
        tile_done = sem("tile_done")
        tile_free = sem("tile_free")
        half_used = sem("half_used")
        sq_ready = sem("sq_ready")
        ssum_ready = sem("ssum_ready")
        rvar_ready = sem("rvar_ready")
        rstd_ready = sem("rstd_ready")
        xn_ready = sem("xn_ready")
        dve_step = sem("dve_step")
        act_step = sem("act_step")
        state = {"split": 0, "unit": 0, "tile": 0, "norm": 0, "stage": 0, "stores": 0, "half": 0}
        used_up = {}

        class Chain:
            def __init__(self, eng, s, key):
                self.eng, self.sem, self.key = eng, s, key
                state.setdefault(key, 0)

            def __call__(self, ins):
                state[self.key] += 1
                ins.then_inc(self.sem, 1)
                self.eng.wait_ge(self.sem, state[self.key])

        halves = lambda ap: ap.rearrange("p (a b) -> p a b", a=2)

        def stream_weights(sp, upto):
            upto = min(upto, NU)
            for u in range(state["unit"], upto):
                if u >= RING:
                    sp.wait_ge(wsplit_ready, u - RING + 1)
                sp.dma_start(ring[:, u % RING, :], a["weights"][u]).then_inc(weight_in[u % RING], 16)
            state["unit"] = max(upto, state["unit"])

        def plan(units, per_group=1, times=1):
            first = state["tile"]
            n = first
            for g in range(0, len(units), per_group):
                n += 2 * times
                for u in units[g:g + per_group - 1]:
                    state["half"] += 1
                    used_up[u] = half_used, state["half"]
                used_up[units[g + per_group - 1]] = tile_done, n
            state["tile"] = n
            return first

        def dense(pe, first, units, ws, x, nk=KC, cols=256, per_group=1, times=1, chunk_ready=None):
            xh, xl = x
            n = first
            for g in range(0, len(units), per_group):
                for rep in range(times):
                    if n >= 4:
                        pe.wait_ge(tile_free, n - 2)
                    for i, u in enumerate(units[g:g + per_group]):
                        pe.wait_ge(wsplit_ready, u + 1)
                        for m in range(2):
                            for k in range(nk):
                                if chunk_ready and m == 0 and rep == 0:
                                    chunk_ready(i * nk + k)
                                c = slice(k * cols + (2 * rep + m) * 128, k * cols + (2 * rep + m + 1) * 128)
                                wh, wl = ws[:, u % 2, 0, c], ws[:, u % 2, 1, c]
                                first_k, last_k = i == 0 and k == 0, i == per_group - 1 and k == nk - 1
                                for w, xs in ((wh, xh), (wh, xl), (wl, xh)):
                                    for hf in range(2):
                                        mm = pe.matmul(P[:, n // 2 % 2 * 4 + 2 * m + hf, 0:HT], w,
                                                       xs[:, i * nk + k, hf * HT:(hf + 1) * HT],
                                                       start=first_k and w is wh and xs is xh,
                                                       stop=last_k and w is wl)
                            if i == per_group - 1:
                                mm.then_inc(tile_done, 1)
                        if i < per_group - 1:
                            mm.then_inc(half_used, 1)
                    n += 2

        def weight_head(act, u, units, ws):
            if u >= units[-1] + 1:
                return
            act.wait_ge(weight_in[u % RING], 16 * (u // RING + 1))
            if u >= units[0] + 2:
                act.wait_ge(*used_up[u - 2])
            act.activation(ws[:, u % 2, 0, :], ring[:, u % RING, :], ACT.Copy).then_inc(whead_ready, 1)

        def weight_rests(pool, units, ws):
            for u in units:
                pool.wait_ge(whead_ready, u + 1)
                pool.tensor_tensor(ws[:, u % 2, 1, :], ring[:, u % RING, :], ws[:, u % 2, 0, :].bitcast(F32),
                                   ALU.subtract).then_inc(wsplit_ready, 1)

        def take_splits(n):
            state["split"] += n
            return state["split"] - n

        def split_head(act, src, dst):
            act.activation(dst, src, ACT.Copy).then_inc(xhead_ready, 1)

        def split_rest(dve, n, src, xh, dst):
            dve.wait_ge(xhead_ready, n + 1)
            dve.tensor_tensor(dst, src, xh.bitcast(F32), ALU.subtract).then_inc(xsplit_ready, 1)

        def tile(n):
            b = n // 2 % 2 * 4 + n % 2 * 2
            return P[:, b:b + 2, 0:HT]

        def norm_act(act, i, dst, halves_of=None, units=None, ws=None):
            for k in range(KC):
                act.activation(dst[:, k, :], h[:, k, :], ACT.Square).then_inc(sq_ready, 1)
            if units:
                for u in units[0:2]:
                    weight_head(act, u, units, ws)
            act.wait_ge(rvar_ready, i + 1)
            act.activation(rstd[:, :], rstd[:, :], ACT.Sqrt).then_inc(rstd_ready, 1)
            if halves_of:
                for k in range(KC):
                    act.wait_ge(xn_ready, i * KC + k + 1)
                    split_head(act, dst[:, k, :], halves_of[0][:, k, :])

        def norm_pe(pe, i, dst):
            for k in range(KC):
                pe.wait_ge(sq_ready, i * KC + k + 1)
                for hf in range(2):
                    mm = pe.matmul(P[:, 6 + hf, 0:HT], ones[:, :], dst[:, k, hf * HT:(hf + 1) * HT],
                                   start=k == 0, stop=k == KC - 1)
            mm.then_inc(ssum_ready, 1)

        def norm_dve(dve, step, i, dst, col, halves_of=None, n=0):
            dve.wait_ge(ssum_ready, i + 1)
            step(dve.tensor_scalar(halves(rstd[:, :]), P[:, 6:8, 0:HT], 1.0 / D, EPS, ALU.mult, ALU.add))
            dve.reciprocal(rstd[:, :], rstd[:, :]).then_inc(rvar_ready, 1)
            dve.wait_ge(rstd_ready, i + 1)
            for k in range(KC):
                dve.scalar_tensor_tensor(out=dst[:, k, :], in0=h[:, k, :], scalar=vec[:, col + k:col + k + 1],
                                         in1=rstd[:, :], op0=ALU.mult, op1=ALU.mult).then_inc(xn_ready, 1)
                if halves_of and k >= 2:
                    split_rest(dve, n + k - 2, dst[:, k - 2, :], halves_of[0][:, k - 2, :], halves_of[1][:, k - 2, :])
            for k in range(KC - 2, KC):
                if halves_of:
                    split_rest(dve, n + k, dst[:, k, :], halves_of[0][:, k, :], halves_of[1][:, k, :])

        def tail(layer, u0):
            HC = FF // 128 // 2
            with ExitStack() as ctx:
                ws = sb(ctx, f"ws_t{layer}", [128, 2, 2, UW], F32R)
                u = [sb(ctx, f"u{n}{layer}", [128, KC, T], F32R) for n in "hl"]
                hid = [sb(ctx, f"hid{n}{layer}", [128, HC, T], F32R) for n in "hl"]
                full = sb(ctx, f"full{layer}", [128, KC, T])
                act_ = sb(ctx, f"act{layer}", [128, 2, T])
                sqr = sb(ctx, f"sqr{layer}", [128, 2, T])
                pl, pls = full[:, 0:2, :], [x[:, 0:2, :] for x in hid]
                sq_done = sem(f"hid_squared{layer}")
                block = ctx.enter_context(nc.Block(no_gpsimd_drain=True))
                halves_ = []
                for b in range(2):
                    up = list(range(u0 + 16 * b, u0 + 16 * b + 8))
                    down = list(range(u0 + 16 * b + 8, u0 + 16 * b + 16))
                    halves_.append((up, plan(up), down, plan(down, per_group=2)))
                gate, proj = list(range(u0 + 32, u0 + 36)), [u0 + 36]
                t_gate = plan(gate)
                t_proj = plan(proj, times=4)
                n1 = state["norm"]
                n2 = n1 + 1
                state["norm"] += 2
                state["stage"] += 16
                landed = state["stage"]
                x_1 = take_splits(KC)
                x_hid = [take_splits(HC) for _ in range(2)]
                x_pl = take_splits(2)
                x_2 = take_splits(KC)
                ready = lambda pe, n: (lambda k: pe.wait_ge(xsplit_ready, n + k + 1))

                @block.sync
                def _(sp):
                    stream_weights(sp, u0 + 16)
                    sp.wait_ge(xsplit_ready, x_1 + KC)
                    sp.dma_start(pl, a["p"][layer]).then_inc(stage_in, 16)
                    stream_weights(sp, u0 + TAIL + RING)

                @block.gpsimd
                def _(pool):
                    weight_rests(pool, range(u0, u0 + TAIL), ws)

                @block.tensor
                def _(pe):
                    norm_pe(pe, n1, full)
                    for b, (up, t_up, down, t_down) in enumerate(halves_):
                        dense(pe, t_up, up, ws, u, chunk_ready=ready(pe, x_1))
                        dense(pe, t_down, down, ws, hid, per_group=2, chunk_ready=ready(pe, x_hid[b]))
                    pe.wait_ge(tile_free, t_gate)
                    norm_pe(pe, n2, full)
                    dense(pe, t_gate, gate, ws, u, chunk_ready=ready(pe, x_2))
                    dense(pe, t_proj, proj, ws, pls, nk=2, cols=D, times=4, chunk_ready=ready(pe, x_pl))

                @block.scalar
                def _(act):
                    units = range(u0, u0 + TAIL)
                    norm_act(act, n1, full, u, units, ws)
                    for b, (up, t_up, down, t_down) in enumerate(halves_):
                        for m in range(HC + 1):
                            if m < HC:
                                if m >= 2 or b:
                                    act.wait_ge(sq_done, HC * b + m - 1)
                                act.wait_ge(tile_done, t_up + m + 1)
                                act.activation(halves(act_[:, m % 2, :]), tile(t_up + m), ACT.Relu)\
                                   .then_inc(tile_free, 1)
                            if m:
                                act.wait_ge(sq_done, HC * b + m)
                                split_head(act, sqr[:, (m - 1) % 2, :], hid[0][:, m - 1, :])
                            if m % 2 and m < HC:
                                weight_head(act, up[m // 2] + 2, units, ws)
                        for d in down:
                            weight_head(act, d + 2, units, ws)
                        if b == 0:
                            act.wait_ge(tile_free, t_down + KC)
                    act.wait_ge(stage_in, landed)
                    act.wait_ge(tile_free, t_gate)
                    for k in range(2):
                        split_head(act, pl[:, k, :], pls[0][:, k, :])
                    act.wait_ge(xsplit_ready, x_pl + 2)
                    norm_act(act, n2, full, u)
                    act.wait_ge(xsplit_ready, x_2 + KC)
                    for m in range(KC):
                        act.wait_ge(tile_done, t_gate + m + 1)
                        act.activation(halves(full[:, m, :]), tile(t_gate + m), ACT.Sigmoid).then_inc(tile_free, 1)
                        if m % 2:
                            weight_head(act, gate[m // 2] + 2, units, ws)

                @block.vector
                def _(dve):
                    step = Chain(dve, dve_step, "dve")
                    norm_dve(dve, step, n1, full, V_MLP + KC * layer, u, x_1)
                    for b, (up, t_up, down, t_down) in enumerate(halves_):
                        for m in range(HC + 2):
                            if m < HC:
                                dve.wait_ge(tile_free, t_up + m + 1)
                                if m >= 2:
                                    dve.wait_ge(xsplit_ready, x_hid[b] + m - 1)
                                dve.tensor_tensor(sqr[:, m % 2, :], act_[:, m % 2, :], act_[:, m % 2, :], ALU.mult)\
                                   .then_inc(sq_done, 1)
                            if m >= 1 and m <= HC:
                                split_rest(dve, x_hid[b] + m - 1, sqr[:, (m - 1) % 2, :], hid[0][:, m - 1, :],
                                           hid[1][:, m - 1, :])
                        for m in range(KC):
                            dve.wait_ge(tile_done, t_down + m + 1)
                            hv = halves(h[:, m, :])
                            dve.tensor_tensor(hv, hv, tile(t_down + m), ALU.add).then_inc(tile_free, 1)
                    for k in range(2):
                        split_rest(dve, x_pl + k, pl[:, k, :], pls[0][:, k, :], pls[1][:, k, :])
                    norm_dve(dve, step, n2, full, V_PLE + KC * layer, u, x_2)
                    dve.wait_ge(tile_free, t_proj)
                    for m in range(KC):
                        dve.wait_ge(tile_done, t_proj + m + 1)
                        gv = halves(full[:, m, :])
                        dve.tensor_tensor(gv, gv, tile(t_proj + m), ALU.mult).then_inc(tile_free, 1)
                        dve.wait_ge(tile_free, t_proj + m + 1)
                        step(dve.tensor_tensor(h[:, m, :], h[:, m, :], full[:, m, :], ALU.add))

        def layer0():
            with ExitStack() as c0:
                xn = sb(c0, "xn0", [128, KC, T])
                Z = sb(c0, "Z", [128, 20, T])
                gates = sb(c0, "gates", [128, NQ + 1, 3 * HEADS])
                Vt = sb(c0, "Vt", [128, 2, NQ, 256])
                Vn = sb(c0, "Vn", [NS, 2, 256])
                VCp = sb(c0, "VCp", [128, 256])
                KCb = sb(c0, "KCb", [128, NS + 1, 2, NC_S])
                KB = lambda b, gp: 8 + 2 * b + gp
                pages = sb(c0, "pages", [1, NS * PAGES], I32)
                rows_in = [sem(f"rows_in{i}") for i in range(2)]
                ring_rows = ring[:, 1:RING, :].rearrange("p r (g c) -> p r g c", g=2)
                spare = xn[:, 2:KC, :].rearrange("p k t -> p (k t)")

                def load_rows(sp, s, raw, kwin):
                    for n in range(PAGES):
                        page = sp.value_load(pages[0:1, s * PAGES + n:s * PAGES + n + 1], min_val=0,
                                             max_val=a["rows"].shape[0] - 1)
                        sp.dma_start(raw[:, :, :, n * PAGE:(n + 1) * PAGE].rearrange("p k g c -> p (k g) c"),
                                     a["rows"][bass.ds(page, 1)].rearrange("o p k c -> p (o k) c"))\
                          .then_inc(rows_in[s % 2], 16)
                    for g in range(2):
                        sp.dma_start(kwin[g], a["win_k"][s][:, g, :]).then_inc(rows_in[s % 2], 16)

                project_in(xn, Z, gates)
                pool_and_values(xn, Z, Vt, Vn, pages,
                                lambda sp: load_rows(sp, 0, ring_rows, (spare[:, 0:WIN], spare[:, WIN:2 * WIN])))
                with ExitStack() as c1:
                    VCt = sb(c1, "VCt", [64, NS, 256])
                    compress_and_score(xn, Z, KCb, VCt, VCp, KB, ring_rows, rows_in, load_rows)
                    sample_attention(xn, gates, Vn, VCt, pages)
                prompt_attention(xn, Z, gates, Vt, VCp, KCb, KB)
                add_product(xn, list(range(U_OUT, U_OUT + 4)), "w_out")

        def add_product(x, units, name):
            with ExitStack() as ctx:
                ws = sb(ctx, "ws_" + name, [128, 2, 2, UW], F32R)
                xs = [sb(ctx, f"x{n}_{name}", [128, KC, T], F32R) for n in "hl"]
                first = plan(units)
                x0 = take_splits(KC)
                with nc.Block(no_gpsimd_drain=True) as block:
                    @block.sync
                    def _(sp):
                        stream_weights(sp, units[-1] + 1 + RING)

                    @block.gpsimd
                    def _(pool):
                        weight_rests(pool, units, ws)

                    @block.tensor
                    def _(pe):
                        dense(pe, first, units, ws, xs, chunk_ready=lambda k: pe.wait_ge(xsplit_ready, x0 + k + 1))

                    @block.scalar
                    def _(act):
                        weight_head(act, units[0], units, ws)
                        for k in range(KC):
                            split_head(act, x[:, k, :], xs[0][:, k, :])
                        for u in units[1:]:
                            weight_head(act, u, units, ws)

                    @block.vector
                    def _(dve):
                        for k in range(KC):
                            split_rest(dve, x0 + k, x[:, k, :], xs[0][:, k, :], xs[1][:, k, :])
                        for m in range(KC):
                            dve.wait_ge(tile_done, first + m + 1)
                            hv = halves(h[:, m, :])
                            dve.tensor_tensor(hv, hv, tile(first + m), ALU.add).then_inc(tile_free, 1)

        def project_in(xn, Z, gates):
            with ExitStack() as ctx:
                wgl = sb(ctx, "wgl", [128, KC, 3 * HEADS])
                ws = sb(ctx, "ws_in", [128, 2, 2, UW], F32R)
                xs = [sb(ctx, f"x{n}_in", [128, KC, T], F32R) for n in "hl"]
                zsq = sb(ctx, "zsq", [128, 2, T])
                zr = sb(ctx, "zr", [HROWS, T])
                to_rows = sb(ctx, "to_rows", [128, 10, HROWS])
                from_rows = sb(ctx, "from_rows", [HROWS, 10, 128])
                qg = sb(ctx, "qg", [128, 1])
                logits_ready = sem("logits_ready")
                zsq_ready = sem("zsq_ready")
                zsq_used = sem("zsq_used")
                zss_ready = sem("zss_ready")
                zvar_ready = sem("zvar_ready")
                zroot_ready = sem("zroot_ready")
                zb_done = sem("zb_done")
                zb_read = sem("zb_read")
                normed = list(range(2, 8)) + [12, 13, 16, 17]
                units = list(range(U_IN, U_IN + 10))
                first = plan(units)
                i = state["norm"]
                state["norm"] += 1
                state["stage"] += 48
                landed = state["stage"]
                last = first + 20
                x0 = take_splits(KC)

                with nc.Block(no_gpsimd_drain=True) as block:
                    @block.gpsimd
                    def _(pool):
                        weight_rests(pool, units, ws)

                    @block.sync
                    def _(sp):
                        for dst, src in ((wgl, "wgl"), (to_rows, "to_rows"), (from_rows, "from_rows")):
                            sp.dma_start(dst[:, :, :], a[src]).then_inc(stage_in, 16)
                        stream_weights(sp, U_OUT)

                    @block.tensor
                    def _(pe):
                        norm_pe(pe, i, xn)
                        dense(pe, first, units, ws, xs, chunk_ready=lambda k: pe.wait_ge(xsplit_ready, x0 + k + 1))
                        pe.wait_ge(stage_in, landed)
                        pe.wait_ge(tile_free, last)
                        for t in range(NQ + 1):
                            n = 128 if t < NQ else NS
                            for k in range(KC):
                                mm = pe.matmul(P[0:n, 0, t * 36:t * 36 + 36], xn[:, k, t * 128:t * 128 + n],
                                               wgl[:, k, :], start=k == 0, stop=k == KC - 1)
                        mm.then_inc(logits_ready, 1)
                        for j in range(len(normed)):
                            pe.wait_ge(zsq_ready, j + 1)
                            for hf in range(2):
                                mm = pe.matmul(P[0:HROWS, 4 + hf, 0:HT], to_rows[:, j, :],
                                               zsq[:, j % 2, hf * HT:(hf + 1) * HT], start=j == 0,
                                               stop=j == len(normed) - 1)
                            mm.then_inc(zsq_used, 1)
                        pe.wait_ge(zsq_used, len(normed))
                        pe.sem_inc(zss_ready, 1)
                        pe.wait_ge(zroot_ready, 1)
                        for j in range(len(normed)):
                            if j >= 2:
                                pe.wait_ge(zb_read, j - 1)
                            for hf in range(2):
                                mm = pe.matmul(P[:, (6, 2)[j % 2] + hf, 0:HT], from_rows[:, j, :],
                                               zr[:, hf * HT:(hf + 1) * HT], start=True, stop=True)
                            mm.then_inc(zb_done, 1)

                    @block.scalar
                    def _(act):
                        step = Chain(act, act_step, "act")
                        norm_act(act, i, xn, xs, units, ws)
                        for m in range(20):
                            act.wait_ge(tile_done, first + m + 1)
                            act.activation(halves(Z[:, m, :]), tile(first + m), ACT.Copy).then_inc(tile_free, 1)
                            if m % 2:
                                weight_head(act, units[m // 2] + 2, units, ws)
                        act.wait_ge(logits_ready, 1)
                        act.activation(gates[:, 0:NQ, :], P[:, 0, 0:NQ * 36].rearrange("p (t c) -> p t c", t=NQ),
                                       ACT.Sigmoid)
                        step(act.activation(gates[0:NS, NQ, :], P[0:NS, 0, NQ * 36:NQ * 36 + 36], ACT.Sigmoid))
                        act.wait_ge(tile_free, last)
                        for j, c in enumerate(normed):
                            if j >= 2:
                                act.wait_ge(zsq_used, j - 1)
                            act.activation(zsq[:, j % 2, :], Z[:, c, :], ACT.Square).then_inc(zsq_ready, 1)
                        act.wait_ge(zvar_ready, 1)
                        act.activation(zr[:, :], zr[:, :], ACT.Sqrt).then_inc(zroot_ready, 1)

                    @block.vector
                    def _(dve):
                        step = Chain(dve, dve_step, "dve")
                        norm_dve(dve, step, i, xn, V_MIX, xs, x0)
                        step(dve.tensor_scalar(qg[:, :], vec[:, V_QG:V_QG + 1], HD ** -0.5, None, ALU.mult))
                        dve.wait_ge(zss_ready, 1)
                        step(dve.tensor_scalar(halves(zr[:, :]), P[0:HROWS, 4:6, 0:HT], 1.0 / HD, EPS,
                                               ALU.mult, ALU.add))
                        dve.reciprocal(zr[:, :], zr[:, :]).then_inc(zvar_ready, 1)
                        for j, c in enumerate(normed):
                            dve.wait_ge(zb_done, j + 1)
                            col = V_KG + 1 + (j - 6) // 2
                            dve.scalar_tensor_tensor(out=halves(Z[:, c, :]), in0=halves(Z[:, c, :]),
                                                     scalar=qg[:, :] if j < 6 else vec[:, col:col + 1],
                                                     in1=P[:, (6, 2)[j % 2]:(6, 2)[j % 2] + 2, 0:HT],
                                                     op0=ALU.mult, op1=ALU.mult).then_inc(zb_read, 1)

        def pool_and_values(mix, Z, Vt, Vn, pages, load_first_rows):
            with ExitStack() as ctx:
                ext = sb(ctx, "ext", [128, 2, 15 + SEQ])
                wa = sb(ctx, "wa", [128, 2, 15 + SEQ])
                wb = sb(ctx, "wb", [128, 2, 15 + SEQ])
                dev = sb(ctx, "dev", [128, 2, T])
                inv = sb(ctx, "inv", [128, 2, SEQ])
                past = sb(ctx, "past", [128, 2, NS, 15])
                newpast = sb(ctx, "newpast", [128, 2, NS, 15])
                psum_ = sb(ctx, "psum_", [128, 2, NS])
                pw = sb(ctx, "pw", [128, 2, 128])
                pages_in = sem("pages_in")
                turned = sem("turned")
                vcopied = sem("vcopied")
                dev_ready = sem("dev_ready")
                pooled = sem("pooled")
                rows_ready = sem("rows_ready")
                state["stage"] += 48
                landed = state["stage"]
                state["stores"] += 48
                W = (2, 4, 8, 16)

                with nc.Block(no_gpsimd_drain=True) as block:
                    @block.sync
                    def _(sp):
                        sp.dma_start(pages[:, :], a["page_table"]).then_inc(pages_in, 16)
                        sp.dma_start(inv[:, :, :], a["invcnt"]).then_inc(stage_in, 16)
                        sp.dma_start(past[:, :, :, :], a["state_pool"]).then_inc(stage_in, 16)
                        sp.dma_start(pw[:, :, :], a["pool_w"]).then_inc(stage_in, 16)
                        sp.dma_start(o["kv"], Z[:, 8:20, :]).then_inc(stores, 16)
                        sp.dma_start(o["pool_p"], Z[:, 0:2, SEQ - 15:SEQ]).then_inc(stores, 16)
                        sp.wait_ge(pages_in, 16)
                        load_first_rows(sp)
                        sp.wait_ge(rows_ready, 1)
                        sp.dma_start(o["pool_s"], newpast[:, :, :, :]).then_inc(stores, 16)
                        sp.wait_ge(stores, state["stores"])

                    @block.tensor
                    def _(pe):
                        for b in range(2):
                            for gp in range(2):
                                for t in range(NQ):
                                    mm = pe.transpose(P[:, 2 * b + gp, t * 128:(t + 1) * 128],
                                                      Z[:, 14 + 4 * b + gp, t * 128:(t + 1) * 128], ident[:, :])
                                mm.then_inc(turned, 1)
                        for b in range(2):
                            for gp in range(2):
                                mm = pe.transpose(P[0:NS, 4, (2 * b + gp) * 128:(2 * b + gp + 1) * 128],
                                                  Z[:, 14 + 4 * b + gp, SEQ:T], ident[:, :])
                        mm.then_inc(turned, 1)
                        pe.wait_ge(dev_ready, 1)
                        pe.wait_ge(stage_in, landed)
                        pe.wait_ge(vcopied, 5)
                        for c in range(2):
                            for hf in range(2):
                                mm = pe.matmul(P[:, (5 + hf, hf)[c], 0:HT], pw[:, c, :],
                                               dev[:, c, hf * HT:(hf + 1) * HT], start=True, stop=True)
                            mm.then_inc(pooled, 1)

                    @block.scalar
                    def _(act):
                        for b in range(2):
                            for gp in range(2):
                                act.wait_ge(turned, 2 * b + gp + 1)
                                act.activation(Vt[:, b, :, gp * 128:(gp + 1) * 128],
                                               P[:, 2 * b + gp, :].rearrange("p (t d) -> p t d", t=NQ),
                                               ACT.Copy).then_inc(vcopied, 1)
                        act.wait_ge(turned, 5)
                        act.activation(Vn[:, :, :], P[0:NS, 4, :].rearrange("p (b d) -> p b d", b=2),
                                       ACT.Copy).then_inc(vcopied, 1)

                    @block.vector
                    def _(dve):
                        step = Chain(dve, dve_step, "dve")
                        n = 15 + SEQ
                        dve.memset(ext[:, :, 0:15], 0.0)
                        step(dve.tensor_copy(ext[:, :, 15:n], Z[:, 0:2, 0:SEQ]))
                        dve.wait_ge(stage_in, landed)
                        dve.tensor_copy(newpast[:, :, :, 0:14], past[:, :, :, 1:15])
                        dve.tensor_copy(newpast[:, :, :, 14], Z[:, 0:2, SEQ:T]).then_inc(rows_ready, 1)
                        src = ext
                        for gi, w in enumerate(W):
                            dst = (wa, wb)[gi % 2]
                            step(dve.tensor_tensor(dst[:, :, w - 1:n], src[:, :, w - 1:n],
                                                   src[:, :, w // 2 - 1:n - w // 2], ALU.add))
                            c, r = gi // 2, slice(gi % 2 * 64, gi % 2 * 64 + 64)
                            step(dve.tensor_tensor(dev[r, c, 0:SEQ], dst[r, c, 15:n], inv[r, c, :], ALU.mult))
                            step(dve.tensor_reduce(psum_[r, c, :], past[r, c, :, 16 - w:15], AX.X, ALU.add))
                            src = dst
                        step(dve.tensor_tensor(dev[:, :, 0:SEQ], dev[:, :, 0:SEQ], Z[:, 0:2, 0:SEQ], ALU.subtract))
                        step(dve.tensor_tensor(psum_[:, :, :], psum_[:, :, :], Z[:, 0:2, SEQ:T], ALU.add))
                        for gi, w in enumerate(W):
                            c, r = gi // 2, slice(gi % 2 * 64, gi % 2 * 64 + 64)
                            mm = dve.scalar_tensor_tensor(out=dev[r, c, SEQ:T], in0=psum_[r, c, :], scalar=1.0 / w,
                                                          in1=Z[r, c, SEQ:T], op0=ALU.mult, op1=ALU.subtract)
                            step(mm)
                        dve.sem_inc(dev_ready, 1)
                        for c in range(2):
                            dve.wait_ge(pooled, c + 1)
                            b = (5, 0)[c]
                            step(dve.tensor_scalar(halves(mix[:, c, :]), P[:, b:b + 2, 0:HT],
                                                   vec[:, V_PS + c:V_PS + c + 1], None, ALU.mult))

        def compress_and_score(mix, Z, KCb, VCt, VCp, KB, ring_rows, rows_in, load_rows):
            with ExitStack() as ctx:
                cw = sb(ctx, "cw", [128, 2, CL, 128])
                pe_ = sb(ctx, "pe_", [128, 2, CL])
                peb = sb(ctx, "peb", [128, 2])
                raw = [ring_rows, sb(ctx, "raw", [128, 3, 2, PAST])]
                QA = sb(ctx, "QA", [128, 2, 64])
                spare = mix[:, 2:KC, :].rearrange("p k t -> p (k t)")
                kwin = [[spare[:, 0:WIN], spare[:, WIN:2 * WIN]], [spare[:, 2 * WIN:3 * WIN], rstd[:, 0:WIN]]]
                VCb = spare[:, 3 * WIN:3 * WIN + (NS + 1) * 2 * NC_S].rearrange("p (s g c) -> p s g c", s=NS + 1, g=2)
                QZ = Z[:, 0:2, :].rearrange("p k t -> p (k t)")[:, 0:1024].rearrange("p (g s c) -> p g s c", g=2, s=NS)
                cmp_done = sem("cmp_done")
                cmp_free = sem("cmp_free")
                scored = sem("scored")
                q_ready = sem("q_ready")
                peb_done = sem("peb_done")
                ksq_ready = sem("ksq_ready")
                kss_ready = sem("kss_ready")
                kvar_ready = sem("kvar_ready")
                kroot_ready = sem("kroot_ready")
                kspread = sem("kspread")
                rows_const_in = sem("rows_const_in")
                kc_ready = sem("kc_ready")
                vturned = sem("vturned")
                vct_copied = sem("vct_copied")
                state["stage"] += 32
                landed = state["stage"]
                stored = state["stores"]
                state["stores"] += 32 * NS
                NK = (NS + 1) * 2 * NC_S
                kflat = KCb[:, :, :, :].rearrange("p s g c -> p (s g c)")
                sq = raw[0][:, 0, :, :].rearrange("p g c -> p (g c)")[:, 0:NK]
                NH = 2 * NC_S
                kr = raw[0][0:HROWS, 1, 0, 0:NH]
                to_rows = raw[0][:, 2, 0, 0:10 * HROWS].rearrange("p (j r) -> p j r", j=10)
                from_rows = raw[1][0:HROWS, 1, :, :].rearrange("p g c -> p (g c)")[:, 0:1280]\
                    .rearrange("p (j f) -> p j f", j=10)

                with nc.Block(no_gpsimd_drain=True) as block:
                    @block.sync
                    def _(sp):
                        sp.dma_start(pe_[:, :, :], a["cmp_pe"]).then_inc(stage_in, 16)
                        sp.dma_start(cw[:, :, :, :], a["cmp_w"]).then_inc(stage_in, 16)
                        for s in range(1, NS + 1):
                            if s < NS:
                                if s >= 2:
                                    sp.wait_ge(cmp_done, 2 * (s - 1))
                                    sp.wait_ge(stores, stored + 32 * (s - 1))
                                load_rows(sp, s, raw[s % 2], kwin[s % 2])
                            if s >= 1:
                                v = s - 1
                                sp.wait_ge(rows_in[v % 2], 16 * (PAGES + 2) * (v // 2 + 1))
                                for g in range(2):
                                    sp.dma_start(o["win_k"][v][:, g, :], kwin[v % 2][g]).then_inc(stores, 16)
                        sp.wait_ge(cmp_done, 2 * NS)
                        sp.dma_start(to_rows, a["to_rows"]).then_inc(rows_const_in, 16)
                        sp.dma_start(from_rows, a["from_rows"]).then_inc(rows_const_in, 16)
                        sp.wait_ge(stores, state["stores"])

                    @block.tensor
                    def _(pe):
                        pe.wait_ge(q_ready, 1)
                        for s in range(NS + 1):
                            if s < NS:
                                pe.wait_ge(rows_in[s % 2], 16 * (PAGES + 2) * (s // 2 + 1))
                                for gp in range(2):
                                    kslc = raw[s % 2][:, 2, gp, :]
                                    for bank, keys in ((0, kslc[:, 0:512]), (1, kslc[:, 512:1024]),
                                                       (2, kwin[s % 2][gp])):
                                        mm = pe.matmul(P[64 * gp:64 * gp + 64, bank, :], QZ[:, gp, s, :], keys,
                                                       start=s == 0, stop=s == NS - 1)
                                mm.then_inc(scored, 1)
                                if s == 0:
                                    pe.wait_ge(stage_in, landed)
                                    for kv in range(2):
                                        for l in range(CL):
                                            mm = pe.matmul(P[:, 3, kv:kv + 1], cw[:, kv, l, :], pe_[:, kv, l:l + 1],
                                                           start=l == 0, stop=l == CL - 1)
                                    mm.then_inc(peb_done, 1)
                            for kv in range(2):
                                if s >= 2:
                                    pe.wait_ge(cmp_free, 2 * (s - 2) + kv + 1)
                                nc_, width = (NC_S, 2 * NC_S) if s < NS else (NC_P, 2 * NC_P)
                                for l in range(CL):
                                    rows = slice(l, l + CS * (nc_ - 1) + 1, CS)
                                    src = raw[s % 2][:, kv, :, rows] if s < NS else Z[:, KB(kv, 0):KB(kv, 0) + 2, rows]
                                    mm = pe.matmul(P[:, 4 + 2 * kv + s % 2, 0:width]
                                                   .rearrange("p (g c) -> p g c", g=2), cw[:, kv, l, :], src,
                                                   start=l == 0, stop=l == CL - 1)
                                mm.then_inc(cmp_done, 1)
                        pe.wait_ge(ksq_ready, 1)
                        pe.wait_ge(cmp_free, 2 * NS + 2)
                        pe.wait_ge(rows_const_in, 32)
                        for s in range(NS + 1):
                            mm = pe.matmul(P[0:HROWS, 4, 0:NH], to_rows[:, s, :], sq[:, s * NH:(s + 1) * NH],
                                           start=s == 0, stop=s == NS)
                        mm.then_inc(kss_ready, 1)
                        pe.wait_ge(kroot_ready, 1)
                        for s in range(NS + 1):
                            mm = pe.matmul(P[:, 5 + s // 3, s % 3 * NH:(s % 3 + 1) * NH], from_rows[:, s, :], kr,
                                           start=True, stop=True)
                        mm.then_inc(kspread, 1)
                        pe.wait_ge(kc_ready, 1)
                        for gp in range(2):
                            rows = P[64 * gp:64 * gp + 64, 3, :]
                            for s in range(NS):
                                pe.matmul(rows[:, 0:NC_S], QZ[:, gp, s, :], KCb[:, s, gp, :],
                                          start=s == 0, stop=s == NS - 1)
                            pe.matmul(rows[:, 64:72], QA[:, gp, :], Z[:, KB(2, gp), SEQ:T], start=True, stop=True)
                            pe.matmul(rows[:, 72:80], QA[:, gp, :], Z[:, KB(4, gp), SEQ:T], start=True, stop=True)
                        for s in range(NS):
                            for gp in range(2):
                                c = (2 * s + gp) * 128
                                mm = pe.transpose(P[0:NC_S, 4 + c // 512, c % 512:c % 512 + 128],
                                                  VCb[:, s, gp, :], ident[:, :])
                        mm.then_inc(vturned, 1)
                        pe.wait_ge(vct_copied, 2)
                        for j in range(4):
                            for gp in range(2):
                                mm = pe.matmul(P[32 * j:32 * j + 32, 4, gp * 128:(gp + 1) * 128],
                                               VCb[:, NS, gp, 0:32], ident[:, :], start=True, stop=True)
                        mm.then_inc(vturned, 1)

                    @block.scalar
                    def _(act):
                        act.wait_ge(cmp_free, 2 * NS + 2)
                        act.activation(sq, kflat, ACT.Square).then_inc(ksq_ready, 1)
                        act.wait_ge(kvar_ready, 1)
                        act.activation(kr, kr, ACT.Sqrt).then_inc(kroot_ready, 1)
                        act.wait_ge(vturned, 1)
                        for half in range(2):
                            act.activation(VCt[0:NC_S, 4 * half:4 * half + 4, :],
                                           P[0:NC_S, 4 + 2 * half:6 + 2 * half, :]
                                           .rearrange("p b (s d) -> p (b s) d", s=2),
                                           ACT.Copy).then_inc(vct_copied, 1)
                        act.wait_ge(vturned, 2)
                        act.activation(VCp[:, :], P[:, 4, 0:256], ACT.Copy).then_inc(vct_copied, 1)

                    @block.vector
                    def _(dve):
                        step = Chain(dve, dve_step, "dve")
                        step(dve.memset(QZ[:, :, :, :], 0.0))
                        step(dve.memset(QA[:, :, :], 0.0))
                        step(dve.memset(KCb[:, NS, :, :], 0.0))
                        step(dve.memset(VCb[:, NS, :, :], 0.0))
                        for gp in range(2):
                            for g2 in range(2):
                                r = slice(64 * g2, 64 * g2 + 64)
                                step(dve.tensor_copy(
                                    QA[r, gp, 32 * g2:32 * g2 + 24].rearrange("p (s r) -> p s r", r=REP),
                                    Z[r, 2 + 3 * gp:5 + 3 * gp, SEQ:T].rearrange("p r s -> p s r")))
                        for s in range(NS):
                            step(dve.tensor_copy(
                                QZ[:, :, s, :].rearrange("p g (h c) -> p g h c", h=2)[:, :, :, 3 * s:3 * s + 3],
                                QA[:, :, :].rearrange("p g (h c) -> p g h c", h=2)[:, :, :, 3 * s:3 * s + 3]))
                        dve.sem_inc(q_ready, 1)
                        dve.wait_ge(peb_done, 1)
                        step(dve.tensor_copy(peb[:, :], P[:, 3, 0:2]))
                        for s in range(NS + 1):
                            for kv, dst in ((0, KCb), (1, VCb)):
                                n = NC_S if s < NS else NC_P
                                dve.wait_ge(cmp_done, 2 * s + kv + 1)
                                dve.tensor_scalar(dst[:, s, :, 0:n],
                                                  P[:, 4 + 2 * kv + s % 2, 0:2 * n].rearrange("p (g c) -> p g c", g=2),
                                                  peb[:, kv:kv + 1], None, ALU.add).then_inc(cmp_free, 1)
                        dve.wait_ge(kss_ready, 1)
                        step(dve.tensor_scalar(kr, P[0:HROWS, 4, 0:NH], 1.0 / HD, EPS, ALU.mult, ALU.add))
                        dve.reciprocal(kr, kr).then_inc(kvar_ready, 1)
                        dve.wait_ge(kspread, 1)
                        k3 = kflat.rearrange("p (b c) -> p b c", b=3)
                        dve.scalar_tensor_tensor(out=k3, in0=k3, scalar=vec[:, V_KG:V_KG + 1], in1=P[:, 5:8, 0:3 * NH],
                                                 op0=ALU.mult, op1=ALU.mult).then_inc(kc_ready, 1)

        def sample_attention(mix, gates, Vn, VCt, pages):
            with ExitStack() as ctx:
                S = sb(ctx, "S", [128, NCOL])
                bias = sb(ctx, "bias", [128, NCOL])
                samegs = sb(ctx, "samegs", [128, 128])
                blockno = sb(ctx, "blockno", [128, 14])
                own_sample = sb(ctx, "own_sample", [NS, 128])
                own_head = sb(ctx, "own_head", [128, HEADS])
                gall = sb(ctx, "gall", [128, HEADS, 3])
                grow = sb(ctx, "grow", [128, 3])
                PT = sb(ctx, "PT", [128, 15, 128])
                VB = 4
                vs = sb(ctx, "vs", [128, VB, PAGES, 256])
                vw = sb(ctx, "vw", [128, VB, WIN // 128, 256])
                osb = sb(ctx, "osb", [128, NS, HD])
                st = sb(ctx, "st", [128, 64])
                osb_zero = sem("osb_zero")
                osb_ready = sem("osb_ready")
                oturned = sem("oturned")
                stored = [sem(f"stored{i}") for i in range(VB)]
                v_in = [sem(f"v_in{i}") for i in range(VB)]
                grow_done = sem("grow_done")
                mx_ready = sem("mx_ready")
                exp_done = sem("exp_done")
                pc_ready = sem("pc_ready")
                imp_done = sem("imp_done")
                p_ready = sem("p_ready")
                pturned = sem("pturned")
                pt_ready = sem("pt_ready")
                pv_done = sem("pv_done")
                state["stage"] += 80
                landed = state["stage"]
                BR = ((C_CMP, NCOL), (C_SLC, C_WIN), (C_WIN, C_CMP))
                PIECES = [(128 * t, 128) for t in range(8)] + [(C_WIN + 128 * t, 128) for t in range(4)] \
                    + [(C_CMP, NC_S), (C_NSLC, NS), (C_NWIN, NS)]

                def load_values(eng, s):
                    page = [eng.value_load(pages[0:1, s * PAGES + n:s * PAGES + n + 1], min_val=0,
                                           max_val=a["cv_slc"].shape[0] - 1) for n in range(PAGES)]
                    if s >= VB:
                        eng.wait_ge(pv_done, s - VB + 1)
                        eng.wait_ge(stored[s % VB], 16 * (s // VB))
                    for n in range(PAGES):
                        eng.dma_start(vs[:, s % VB, n, :], a["cv_slc"][bass.ds(page[n], 1)]
                                      .rearrange("o p c -> (o p) c")).then_inc(v_in[s % VB], 16)
                    eng.dma_start(vw[:, s % VB, :, :], a["win_v"][s]).then_inc(v_in[s % VB], 16)

                def store_window(eng, s):
                    eng.wait_ge(v_in[s % VB], 16 * (PAGES + 1) * (s // VB + 1))
                    eng.dma_start(o["win_v"][s], vw[:, s % VB, :, :]).then_inc(stored[s % VB], 16)

                with nc.Block(no_gpsimd_drain=True) as block:
                    @block.sync
                    def _(sp):
                        for dst, src in ((bias[:, :], "sbias"), (samegs[:, :], "samegs"), (blockno[:, :], "blockno"),
                                         (own_sample[:, :], "own_sample"), (own_head[:, :], "own_head")):
                            sp.dma_start(dst, a[src]).then_inc(stage_in, 16)
                        for s in range(0, NS, VB):
                            load_values(sp, s)
                            load_values(sp, s + 2)
                            store_window(sp, s)
                            store_window(sp, s + 2)
                        for slot in stored:
                            sp.wait_ge(slot, 16 * NS // VB)

                    @block.tensor
                    def _(pe):
                        pe.wait_ge(stage_in, landed)
                        pe.matmul(P[:, 5, 0:36], own_sample[:, :], gates[0:NS, NQ, :], start=True, stop=True)\
                          .then_inc(grow_done, 1)
                        pe.wait_ge(pc_ready, 1)
                        pe.matmul(P[:, 4, 0:NC_S], samegs[:, :], S[:, C_CMP:NCOL], start=True, stop=True)\
                          .then_inc(imp_done, 1)
                        pe.wait_ge(p_ready, 1)
                        for i, (c, n) in enumerate(PIECES):
                            mm = pe.transpose(P[0:n, 4 + i // 4, i % 4 * 128:i % 4 * 128 + 128], S[:, c:c + n],
                                              ident[:, :])
                        mm.then_inc(pturned, 1)
                        pe.wait_ge(pt_ready, 1)
                        for s in range(NS):
                            pe.wait_ge(v_in[s % VB], 16 * (PAGES + 1) * (s // VB + 1))
                            for g in range(GROUPS):
                                d = slice(64 * g, 64 * g + 64)
                                out = P[32 * g:32 * g + 3, 0, 64 * s:64 * s + 64]
                                for i in range(15):
                                    n = PIECES[i][1]
                                    v = vs[:, s % VB, i, d] if i < 8 else vw[:, s % VB, i - 8, d] if i < 12 \
                                        else VCt[0:n, s, d] if i == 12 else Vn[:, i - 13, d]
                                    mm = pe.matmul(out, PT[0:n, i, 32 * g + 3 * s:32 * g + 3 * s + 3], v,
                                                   start=i == 0, stop=i == 14)
                            mm.then_inc(pv_done, 1)
                        pe.wait_ge(osb_ready, 1)
                        own = ident[:, :].rearrange("p (a b c) -> p a b c", a=2, b=2)
                        for s in range(NS):
                            for g2 in range(2):
                                mm = pe.matmul(P[64 * g2:64 * g2 + 64, 1, 6 * s:6 * s + 6]
                                               .rearrange("p (a r) -> p a r", a=2), osb[:, s, :],
                                               own[:, :, g2, 0:REP], start=True, stop=True)
                        mm.then_inc(oturned, 1)

                    @block.scalar
                    def _(act):
                        load_values(act, 1)
                        load_values(act, 3)
                        for i, b in enumerate((0, 1, 2)):
                            act.wait_ge(mx_ready, i + 1)
                            x = S[:, BR[b][0]:BR[b][1]]
                            act.activation(x, x, ACT.Exp, bias=st[:, b:b + 1], accum_out=st[:, 4 + b:5 + b])\
                               .then_inc(exp_done, 1)
                        act.wait_ge(pturned, 1)
                        step = Chain(act, act_step, "act")
                        step(act.activation(PT[:, 0:12, :], P[:, 4:7, :].rearrange("p b (i c) -> p (b i) c", i=4),
                                            ACT.Copy))
                        step(act.activation(PT[0:NC_S, 12, :], P[0:NC_S, 7, 0:128], ACT.Copy))
                        act.activation(PT[0:NS, 13:15, :], P[0:NS, 7, 128:384].rearrange("p (b c) -> p b c", b=2),
                                       ACT.Copy).then_inc(pt_ready, 1)
                        for s in (1, 3):
                            store_window(act, s)
                        for s in (5, 7):
                            load_values(act, s)
                        for s in (5, 7):
                            store_window(act, s)
                        act.wait_ge(pv_done, NS)
                        act.wait_ge(osb_zero, 1)
                        for g in range(GROUPS):
                            r = slice(32 * g, 32 * g + REP)
                            step(act.activation(osb[r, :, :], P[r, 0, :].rearrange("p (s d) -> p s d", s=NS), ACT.Copy))
                        act.sem_inc(osb_ready, 1)

                    @block.vector
                    def _(dve):
                        step = Chain(dve, dve_step, "dve")
                        dve.memset(osb[:, :, :], 0.0).then_inc(osb_zero, 1)
                        dve.wait_ge(stage_in, landed)
                        add = lambda c, n, ps: step(dve.tensor_tensor(S[:, c:c + n], ps, bias[:, c:c + n], ALU.add))
                        add(C_CMP, NC_S, P[:, 3, 0:NC_S])
                        add(C_SLC, PAST, P[:, 0:2, :].rearrange("p b c -> p (b c)"))
                        add(C_NSLC, NS, P[:, 3, 64:72])
                        add(C_WIN, WIN, P[:, 2, :])
                        add(C_NWIN, NS, P[:, 3, 72:80])

                        def maximum(b):
                            dve.tensor_reduce(st[:, b:b + 1], S[:, BR[b][0]:BR[b][1]], AX.X, ALU.max, negate=True)\
                               .then_inc(mx_ready, 1)

                        def scale(b, gate):
                            c = st[:, 4 + b:5 + b]
                            step(dve.tensor_scalar(c, c, 1e-30, None, ALU.max))
                            step(dve.reciprocal(c, c))
                            if gate:
                                step(dve.tensor_tensor(c, c, grow[:, b:b + 1], ALU.mult))
                            x = S[:, BR[b][0]:BR[b][1]]
                            return dve.tensor_scalar(x, x, c, None, ALU.mult)

                        maximum(0)
                        dve.wait_ge(grow_done, 1)
                        step(dve.tensor_tensor(gall[:, :, :], P[:, 5, 0:36].rearrange("p (h b) -> p h b", b=3),
                                               own_head[:, :].unsqueeze(2).to_broadcast([128, HEADS, 3]), ALU.mult))
                        step(dve.tensor_reduce(grow[:, :], gall[:, :, :].rearrange("p h b -> p b h"), AX.X, ALU.add))
                        dve.wait_ge(exp_done, 1)
                        scale(0, False).then_inc(pc_ready, 1)
                        dve.wait_ge(imp_done, 1)
                        score, last = st[:, 16:30], st[:, 10:11]
                        step(dve.tensor_reduce(score, P[:, 4, 4:60].rearrange("p (b c) -> p b c", c=4), AX.X, ALU.add))
                        step(dve.tensor_tensor(score, score, P[:, 4, 3:56:4], ALU.add))
                        step(dve.tensor_reduce(st[:, 8:9], score, AX.X, ALU.min))
                        step(dve.tensor_scalar(score, score, st[:, 8:9], None, ALU.is_le))
                        step(dve.tensor_tensor(score, score, blockno[:, :], ALU.mult))
                        step(dve.tensor_reduce(last, score, AX.X, ALU.max))
                        step(dve.tensor_scalar(score, blockno[:, :], last, NEG, ALU.is_equal, ALU.mult))
                        sel = S[:, 64:960].rearrange("p (b c) -> p b c", b=14)
                        step(dve.tensor_tensor(sel, sel, score.unsqueeze(2).to_broadcast([128, 14, 64]), ALU.add))
                        maximum(1)
                        maximum(2)
                        x = S[:, C_CMP:NCOL]
                        step(dve.tensor_scalar(x, x, grow[:, 0:1], None, ALU.mult))
                        dve.wait_ge(exp_done, 2)
                        step(scale(1, True))
                        dve.wait_ge(exp_done, 3)
                        scale(2, True).then_inc(p_ready, 1)
                        dve.wait_ge(oturned, 1)
                        step(dve.tensor_copy(mix[:, 2:KC, SEQ:T].rearrange("p c s -> p s c"),
                                             P[:, 1, 0:6 * NS].rearrange("p (s c) -> p s c", s=NS)))

        def prompt_attention(mix, Z, gates, Vt, VCp, KCb, KB):
            with ExitStack() as ctx:
                dist = sb(ctx, "dist", [128, 512])
                cbias = sb(ctx, "cbias", [128, NQ, HEADS, 32])
                cok = sb(ctx, "cok", [128, NQ, 1, 32])
                Pc = sb(ctx, "Pc", [128, NQ, HEADS, 32])
                PcT = sb(ctx, "PcT", [128, NQ, 3, 128])
                cst = sb(ctx, "cst", [128, 2, NQ * HEADS])
                SB = 5
                S = sb(ctx, "S_", [128, SB, 2, 512])
                PT = sb(ctx, "PT_", [128, 2, 2, 512])
                st = sb(ctx, "st_", [128, SB, 4])
                kdiag = sb(ctx, "kdiag", [128, 2, 2, 32])
                kdiag_ready = sem("kdiag_ready")
                cscored = sem("cscored")
                cmx_ready = sem("cmx_ready")
                cexp_done = sem("cexp_done")
                cp_ready = sem("cp_ready")
                cturned = sem("cturned")
                cpt_ready = sem("cpt_ready")
                s_done = sem("s_done")
                s_read = sem("s_read")
                m_ready = sem("m_ready")
                e_done = sem("e_done")
                pr_ready = sem("pr_ready")
                t_done = sem("t_done")
                t_copied = sem("t_copied")
                o_done = sem("o_done")
                o_copied = sem("o_copied")
                state["stage"] += 48
                landed = state["stage"]
                UNITS = [(gp, r, i, g2) for gp in range(2) for r in range(REP) for i in range(NQ) for g2 in range(2)]
                NUN = len(UNITS)
                head = lambda gp, r, g2: (gp * REP + r) * 2 + g2
                gate_col = lambda gp, r, g2, b: 9 * (2 * gp + g2) + 3 * r + b

                with nc.Block(no_gpsimd_drain=True) as block:
                    @block.sync
                    def _(sp):
                        sp.dma_start(cbias[:, :, :, :], a["cmpbias"]).then_inc(stage_in, 16)
                        sp.dma_start(cok[:, :, :, :], a["cmpok"]).then_inc(stage_in, 16)
                        sp.dma_start(dist[:, :], a["dist"]).then_inc(stage_in, 16)
                        stream_weights(sp, U_OUT + RING)

                    @block.tensor
                    def _(pe):
                        def scores(u):
                            gp, r, i, g2 = UNITS[u]
                            if u >= 2:
                                pe.wait_ge(s_read, u - 1)
                            q = slice(64 * g2, 64 * g2 + 64)
                            for b in range(2):
                                mm = pe.matmul(P[:, u % 2 * 2 + b, 0:128 * (i + 1)],
                                               Z[q, 2 + 3 * gp + r, i * 128:i * 128 + 128],
                                               Z[q, KB(2 + 2 * b, gp), 0:128 * (i + 1)], start=True, stop=True)
                            mm.then_inc(s_done, 1)

                        pe.wait_ge(kdiag_ready, 1)
                        for i in range(NQ):
                            for gp in range(2):
                                for r in range(REP):
                                    c = 32 * head(gp, r, 0)
                                    mm = pe.matmul(P[:, 4 + i, c:c + 64],
                                                   Z[:, 2 + 3 * gp + r, i * 128:i * 128 + 128],
                                                   kdiag[:, gp, :, :].rearrange("p g c -> p (g c)"),
                                                   start=True, stop=True)
                        mm.then_inc(cscored, 1)
                        scores(0)
                        scores(1)
                        pe.wait_ge(cp_ready, 1)
                        for i in range(NQ):
                            for n in range(3):
                                mm = pe.transpose(P[:, 4 + i, n * 128:n * 128 + 128],
                                                  Pc[:, i, 4 * n:4 * n + 4, :].rearrange("p h c -> p (h c)"),
                                                  ident[:, :])
                        mm.then_inc(cturned, 1)

                        def turn(u):
                            pe.wait_ge(pr_ready, u + 1)
                            if u == 0:
                                pe.wait_ge(cpt_ready, 1)
                            i = UNITS[u][2]
                            for b in range(2):
                                if u:
                                    pe.wait_ge(t_copied, 2 * u - 1 + b)
                                for t in range(i + 1):
                                    mm = pe.transpose(P[:, 4 + b, t * 128:t * 128 + 128],
                                                      S[:, u % SB, b, t * 128:t * 128 + 128], ident[:, :])
                                mm.then_inc(t_done, 1)

                        def values(u):
                            gp, r, i, g2 = UNITS[u]
                            pair = u // 8
                            if u % 8 == 0 and pair >= 2:
                                pe.wait_ge(o_copied, pair - 1)
                            out = P[64 * g2:64 * g2 + 64, 6 + pair % 2, i * 128:i * 128 + 128]
                            d = slice(128 * gp + 64 * g2, 128 * gp + 64 * g2 + 64)
                            hh = head(gp, r, g2)
                            k = slice(32 * (hh % 4), 32 * (hh % 4) + 32)
                            first = True
                            for b in range(2):
                                pe.wait_ge(t_copied, 2 * u + b + 1)
                                for t in range(i + 1):
                                    pe.matmul(out, Vt[:, b, t, d], PT[:, u % 2, b, t * 128:t * 128 + 128],
                                              start=first, stop=False)
                                    first = False
                            pe.matmul(out, VCp[k, d], PcT[k, i, hh // 4, :], start=False, stop=True)\
                              .then_inc(o_done, 1)

                        scores(2)
                        for u in range(NUN + 1):
                            if u + 3 < NUN:
                                scores(u + 3)
                            if u < NUN:
                                turn(u)
                            if u >= 1:
                                values(u - 1)

                    @block.scalar
                    def _(act):
                        act.wait_ge(cmx_ready, 1)
                        act.activation(Pc[:, :, :, :], Pc[:, :, :, :], ACT.Exp).then_inc(cexp_done, 1)
                        act.wait_ge(cturned, 1)
                        act.activation(PcT[:, :, :, :].rearrange("p i n c -> p i (n c)"), P[:, 4:8, 0:384],
                                       ACT.Copy).then_inc(cpt_ready, 1)

                        for u in range(NUN + 3):
                            if u < NUN:
                                act.wait_ge(m_ready, u + 1)
                                n = 128 * (UNITS[u][2] + 1)
                                for b in range(2):
                                    mm = act.activation(S[:, u % SB, b, 0:n], S[:, u % SB, b, 0:n], ACT.Exp,
                                                        bias=st[:, u % SB, b:b + 1],
                                                        accum_out=st[:, u % SB, 2 + b:3 + b])
                                mm.then_inc(e_done, 1)
                            if u >= 3:
                                v = u - 3
                                if v >= 2:
                                    act.wait_ge(o_done, v - 1)
                                n = 128 * (UNITS[v][2] + 1)
                                for b in range(2):
                                    act.wait_ge(t_done, 2 * v + b + 1)
                                    act.activation(PT[:, v % 2, b, 0:n], P[:, 4 + b, 0:n], ACT.Copy)\
                                       .then_inc(t_copied, 1)

                    @block.vector
                    def _(dve):
                        step = Chain(dve, dve_step, "dve")
                        step(dve.memset(kdiag[:, :, :, :], 0.0))
                        for g2 in range(2):
                            r = slice(64 * g2, 64 * g2 + 64)
                            mm = dve.tensor_copy(kdiag[r, :, g2, :], KCb[r, NS, :, 0:32])
                        mm.then_inc(kdiag_ready, 1)
                        dve.wait_ge(stage_in, landed)
                        dve.wait_ge(cscored, 1)
                        flat = lambda x: x[:, :, :, :].rearrange("p i h c -> p i (h c)")
                        step(dve.tensor_tensor(flat(Pc), P[:, 4:8, 0:32 * HEADS], flat(cbias), ALU.add))
                        rows = Pc[:, :, :, :].rearrange("p i h c -> p (i h) c")
                        mx, sm = cst[:, 0, :], cst[:, 1, :]
                        wide = lambda x: x.unsqueeze(2).to_broadcast([128, NQ * HEADS, 32])
                        step(dve.tensor_reduce(mx, rows, AX.X, ALU.max))
                        dve.tensor_tensor(rows, rows, wide(mx), ALU.subtract).then_inc(cmx_ready, 1)
                        dve.wait_ge(cexp_done, 1)
                        step(dve.tensor_tensor(Pc[:, :, :, :], Pc[:, :, :, :],
                                               cok[:, :, :, :].to_broadcast([128, NQ, HEADS, 32]), ALU.mult))
                        step(dve.tensor_reduce(sm, rows, AX.X, ALU.add))
                        step(dve.tensor_scalar(sm, sm, 1e-30, None, ALU.max))
                        step(dve.reciprocal(sm, sm))
                        for gp in range(2):
                            for g2 in range(2):
                                c = gate_col(gp, 0, g2, 0)
                                x = sm.rearrange("p (i q r g) -> p i q r g", i=NQ, q=2, g=2)[:, :, gp, :, g2]
                                step(dve.tensor_tensor(x, x, gates[:, 0:NQ, c:c + 7:3], ALU.mult))
                        dve.tensor_tensor(rows, rows, wide(sm), ALU.mult).then_inc(cp_ready, 1)

                        def copy_out(pair):
                            dve.wait_ge(o_done, 8 * (pair + 1))
                            dve.tensor_copy(mix[:, 2 + pair, 0:SEQ], P[:, 6 + pair % 2, :]).then_inc(o_copied, 1)

                        for u in range(NUN + 2):
                            if u < NUN:
                                gp, r, i, g2 = UNITS[u]
                                n = 128 * (i + 1)
                                dve.wait_ge(s_done, u + 1)
                                if u >= SB:
                                    dve.wait_ge(t_done, 2 * (u - SB + 1))
                                slope = float(SLOPE[(2 * gp + g2) * REP + r])
                                for b in range(2):
                                    mm = dve.scalar_tensor_tensor(
                                        out=S[:, u % SB, b, 0:n], in0=dist[:, 512 - n:512], scalar=slope,
                                        in1=P[:, u % 2 * 2 + b, 0:n], op0=ALU.mult, op1=ALU.add)
                                mm.then_inc(s_read, 1)
                                dve.wait_ge(s_read, u + 1)
                                dve.tensor_reduce(st[:, u % SB, 0:2], S[:, u % SB, :, 0:n], AX.X, ALU.max, negate=True)\
                                   .then_inc(m_ready, 1)
                            if u >= 2:
                                v = u - 2
                                gp, r, i, g2 = UNITS[v]
                                n = 128 * (i + 1)
                                dve.wait_ge(e_done, v + 1)
                                sums = st[:, v % SB, 2:4]
                                step(dve.tensor_scalar(sums, sums, 1e-30, None, ALU.max))
                                step(dve.reciprocal(sums, sums))
                                c = gate_col(gp, r, g2, 1)
                                step(dve.tensor_tensor(sums, sums, gates[:, i, c:c + 2], ALU.mult))
                                for b in range(2):
                                    x = S[:, v % SB, b, 0:n]
                                    mm = dve.tensor_scalar(x, x, sums[:, b:b + 1], None, ALU.mult)
                                mm.then_inc(pr_ready, 1)
                            if u >= 12 and (u - 12) % 8 == 0:
                                copy_out((u - 12) // 8)
                        copy_out(NUN // 8 - 1)

        def layer1():
            with ExitStack() as c0:
                R = sb(c0, "R", [128, KC, T])
                with ExitStack() as c1:
                    K, V = (sb(c1, n, [128, KC, T]) for n in ("K", "V"))
                    tg = sb(c1, "tg", [128, T])
                    tw = sb(c1, "tw", [64, T])
                    ta = sb(c1, "ta", [64, T])
                    mix_and_project(R, K, V, tw, ta, tg)
                    L = sb(c1, "L", [128, KC, T])
                    A = sb(c1, "A", [128, KC, T])
                    N_ = sb(c1, "N_", [128, KC, T])
                    rates(R, K, L, A, N_, tw, ta)
                    chunks(R, K, V, L, A, N_)
                    sample_state(R, K, V, L, A, N_)
                    output(R, K, V, L, A, tg)
                add_product(R, list(range(U_WO, U_WO + 4)), "wo")

        def mix_and_project(R, K, V, tw, ta, tg):
            with ExitStack() as ctx:
                xn = sb(ctx, "xn1", [128, KC, T])
                xx = sb(ctx, "xx", [128, KC, T])
                xf = V[:, 5:7, :]
                xm = [sb(ctx, "xm" + n, [128, KC, T], F32R) for n in "hl"]
                ws = sb(ctx, "ws_mix", [128, 2, 2, UW], F32R)
                lw = [V[:, 0, k * 64:k * 64 + 64] for k in range(KC)]
                la = [V[:, 1, k * 64:k * 64 + 64] for k in range(KC)]
                lg = [V[:, 2 + k // 4, k % 4 * 128:k % 4 * 128 + 128] for k in range(KC)]
                prev = V[:, 4, 0:KC * NS].rearrange("p (k s) -> p k s", k=KC)
                mixed = sem("mixed")
                low_free = sem("low_free")
                low_used = sem("low_used")
                normed = sem("normed")
                ORDER = ((1, (lw, tw, 64, ACT.Tanh)), (4, (la, ta, 64, ACT.Copy)), (5, (lg, tg, 128, ACT.Sigmoid)),
                         (0, R), (2, K), (3, V))
                x0 = take_splits(3 * KC)
                firsts = [plan(list(range(U_R + 4 * j, U_R + 4 * j + 4))) for j in range(3)]
                i = state["norm"]
                state["norm"] += 1
                state["stage"] += 64
                landed = state["stage"]
                state["stores"] += 16

                with nc.Block(no_gpsimd_drain=True) as block:
                    @block.sync
                    def _(sp):
                        for dst, src in ((prev, a["state_shift"]),
                                         (V[:, 0, 0:512], a["rwkv_w1"].rearrange("p k c -> p (k c)")),
                                         (V[:, 1, 0:512], a["rwkv_a1"].rearrange("p k c -> p (k c)")),
                                         (V[:, 2:4, 0:512], a["rwkv_g1"].rearrange("p (b k) c -> p b (k c)", b=2))):
                            sp.dma_start(dst, src).then_inc(stage_in, 16)
                        stream_weights(sp, U_WO)
                        sp.wait_ge(normed, 1)
                        sp.dma_start(o["shift"], xn[:, :, SEQ - 1:T]).then_inc(stores, 16)
                        stream_weights(sp, U_WO + 1)
                        sp.wait_ge(stores, state["stores"])

                    @block.gpsimd
                    def _(pool):
                        weight_rests(pool, range(U_R, U_WO), ws)

                    @block.tensor
                    def _(pe):
                        norm_pe(pe, i, xn)
                        for j in range(3):
                            w, _, n, _ = ORDER[j][1]
                            for k in range(KC):
                                pe.wait_ge(mixed, j * KC + k + 1)
                                for hf in range(2):
                                    mm = pe.matmul(P[0:n, 2 * j + hf, 0:HT], w[k],
                                                   xf[:, k % 2, hf * HT:(hf + 1) * HT], start=k == 0,
                                                   stop=k == KC - 1)
                                mm.then_inc(low_used, 1)
                        pe.wait_ge(low_free, 3)
                        for j in range(3):
                            dense(pe, firsts[j], list(range(U_R + 4 * j, U_R + 4 * j + 4)), ws, xm,
                                  chunk_ready=lambda k, j=j: pe.wait_ge(xsplit_ready, x0 + j * KC + k + 1))

                    @block.scalar
                    def _(act):
                        units = range(U_R, U_WO)
                        norm_act(act, i, xn, None, units, ws)
                        for j in range(3):
                            _, dst, n, f = ORDER[j][1]
                            act.wait_ge(low_used, KC * (j + 1))
                            act.activation(halves(dst[0:n, :]), P[0:n, 2 * j:2 * j + 2, 0:HT], f).then_inc(low_free, 1)
                        for j, dst in enumerate((R, K, V)):
                            for k in range(KC):
                                act.wait_ge(mixed, (3 + j) * KC + k + 1)
                                if k == 0 and j:
                                    act.wait_ge(tile_done, firsts[j])
                                split_head(act, xf[:, k % 2, :], xm[0][:, k, :])
                            for m in range(KC):
                                act.wait_ge(tile_done, firsts[j] + m + 1)
                                act.activation(halves(dst[:, m, :]), tile(firsts[j] + m), ACT.Copy)\
                                   .then_inc(tile_free, 1)
                                if m % 2:
                                    weight_head(act, U_R + 4 * j + m // 2 + 2, units, ws)

                    @block.vector
                    def _(dve):
                        step = Chain(dve, dve_step, "dve")
                        norm_dve(dve, step, i, xn, V_MIX + KC)
                        dve.wait_ge(xn_ready, (i + 1) * KC)
                        dve.wait_ge(stage_in, landed)
                        dve.tensor_tensor(xx[:, :, 1:SEQ], xn[:, :, 0:SEQ - 1], xn[:, :, 1:SEQ], ALU.subtract)\
                           .then_inc(normed, 1)
                        dve.tensor_scalar(xx[:, :, 0:1], xn[:, :, 0:1], -1.0, None, ALU.mult)
                        step(dve.tensor_tensor(xx[:, :, SEQ:T], prev, xn[:, :, SEQ:T], ALU.subtract))
                        dve.wait_ge(normed, 1)
                        for j, (mu, _) in enumerate(ORDER):
                            for k in range(KC):
                                n = j * KC + k
                                if 2 <= n < 3 * KC + 2:
                                    dve.wait_ge(low_used, n - 1)
                                c = V_MU + KC * mu + k
                                dve.scalar_tensor_tensor(out=xf[:, k % 2, :], in0=xx[:, k, :], scalar=vec[:, c:c + 1],
                                                         in1=xn[:, k, :], op0=ALU.mult, op1=ALU.add)\
                                   .then_inc(mixed, 1)
                                if j >= 3:
                                    if k == 0 and j > 3:
                                        dve.wait_ge(tile_done, firsts[j - 3])
                                    split_rest(dve, x0 + n - 3 * KC, xf[:, k % 2, :], xm[0][:, k, :], xm[1][:, k, :])

        def rates(R, K, L, A, N_, tw, ta):
            with ExitStack() as ctx:
                w2 = sb(ctx, "w2", [64, D])
                a2 = sb(ctx, "a2", [64, D])
                sq = sb(ctx, "sq2", [128, 2, T])
                s = sb(ctx, "s2", [128, T])
                inv = sb(ctx, "kkinv", [HROWS, T])
                to_rows = sb(ctx, "to_rows2", [128, 10, HROWS])
                from_rows = sb(ctx, "from_rows2", [HROWS, 10, 128])
                lo_done = sem("lo_done")
                lo_free = sem("lo_free")
                kk_ready = sem("kk_ready")
                kk_sq = sem("kk_sq")
                kk_used = sem("kk_used")
                kk_root = sem("kk_root")
                kk_inv = sem("kk_inv")
                kb_done = sem("kb_done")
                kb_read = sem("kb_read")
                kka_ready = sem("kka_ready")
                state["stage"] += 64
                landed = state["stage"]
                with nc.Block(no_gpsimd_drain=True) as block:
                    @block.sync
                    def _(sp):
                        for dst, src in ((w2[:, :], "rwkv_w2"), (a2[:, :], "rwkv_a2"), (to_rows[:, :, :], "to_rows"),
                                         (from_rows[:, :, :], "from_rows")):
                            sp.dma_start(dst, a[src]).then_inc(stage_in, 16)

                    @block.gpsimd
                    def _(pool):
                        for m in range(KC):
                            c = V_KK + m
                            pool.tensor_tensor(N_[:, m, :], K[:, m, :], vec[:, c:c + 1].to_broadcast([128, T]),
                                               ALU.mult).then_inc(kk_ready, 1)
                        for m in range(KC):
                            pool.wait_ge(kb_read, m + 1)
                            pool.tensor_tensor(A[:, m, :], A[:, m, :], N_[:, m, :], ALU.mult).then_inc(kka_ready, 1)
                        pool.wait_ge(kka_ready, KC)

                    @block.tensor
                    def _(pe):
                        def head_sums(m):
                            pe.wait_ge(kk_sq, m + 1)
                            for hf in range(2):
                                mm = pe.matmul(P[0:HROWS, 4 + hf, 0:HT], to_rows[:, m, :],
                                               sq[:, m % 2, hf * HT:(hf + 1) * HT], start=m == 0, stop=m == KC - 1)
                            mm.then_inc(kk_used, 1)

                        pe.wait_ge(stage_in, landed)
                        for n in range(2 * KC):
                            if n >= 2:
                                pe.wait_ge(lo_free, n - 1)
                            w, x = ((w2, tw), (a2, ta))[n // KC]
                            m = n % KC
                            for hf in range(2):
                                mm = pe.matmul(P[:, 2 * (n % 2) + hf, 0:HT], w[:, m * 128:(m + 1) * 128],
                                               x[:, hf * HT:(hf + 1) * HT], start=True, stop=True)
                            mm.then_inc(lo_done, 1)
                            if n % 2 and n > 1:
                                head_sums(n // 2 - 1)
                        head_sums(KC - 1)
                        pe.wait_ge(kk_inv, 1)
                        pe.wait_ge(lo_free, 2 * KC)
                        for m in range(KC):
                            if m >= 2:
                                pe.wait_ge(kb_read, m - 1)
                            for hf in range(2):
                                mm = pe.matmul(P[:, (6, 0)[m % 2] + hf, 0:HT], from_rows[:, m, :],
                                               inv[:, hf * HT:(hf + 1) * HT], start=True, stop=True)
                            mm.then_inc(kb_done, 1)

                    @block.scalar
                    def _(act):
                        for n in range(2 * KC):
                            dst, col = ((L, V_W0), (A, V_A0))[n // KC]
                            m = n % KC
                            act.wait_ge(lo_done, n + 1)
                            act.activation(halves(dst[:, m, :]), P[:, 2 * (n % 2):2 * (n % 2) + 2, 0:HT], ACT.Sigmoid,
                                           bias=vec[:, col + m:col + m + 1]).then_inc(lo_free, 1)
                            if n % 2:
                                m = n // 2
                                act.wait_ge(kk_ready, m + 1)
                                if m >= 2:
                                    act.wait_ge(kk_used, m - 1)
                                act.activation(sq[:, m % 2, :], N_[:, m, :], ACT.Square).then_inc(kk_sq, 1)
                        act.wait_ge(kk_used, KC)
                        act.activation(halves(inv[:, :]), P[0:HROWS, 4:6, 0:HT], ACT.Sqrt).then_inc(kk_root, 1)

                    @block.vector
                    def _(dve):
                        step = Chain(dve, dve_step, "dve")
                        dve.wait_ge(lo_free, KC)
                        Lf = L[:, :, :].rearrange("p k t -> p (k t)")
                        step(dve.tensor_scalar(Lf, Lf, -math.exp(-0.5), None, ALU.mult))
                        dve.wait_ge(kk_ready, KC)
                        for m in range(KC):
                            c = V_KA + m
                            dve.wait_ge(lo_free, KC + m + 1)
                            step(dve.tensor_scalar(s[:, :], A[:, m, :], 1.0, vec[:, c:c + 1], ALU.subtract, ALU.mult))
                            step(dve.scalar_tensor_tensor(out=K[:, m, :], in0=s[:, :], scalar=1.0, in1=K[:, m, :],
                                                          op0=ALU.add, op1=ALU.mult))
                        dve.wait_ge(kk_root, 1)
                        step(dve.tensor_scalar(inv[:, :], inv[:, :], 1e-12, None, ALU.max))
                        dve.reciprocal(inv[:, :], inv[:, :]).then_inc(kk_inv, 1)
                        for m in range(KC):
                            dve.wait_ge(kb_done, m + 1)
                            dve.tensor_tensor(halves(N_[:, m, :]), halves(N_[:, m, :]),
                                              P[:, (6, 0)[m % 2]:(6, 0)[m % 2] + 2, 0:HT], ALU.mult)\
                               .then_inc(kb_read, 1)

        def chunks(R, K, V, L, A, N_):
            with ExitStack() as ctx:
                tri = sb(ctx, "tri", [128, 128])
                level = sb(ctx, "level", [128, 6, CH])
                ident2 = sb(ctx, "ident2", [128, 64])
                restart = sb(ctx, "restart", [128, KC, CH + 1])
                Eend = sb(ctx, "Eend", [128, 3, KC])
                E = sb(ctx, "E", [128, 2, KC, CH + 1])
                Ls, Lc = E[:, 0], E[:, 1]
                Ep, Em = E[:, 0], E[:, 1]
                AR = sb(ctx, "AR", [128, 2, KC, 2, CH])
                BK = sb(ctx, "BK", [128, 2, KC, CH])
                G = sb(ctx, "G", [128, 2, 2, KC, 2, CH])
                assert U_WO % RING == RING - 1
                spare = ring[:, 0:RING - 1, :].rearrange("p r c -> p (r c)")
                tm = spare[:, 0:3072].rearrange("p (d j n t) -> p d j n t", d=2, j=3, n=KC)
                XL = spare[:, 3072:4096].rearrange("p (d n t) -> p d n t", d=2, n=KC)
                Uf = spare[:, 4096:4608].rearrange("p (n t) -> p n t", n=KC)
                TUP = 512 + 32
                TU = spare[:, 4608:4608 + 2 * TUP].rearrange("p (h c) -> p h c", h=2)
                Tm = lambda hf: TU[:, hf, 0:256].rearrange("p (n t) -> p n t", n=4)
                Um = lambda hf: TU[:, hf, 256:512].rearrange("p (n t) -> p n t", n=4)
                Y = sb(ctx, "Y", [128, 5, 2, 4, CH])
                X = rstd[:, 0:512].rearrange("p (n t) -> p n t", n=KC)
                SA = sb(ctx, "SA", [128, KC, CH])
                S = sb(ctx, "S1", [128, KC, CH])
                names = ("ls_ready ep_done em_done til_ready g_done g_ready tm_done tm_ready y_done y_ready tu_done "
                         "tu_ready uf_ready y_zero xl_ready x_done x_ready sa_done sa_ready o_done s_done s_ready o_read")
                (ls_ready, ep_done, em_done, til_ready, g_done, g_ready, tm_done, tm_ready, y_done, y_ready, tu_done,
                 tu_ready, uf_ready, y_zero, xl_ready, x_done, x_ready, sa_done, sa_ready, o_done, s_done, s_ready, o_read) = \
                    (sem("w_" + n) for n in names.split())
                state["stage"] += 64
                landed = state["stage"]
                state["stores"] += 16
                LEV = 5
                half_rows = [(p, slice(64 * p, 64 * p + 64)) for p in range(2)]
                blocks = lambda x, lv, odd: x.rearrange("p (m two w) -> p m two w", two=2, w=1 << lv)[:, :, odd, :]
                compact = lambda x, lv: x.rearrange("p (m w) -> p m w", w=1 << lv)
                y_no = lambda c, lv, hf: 2 * (c * LEV + lv - 1) + hf + 1
                tu_no = lambda c, lv, hf: 2 * (c * (LEV + 1) + lv) + hf + 1

                with nc.Block(no_gpsimd_drain=True) as block:
                    @block.sync
                    def _(sp):
                        for dst, src in ((tri[:, :], "tri"), (level[:, :, :], "level"), (ident2[:, :], "ident2"),
                                         (restart[:, :, :], "restart")):
                            sp.dma_start(dst, a[src]).then_inc(stage_in, 16)
                        sp.wait_ge(x_ready, NCH + 1)
                        sp.dma_start(o["wkv_p"], X[:, :, :]).then_inc(stores, 16)
                        sp.wait_ge(stores, state["stores"])

                    G_BANK = (2, 3, 6, 7)

                    @block.tensor
                    def _(pe):
                        pe.wait_ge(stage_in, landed)

                        def scores(c, q):
                            pe.wait_ge(til_ready, c + 1)
                            if c and q < 3:
                                pe.wait_ge(tm_ready, 3 * (c - 1) + q + 1)
                            elif c:
                                pe.wait_ge(g_ready, 4 * c)
                            for p, r in half_rows:
                                for n in range(4):
                                    nn = q % 2 * 4 + n
                                    mm = pe.matmul(P[r, G_BANK[q], n * 128:n * 128 + 128], BK[r, q // 2, nn, :],
                                                   AR[r, c % 2, nn, :, :].rearrange("p a t -> p (a t)"),
                                                   start=True, stop=True)
                            mm.then_inc(g_done, 1)

                        def turn(c, j):
                            pe.wait_ge(g_ready, 4 * c + j + 1)
                            for p, r in half_rows:
                                for n in range(KC):
                                    x = V[r, n, c * CH:(c + 1) * CH] if j == 0 else BK[r, j - 1, n, :]
                                    mm = pe.matmul(P[r, G_BANK[j], n * CH:(n + 1) * CH], x, ident2[r, :],
                                                   start=True, stop=True)
                            mm.then_inc(tm_done, 1)

                        def times_t(c, lv):
                            pe.wait_ge(xl_ready, c * (LEV + 1) + lv + 1)
                            for hf in range(2):
                                if c or lv:
                                    pe.wait_ge(tu_ready, tu_no(c, lv, hf) - 2)
                                for p, r in half_rows:
                                    for n in range(4):
                                        t = blocks(Tm(hf)[r, n, :] if lv else ident2[r, :], lv, 0)
                                        mm = pe.matmul(compact(P[r, hf, n * 32:n * 32 + 32], lv),
                                                       XL[r, (c * (LEV + 1) + lv) % 2, 4 * hf + n, :], t,
                                                       start=True, stop=True)
                                mm.then_inc(y_done, 1)

                        def t_times(c, lv):
                            for hf in range(2):
                                pe.wait_ge(y_ready, y_no(c, lv, hf))
                                for which in range(2):
                                    if which == 0 and lv == LEV:
                                        continue
                                    for p, r in half_rows:
                                        for n in range(4):
                                            u, y = Um(hf)[r, n, :], Y[r, lv - 1, hf, n, :]
                                            w, x = (u, blocks(y, lv, 0)) if which == 0 else (y, blocks(u, lv, 1))
                                            at = 128 + 128 * which + 32 * n
                                            mm = pe.matmul(compact(P[r, hf, at:at + 32], lv), w, x,
                                                           start=True, stop=True)
                                mm.then_inc(tu_done, 1)

                        def x_part(c):
                            pe.wait_ge(s_ready, c + 1)
                            pe.wait_ge(g_ready, 4 * c + 4)
                            pe.wait_ge(tm_ready, 3 * c + 3)
                            if c:
                                pe.wait_ge(o_read, c)
                            for p, r in half_rows:
                                for n in range(KC):
                                    out = P[r, 4, n * CH:(n + 1) * CH]
                                    pe.matmul(out, AR[r, c % 2, n, 0, :], S[r, n, :], start=True, stop=False)
                                    mm = pe.matmul(out, G[r, c % 2, 1, n, 0, :], tm[r, c % 2, 0, n, :],
                                                   start=False, stop=True)
                            mm.then_inc(x_done, 1)

                        def sa_part(c):
                            pe.wait_ge(tu_ready, tu_no(c, LEV, 1))
                            pe.wait_ge(uf_ready, c + 1)
                            pe.wait_ge(x_ready, c + 1)
                            for p, r in half_rows:
                                for n in range(KC):
                                    mm = pe.matmul(P[r, 5, n * CH:(n + 1) * CH], Uf[r, n, :], X[r, n, :],
                                                   start=True, stop=True)
                            mm.then_inc(sa_done, 1)

                        def o_part(c, hf):
                            pe.wait_ge(sa_ready, c + 1)
                            for p, r in half_rows:
                                for n in range(4 * hf, 4 * hf + 4):
                                    out = P[r, 4, n * CH:(n + 1) * CH]
                                    pe.matmul(out, S[r, n, :], AR[r, c % 2, n, 1, :], start=True, stop=False)
                                    pe.matmul(out, SA[r, n, :], G[r, c % 2, 0, n, 1, :], start=False, stop=False)
                                    mm = pe.matmul(out, tm[r, c % 2, 0, n, :], G[r, c % 2, 1, n, 1, :],
                                                   start=False, stop=True)
                            if hf:
                                mm.then_inc(o_done, 1)

                        def s_part(c):
                            for p, r in half_rows:
                                for n in range(KC):
                                    out = P[r, 5, n * CH:(n + 1) * CH]
                                    pe.matmul(out, tm[r, c % 2, 1, n, :], SA[r, n, :], start=True, stop=False)
                                    mm = pe.matmul(out, tm[r, c % 2, 2, n, :], tm[r, c % 2, 0, n, :],
                                                   start=False, stop=True)
                            mm.then_inc(s_done, 1)

                        for q in range(4):
                            scores(0, q)
                        for j in range(3):
                            turn(0, j)
                        for c in range(NCH + 1):
                            before, after = c > 0, c + 1 < NCH
                            for lv in range(LEV + 1):
                                if c < NCH:
                                    times_t(c, lv)
                                if before and lv == 0:
                                    x_part(c - 1)
                                if before and lv == 1:
                                    sa_part(c - 1)
                                if before and lv == 2:
                                    o_part(c - 1, 1)
                                if after and lv in (3, 4):
                                    scores(c + 1, 2 * (lv - 3))
                                if after and lv == 5:
                                    turn(c + 1, 0)
                                if c < NCH and lv:
                                    t_times(c, lv)
                                if before and lv == 1:
                                    o_part(c - 1, 0)
                                if before and lv == 2:
                                    s_part(c - 1)
                                if after and lv in (3, 4):
                                    scores(c + 1, 2 * (lv - 3) + 1)
                                if after and lv == 5:
                                    turn(c + 1, 1)
                                    turn(c + 1, 2)
                        pe.wait_ge(s_ready, NCH + 1)
                        pe.wait_ge(o_read, NCH)
                        for p, r in half_rows:
                            for n in range(KC):
                                mm = pe.matmul(P[r, 4, n * CH:(n + 1) * CH], S[r, n, :], ident2[r, :],
                                               start=True, stop=True)
                        mm.then_inc(x_done, 1)

                    @block.scalar
                    def _(act):
                        by_n = lambda bank: P[:, bank, :].rearrange("p (n t) -> p n t", n=KC)

                        def exps(c):
                            act.wait_ge(ls_ready, c + 1)
                            act.activation(Ep, Lc, ACT.Exp).then_inc(ep_done, 1)
                            act.activation(Em, Lc, ACT.Exp, scale=-1.0).then_inc(em_done, 1)

                        def copies(c):
                            if c >= 2:
                                act.wait_ge(o_done, c - 1)
                                act.wait_ge(s_done, c - 1)
                            for j in range(3):
                                act.wait_ge(tm_done, 3 * c + j + 1)
                                act.activation(tm[:, c % 2, j, :, :], by_n(G_BANK[j]), ACT.Copy).then_inc(tm_ready, 1)

                        def y_copy(c, lv):
                            for hf in range(2):
                                act.wait_ge(y_done, tu_no(c, lv, hf))
                                act.activation(blocks(Y[:, lv - 1, hf, :, :].rearrange("p n t -> p (n t)"), lv, 0),
                                               compact(P[:, hf, 0:128], lv), ACT.Copy).then_inc(y_ready, 1)

                        def xc(c):
                            act.wait_ge(x_done, c + 1)
                            act.activation(X[:, :, :], by_n(4), ACT.Copy).then_inc(x_ready, 1)

                        def sac(c):
                            act.wait_ge(sa_done, c + 1)
                            act.activation(SA[:, :, :], by_n(5), ACT.Copy).then_inc(sa_ready, 1)

                        def oc(c):
                            act.wait_ge(o_done, c + 1)
                            act.activation(L[:, :, c * CH:(c + 1) * CH], by_n(4), ACT.Copy).then_inc(o_read, 1)

                        exps(0)
                        exps(1)
                        copies(0)
                        for c in range(NCH + 1):
                            for lv in range(LEV + 1):
                                if lv == 1:
                                    act.wait_ge(y_zero, 1)
                                if c < NCH and lv:
                                    y_copy(c, lv)
                                if c and lv < 3:
                                    (xc, sac, oc)[lv](c - 1)
                            if c + 1 < NCH:
                                copies(c + 1)
                            if c + 2 < NCH:
                                exps(c + 2)
                        xc(NCH)

                    @block.gpsimd
                    def _(pool):
                        pool.wait_ge(stage_in, landed)
                        for c in range(NCH):
                            pool.wait_ge(g_ready, 4 * c + 2)
                            for lv in range(LEV + 1):
                                e = c * (LEV + 1) + lv
                                if e >= 2:
                                    pool.wait_ge(tu_ready, 2 * (e - 1))
                                pool.tensor_tensor(XL[:, e % 2, :, :], G[:, c % 2, 0, :, 0, :],
                                                   level[:, lv, :].unsqueeze(1).to_broadcast([128, KC, CH]),
                                                   ALU.mult).then_inc(xl_ready, 1)
                            pool.wait_ge(tu_ready, tu_no(c, LEV - 1, 1))
                            if c:
                                pool.wait_ge(sa_done, c)
                            pool.tensor_copy(Uf[:, :, 0:32].rearrange("p (h n) t -> p h n t", h=2),
                                             TU[:, :, 256:512].rearrange("p h (n t) -> p h n t", n=4)[:, :, :, 0:32])\
                                .then_inc(uf_ready, 1)

                    @block.vector
                    def _(dve):
                        step = Chain(dve, dve_step, "dve")
                        dve.wait_ge(stage_in, landed)
                        dve.memset(S[:, :, :], 0.0).then_inc(s_ready, 1)
                        dve.memset(Y[:, :, :, :, :], 0.0).then_inc(y_zero, 1)
                        flat = lambda x: x.rearrange("p n t -> p (n t)")

                        def decays(c):
                            step(dve.memset(Ls[:, :, 0:1], 0.0))
                            step(dve.tensor_copy(Ls[:, :, 1:], L[:, :, c * CH:(c + 1) * CH]))
                            dve.tensor_tensor_scan(flat(Lc), flat(restart[:, :, :]), flat(Ls), 0.0,
                                                   ALU.mult, ALU.add).then_inc(ls_ready, 1)

                        def tilde_sources(c):
                            t = slice(c * CH, (c + 1) * CH)
                            dve.wait_ge(em_done, c + 1)
                            if c:
                                dve.wait_ge(tm_done, 3 * c)
                            dve.tensor_tensor(BK[:, 0, :, :], A[:, :, t], Em[:, :, 1:], ALU.mult)
                            step(dve.tensor_tensor(BK[:, 1, :, :], K[:, :, t], Em[:, :, 1:], ALU.mult))

                        def tilde_targets(c):
                            t = slice(c * CH, (c + 1) * CH)
                            dve.wait_ge(ep_done, c + 1)
                            if c >= 2:
                                dve.wait_ge(o_done, c - 1)
                            dve.tensor_copy(Eend[:, c % 3, :], Ep[:, :, CH])
                            dve.scalar_tensor_tensor(out=AR[:, c % 2, :, 0, :], in0=N_[:, :, t], scalar=-1.0,
                                                     in1=Ep[:, :, 0:CH], op0=ALU.mult, op1=ALU.mult)
                            step(dve.tensor_tensor(AR[:, c % 2, :, 1, :], R[:, :, t], Ep[:, :, 1:], ALU.mult))
                            dve.sem_inc(til_ready, 1)

                        def mask(c, q):
                            dve.wait_ge(g_done, 4 * c + q + 1)
                            n = slice(q % 2 * 4, q % 2 * 4 + 4)
                            dve.tensor_tensor(G[:, c % 2, q // 2, n, :, :].rearrange("p n a t -> p n (a t)"),
                                              P[:, G_BANK[q], :].rearrange("p (n t) -> p n t", n=4),
                                              tri[:, :].unsqueeze(1).to_broadcast([128, 4, 128]), ALU.mult)\
                               .then_inc(g_ready, 1)

                        def tu_first(c):
                            e = c * (LEV + 1)
                            dve.wait_ge(xl_ready, e + 1)
                            if c:
                                dve.wait_ge(uf_ready, c)
                                dve.wait_ge(tu_ready, 2 * e)
                            for hf in range(2):
                                dve.tensor_tensor(Um(hf), XL[:, e % 2, 4 * hf:4 * hf + 4, :],
                                                  ident2[:, :].unsqueeze(1).to_broadcast([128, 4, CH]), ALU.add)
                                dve.tensor_copy(Tm(hf)[:, :, 1::2],
                                                ident2[:, 1::2].unsqueeze(1).to_broadcast([128, 4, 32]))
                            for hf in range(2):
                                dve.wait_ge(y_done, tu_no(c, 0, hf))
                                dve.tensor_tensor(Tm(hf)[:, :, 0::2],
                                                  P[:, hf, 0:128].rearrange("p (n t) -> p n t", n=4),
                                                  ident2[:, 0::2].unsqueeze(1).to_broadcast([128, 4, 32]), ALU.add)\
                                   .then_inc(tu_ready, 1)

                        def tu(c, lv):
                            w = 1 << lv
                            for hf in range(2):
                                dve.wait_ge(tu_done, y_no(c, lv, hf))
                                dve.wait_ge(tu_ready, tu_no(c, lv - 1, hf))
                                if lv < LEV:
                                    x = TU[:, hf, 0:512 + 2 * w].rearrange("p (q c) -> p q c", q=2)[:, :, 0:256]
                                    x = x.rearrange("p q (m two w) -> p q m two w", two=2, w=w)[:, :, :, 0, :]
                                    dve.tensor_tensor(x, x, P[:, hf, 128:384].rearrange(
                                        "p (q m w) -> p q m w", q=2, w=w), ALU.add).then_inc(tu_ready, 1)
                                else:
                                    dve.tensor_tensor(Uf[:, 4 * hf:4 * hf + 4, 32:64], Um(hf)[:, :, 32:64],
                                                      P[:, hf, 256:384].rearrange("p (n t) -> p n t", n=4),
                                                      ALU.add).then_inc(tu_ready, 1)

                        def new_state(c):
                            dve.wait_ge(s_done, c + 1)
                            dve.wait_ge(o_done, c + 1)
                            step(dve.tensor_tensor(S[:, :, :], S[:, :, :],
                                                   P[:, 5, :].rearrange("p (n t) -> p n t", n=KC), ALU.add))
                            dve.tensor_tensor(S[:, :, :], S[:, :, :],
                                              Eend[:, c % 3, :].unsqueeze(2).to_broadcast([128, KC, CH]), ALU.mult)\
                               .then_inc(s_ready, 1)

                        decays(0)
                        tilde_sources(0)
                        tilde_targets(0)
                        decays(1)
                        for q in range(4):
                            mask(0, q)
                        for c in range(NCH + 1):
                            before, after = c > 0, c + 1 < NCH
                            for lv in range(LEV + 1):
                                if c < NCH:
                                    tu(c, lv) if lv else tu_first(c)
                                if after and lv == 1:
                                    tilde_sources(c + 1)
                                if after and lv == 2:
                                    tilde_targets(c + 1)
                                if before and lv == 3:
                                    new_state(c - 1)
                                if after and lv in (3, 4):
                                    mask(c + 1, 2 * (lv - 3))
                                    mask(c + 1, 2 * (lv - 3) + 1)
                            if c + 2 < NCH:
                                decays(c + 2)

        def sample_state(R, K, V, L, A, N_):
            with ExitStack() as ctx:
                ident2 = sb(ctx, "ident3", [128, 64])
                S = sb(ctx, "Ss", [128, NS, KC, HD])
                dg = sb(ctx, "dg", [128, NS, KC, HD])
                tmp = sb(ctx, "tmp", [128, NS, KC, HD])
                sa = sb(ctx, "sa", [128, NS, KC])
                dg_ready = sem("dg_ready")
                spread = sem("spread")
                spread_read = sem("spread_read")
                out_ready = sem("out_ready")
                dec_ready = sem("dec_ready")
                state["stage"] += 32
                landed = state["stage"]
                state["stores"] += 16
                VECS = 5
                with nc.Block(no_gpsimd_drain=True) as block:
                    @block.sync
                    def _(sp):
                        sp.dma_start(ident2[:, :], a["ident2"]).then_inc(stage_in, 16)
                        sp.dma_start(S[:, :, :, :], a["state_wkv"]).then_inc(stage_in, 16)
                        stream_weights(sp, U_WO + RING)
                        sp.wait_ge(out_ready, 1)
                        sp.dma_start(o["wkv_s"], S[:, :, :, :]).then_inc(stores, 16)
                        sp.wait_ge(stores, state["stores"])

                    @block.tensor
                    def _(pe):
                        for v in range(VECS):
                            for s in range(NS):
                                n = NS * v + s
                                pe.wait_ge(dg_ready, n + 1)
                                if v:
                                    pe.wait_ge(spread_read, n - NS + 1)
                                pe.matmul(P[:, s, :], headones[:, :], dg[:, s, :, :].rearrange("p n j -> p (n j)"),
                                          start=True, stop=True).then_inc(spread, 1)

                    @block.scalar
                    def _(act):
                        act.activation(L[:, :, SEQ:T], L[:, :, SEQ:T], ACT.Exp).then_inc(dec_ready, 1)

                    @block.gpsimd
                    def _(pool):
                        pool.wait_ge(stage_in, landed)
                        pool.wait_ge(dec_ready, 1)
                        for v, x in enumerate((N_, L, A, K, R)):
                            for s in range(NS):
                                if v:
                                    pool.wait_ge(spread, NS * (v - 1) + s + 1)
                                pool.tensor_tensor(dg[:, s, :, :],
                                                   ident2[:, :].unsqueeze(1).to_broadcast([128, KC, HD]),
                                                   x[:, :, SEQ + s:SEQ + s + 1].to_broadcast([128, KC, HD]),
                                                   ALU.mult).then_inc(dg_ready, 1)

                    @block.vector
                    def _(dve):
                        step = Chain(dve, dve_step, "dve")
                        dve.wait_ge(stage_in, landed)
                        ps = lambda s: P[:, s, :].rearrange("p (n j) -> p n j", n=KC)
                        for v in range(VECS):
                            for s in range(NS):
                                dve.wait_ge(spread, NS * v + s + 1)
                                x, y = S[:, s, :, :], tmp[:, s, :, :]
                                if v == 0:
                                    step(dve.tensor_tensor(y, x, ps(s), ALU.mult))
                                    mm = dve.tensor_reduce(sa[:, s, :], y, AX.X, ALU.add, negate=True)
                                elif v == 1:
                                    mm = dve.tensor_tensor(x, x, ps(s), ALU.mult)
                                elif v < 4:
                                    by = sa[:, s, :] if v == 2 else V[:, :, SEQ + s]
                                    step(dve.tensor_tensor(y, ps(s), by.unsqueeze(2).to_broadcast([128, KC, HD]),
                                                           ALU.mult))
                                    mm = dve.tensor_tensor(x, x, y, ALU.add)
                                else:
                                    step(dve.tensor_tensor(y, x, ps(s), ALU.mult))
                                    mm = dve.tensor_reduce(sa[:, s, :], y, AX.X, ALU.add)
                                mm.then_inc(spread_read, 1)
                                dve.wait_ge(spread_read, NS * v + s + 1)
                            if v == 3:
                                dve.sem_inc(out_ready, 1)
                        step(dve.tensor_copy(L[:, :, SEQ:T].rearrange("p n s -> p s n"), sa[:, :, :]))

        def output(R, K, V, O, B, tg):
            with ExitStack() as ctx:
                g2 = sb(ctx, "g2", [128, D])
                csq = sb(ctx, "csq", [128, 3, T])
                rkv = sb(ctx, "rkv", [128, 3, T])
                rs = sb(ctx, "rs", [128, 2, T])
                rk_step = sem("rk_step")
                rk_ready = sem("rk_ready")
                mean_done = sem("mean_done")
                bonus_done = sem("bonus_done")
                var_done = sem("var_done")
                og_done = sem("og_done")
                centred = sem("centred")
                csq_ready = sem("csq_ready")
                bonus_ready = sem("bonus_ready")
                var_read = sem("var_read")
                n_var = sem("n_var")
                n_root = sem("n_root")
                gated = sem("gated")
                state["stage"] += 16
                landed = state["stage"]
                with nc.Block(no_gpsimd_drain=True) as block:
                    @block.sync
                    def _(sp):
                        sp.dma_start(g2[:, :], a["rwkv_g2"]).then_inc(stage_in, 16)

                    @block.gpsimd
                    def _(pool):
                        step = Chain(pool, rk_step, "rk")
                        for m in range(KC):
                            if m >= 3:
                                pool.wait_ge(gated, m - 2)
                            x = rkv[:, m % 3, :]
                            step(pool.tensor_tensor(x, R[:, m, :], K[:, m, :], ALU.mult))
                            pool.tensor_tensor(x, x, vec[:, V_RK + m:V_RK + m + 1].to_broadcast([128, T]), ALU.mult)\
                                .then_inc(rk_ready, 1)

                    @block.tensor
                    def _(pe):
                        def product(bank, w, x, done):
                            for hf in range(2):
                                mm = pe.matmul(P[:, bank + hf, 0:HT], w, x[:, hf * HT:(hf + 1) * HT],
                                               start=True, stop=True)
                            mm.then_inc(done, 1)

                        def mean(m):
                            if m:
                                pe.wait_ge(centred, m)
                            product(0, headones[:, :], O[:, m, :], mean_done)

                        def bonus(m):
                            pe.wait_ge(rk_ready, m + 1)
                            if m:
                                pe.wait_ge(bonus_ready, m)
                            product(2, headones[:, :], rkv[:, m % 3, :], bonus_done)

                        pe.wait_ge(stage_in, landed)
                        for m in range(2):
                            mean(m)
                            bonus(m)
                        for m in range(KC):
                            pe.wait_ge(csq_ready, m + 1)
                            if m:
                                pe.wait_ge(var_read, m)
                            product(4, headones[:, :], csq[:, m % 3, :], var_done)
                            if m + 2 < KC:
                                mean(m + 2)
                                bonus(m + 2)
                            if m:
                                pe.wait_ge(gated, m)
                            product(6, g2[:, m * 128:(m + 1) * 128], tg[:, :], og_done)

                    @block.scalar
                    def _(act):
                        def square(m):
                            act.wait_ge(centred, m + 1)
                            if m >= 3:
                                act.wait_ge(var_done, m - 2)
                            act.activation(csq[:, m % 3, :], O[:, m, :], ACT.Square).then_inc(csq_ready, 1)

                        square(0)
                        square(1)
                        for m in range(KC):
                            act.wait_ge(n_var, m + 1)
                            act.activation(rs[:, m % 2, :], rs[:, m % 2, :], ACT.Sqrt).then_inc(n_root, 1)
                            if m + 2 < KC:
                                square(m + 2)

                    @block.vector
                    def _(dve):
                        step = Chain(dve, dve_step, "dve")
                        sums = lambda bank: P[:, bank:bank + 2, 0:HT]
                        col = lambda c, m: vec[:, c + m:c + m + 1]

                        def centre(m):
                            x = O[:, m, :]
                            dve.wait_ge(mean_done, m + 1)
                            dve.scalar_tensor_tensor(out=halves(x), in0=sums(0), scalar=-1.0 / HD, in1=halves(x),
                                                     op0=ALU.mult, op1=ALU.add).then_inc(centred, 1)
                            dve.wait_ge(bonus_done, m + 1)
                            dve.tensor_tensor(halves(rkv[:, m % 3, :]), halves(V[:, m, :]), sums(2), ALU.mult)\
                               .then_inc(bonus_ready, 1)

                        centre(0)
                        centre(1)
                        for m in range(KC):
                            r = rs[:, m % 2, :]
                            dve.wait_ge(var_done, m + 1)
                            dve.tensor_scalar(halves(r), sums(4), 1.0 / HD, 64e-5, ALU.mult, ALU.add)\
                               .then_inc(var_read, 1)
                            dve.wait_ge(var_read, m + 1)
                            dve.reciprocal(r, r).then_inc(n_var, 1)
                            if m + 2 < KC:
                                centre(m + 2)
                            x = O[:, m, :]
                            dve.wait_ge(n_root, m + 1)
                            dve.wait_ge(centred, m + 1)
                            dve.wait_ge(bonus_ready, m + 1)
                            step(dve.scalar_tensor_tensor(out=x, in0=x, scalar=col(V_LNW, m), in1=r,
                                                          op0=ALU.mult, op1=ALU.mult))
                            step(dve.scalar_tensor_tensor(out=x, in0=x, scalar=col(V_LNB, m), in1=rkv[:, m % 3, :],
                                                          op0=ALU.add, op1=ALU.add))
                            dve.wait_ge(og_done, m + 1)
                            dve.tensor_tensor(halves(R[:, m, :]), halves(x), sums(6), ALU.mult).then_inc(gated, 1)

        with nc.Block(no_gpsimd_drain=True) as block:
            @block.sync
            def _(sp):
                sp.dma_start(h[:, :, :], a["x"]).then_inc(fixed_in, 16)
                sp.dma_start(vec[:, :], a["vec"]).then_inc(fixed_in, 16)
                sp.dma_start(ones[:, :], a["ones"]).then_inc(fixed_in, 16)
                sp.dma_start(ident[:, :], a["ident"]).then_inc(fixed_in, 16)
                sp.dma_start(headones[:, :], a["headones"]).then_inc(fixed_in, 16)
                stream_weights(sp, RING)
                sp.wait_ge(fixed_in, 80)

        layer0()
        tail(0, U_T0)
        layer1()
        tail(1, U_T1)
        with nc.Block(no_gpsimd_drain=True) as block:
            @block.sync
            def _(sp):
                sp.dma_start(o["y"], h[:, :, :]).then_inc(stores, 16)
                state["stores"] += 16
                sp.wait_ge(stores, state["stores"])


def kernel(**inputs):
    import concourse.bacc as bacc
    from concourse.bass_utils import run_bass_kernel_spmd as run

    x = {k: np.asarray(v) for k, v in inputs.items()}
    fm = lambda v: np.ascontiguousarray(v.reshape(v.shape[0], -1, 128).transpose(2, 1, 0))
    cols = lambda v: v.reshape(-1, 128).T

    def unit_in(w):
        return w.reshape(KC, 128, -1, 256).transpose(2, 1, 0, 3).reshape(-1, 128, UW)

    def unit_down(w):
        return w.reshape(2, 2, KC, 128, 4, 256).transpose(0, 4, 1, 3, 2, 5).reshape(2, 8, 128, UW)

    def unit_ple(w):
        return w.reshape(2, 128, D).transpose(1, 0, 2).reshape(1, 128, UW)

    order = [(2 * gp + g2) * REP + r for gp in range(2) for r in range(REP) for g2 in range(2)]
    w_in = x["even_w_in"][0]
    wq = w_in[:, 256:1024].reshape(D, HEADS, HD)[:, order].reshape(D, 768)
    w_big = np.concatenate([w_in[:, :256], wq, w_in[:, 1024:2560]], 1)
    w_out = x["even_w_out"][0]
    w_out = np.concatenate([w_out[:256], w_out[256:].reshape(HEADS, HD, D)[order].reshape(768, D)], 0)
    units = [unit_in(w_big), unit_in(w_out)]
    for l in range(2):
        if l == 1:
            units += [unit_in(x[n][0]) for n in ("rwkv_wr", "rwkv_wk", "rwkv_wv", "rwkv_wo")]
        up, down = unit_in(x["mlp_w1"][l]).reshape(2, 8, 128, UW), unit_down(x["mlp_w2"][l])
        units += [up[0], down[0], up[1], down[1], unit_in(x["ple_gate"][l]),
                  unit_ple(x["ple_proj"][l])]

    kg = x["k_gain"][0]
    two = lambda v: np.concatenate([v, v])[:, None]
    vec = np.concatenate(
        [cols(x["norm_mix"]), cols(x["norm_mlp"]), cols(x["norm_ple"]), cols(x["rwkv_mu"])]
        + [cols(x["rwkv_" + n]) for n in ("w0", "a0", "kk", "ka", "rk", "lnw", "lnb")]
        + [cols(x["pool_scale"]), two(x["q_gain"][0]), two(kg[0]), two(kg[1]), two(kg[2])], 1)

    def block_diag(m):
        a_, b_ = m
        z = np.zeros(a_.shape[:-2] + (128, 128), np.float32)
        z[..., :64, :64], z[..., 64:, 64:] = a_, b_
        return z

    cw = x["cmp_w"][0]
    pw = x["pool_w"][0]
    ck, cv = x["cache_k"][0], x["cache_v"][0]
    fmc = lambda c: c.reshape(-1, PAGE, 2, 2, HD).transpose(0, 3, 4, 2, 1).reshape(-1, 128, 2, PAGE)
    ws = x["state_win_v"][0].reshape(NS, WIN // 128, 128, 256).transpose(0, 2, 1, 3)
    wk = x["state_win_k"][0].reshape(NS, WIN, 2, 2, HD).transpose(0, 3, 4, 2, 1).reshape(NS, 128, 2, WIN)
    small = lambda w: w.reshape(KC, 128, -1).transpose(1, 0, 2)
    d = {
        "x": fm(np.concatenate([x["x_prompt"][0], x["x_sample"][:, 0]], 0)),
        "p": np.stack([fm(np.concatenate([x["p_prompt"][l, 0], x["p_sample"][l, :, 0]], 0)) for l in range(2)]),
        "weights": np.concatenate(units, 0),
        "vec": vec,
        "wgl": small(w_in[:, 2560:]),
        "state_pool": x["state_pool"][0].reshape(NS, 15, 2, 128).transpose(3, 2, 0, 1),
        "pool_w": block_diag((pw[0::2], pw[1::2])).transpose(1, 0, 2),
        "cmp_w": block_diag((cw, cw)).transpose(2, 0, 1, 3),
        "cmp_pe": np.concatenate([x["cmp_pe"][0].transpose(2, 0, 1)] * 2, 0),
        "page_table": x["page_table"].reshape(1, -1),
        "rows": np.concatenate([fmc(ck[:, :, 0]), fmc(cv[:, :, 0]), fmc(ck[:, :, 1])], 2),
        "cv_slc": cv[:, :, 1].reshape(-1, PAGE, 256),
        "win_k": wk, "win_v": ws,
        "state_shift": fm(x["state_shift"][0]),
        "rwkv_w1": small(x["rwkv_w1"][0]), "rwkv_a1": small(x["rwkv_a1"][0]), "rwkv_g1": small(x["rwkv_g1"][0]),
        "rwkv_w2": x["rwkv_w2"][0], "rwkv_a2": x["rwkv_a2"][0], "rwkv_g2": x["rwkv_g2"][0],
        "state_wkv": x["state_wkv"][0].reshape(NS, KC, 2, HD, HD).transpose(2, 3, 0, 1, 4).reshape(128, NS, KC, HD),
    }
    d.update(constants())
    outs = {
        "y": (128, KC, T), "kv": (128, 12, T), "pool_p": (128, 2, 15), "pool_s": (128, 2, NS, 15),
        "win_k": (NS, 128, 2, WIN), "win_v": (NS, 128, WIN // 128, 256), "shift": (128, KC, NS + 1),
        "wkv_p": (128, KC, HD), "wkv_s": (128, NS, KC, HD),
    }
    nc = bacc.Bacc("TRN2", target_bir_lowering=False, num_devices=1)
    d = {"in_" + k: np.ascontiguousarray(v) for k, v in d.items()}
    ins = {k[3:]: nc.dram_tensor(k, v.shape, mybir.dt.from_np(v.dtype), kind="ExternalInput").ap() for k, v in d.items()}
    res = {k: nc.dram_tensor("out_" + k, s, F32, kind="ExternalOutput").ap() for k, s in outs.items()}
    build(nc, ins, res)
    r = run(nc, [d], core_ids=[0]).results[0]
    r = {k: np.asarray(r["out_" + k]) for k in outs}

    rows = lambda v: v.transpose(2, 1, 0).reshape(v.shape[2], -1)
    y = rows(r["y"])
    kv = r["kv"].reshape(2, HD, 6, 2, T).transpose(4, 2, 3, 0, 1).reshape(T, 6, GROUPS, HD)
    pair = lambda b, c, s: np.stack([kv[s, b], kv[s, c]], 1)
    pr, sa = slice(0, SEQ), slice(SEQ, T)
    wko = r["win_k"].reshape(NS, 2, HD, 2, WIN).transpose(0, 4, 3, 1, 2).reshape(NS, WIN, GROUPS, HD)
    wvo = r["win_v"].transpose(0, 2, 1, 3).reshape(NS, WIN, GROUPS, HD)
    shift = rows(r["shift"])
    return (
        y[None, :SEQ], y[SEQ:, None],
        pair(0, 2, pr)[None, None], pair(1, 3, pr)[None, None],
        pair(0, 2, sa)[None, :, None], pair(1, 3, sa)[None, :, None],
        kv[None, None, :SEQ, 4], kv[None, None, :SEQ, 5],
        np.concatenate([wko[:, 1:], kv[SEQ:, None, 4]], 1)[None], np.concatenate([wvo[:, 1:], kv[SEQ:, None, 5]], 1)[None],
        rows(r["pool_p"])[None, None], r["pool_s"].transpose(2, 3, 1, 0).reshape(1, NS, 15, 256),
        shift[None, :1], shift[None, 1:],
        r["wkv_p"].reshape(2, HD, KC, HD).transpose(2, 0, 1, 3).reshape(1, 1, RH, HD, HD),
        r["wkv_s"].reshape(2, HD, NS, KC, HD).transpose(2, 3, 0, 1, 4).reshape(1, NS, RH, HD, HD),
    )
```
